# Optimizing a Trainium2 kernel written in Bass

```python
import math
import jax, jax.numpy as jnp
from jax import lax
import numpy as np

D_MODEL = 1024
BATCH = 1
SEQ = 256
DEPTH = 2

Q_BLOCK = 128
A_HEADS = 4
A_DH = 64
A_DV = 2 * A_DH
B_HEADS = 8
B_DH = 64
B_PATTERNS = ((128, 1), (512, 4), (2048, 16))
C_HEADS = 8
C_Q_RANK = 384
C_KV_RANK = 256
C_NOPE = 64
C_ROPE = 32
C_DV = 64
ROPE_THETA = 10000.0
N_BRANCHES = 3
BRANCH_WIDTH = A_HEADS * A_DV
MEM_TOKENS = 256
X_HEADS = 4
X_DH = 64
N_GROUPS = 4
EXPERTS_PER_GROUP = 8
N_EXPERTS = N_GROUPS * EXPERTS_PER_GROUP
TOP_K = 2
D_EXPERT = 512
EXPERT_BLOCK = 128
NORM_EPS = 1e-6
COL_SIZES = (A_HEADS * 2 * A_DH, A_HEADS * 2 * A_DH, A_HEADS * A_DV,
             B_HEADS * B_DH, B_HEADS * B_DH, B_HEADS * B_DH,
             C_Q_RANK, C_KV_RANK, C_ROPE, N_BRANCHES * D_MODEL)
IN_COLS = sum(COL_SIZES)

kernel_name = 'hybrid_gated_encoder_block'

def _rms_norm(x, g):
    xf = x.astype(jnp.float32)
    y = xf * lax.rsqrt(jnp.mean(xf * xf, axis=-1, keepdims=True) + NORM_EPS)
    return (y * g.astype(jnp.float32)).astype(x.dtype)

def _to_blocks(a):
    b, s = a.shape[:2]
    a = a.reshape((b, s // Q_BLOCK, Q_BLOCK) + a.shape[2:])
    return jnp.moveaxis(a, 1, 0)

def _from_blocks(a):
    a = jnp.moveaxis(a, 0, 1)
    return a.reshape((a.shape[0], a.shape[1] * a.shape[2]) + a.shape[3:])

def _alibi_slopes(n):
    return jnp.exp2(-8.0 * jnp.arange(1, n + 1, dtype=jnp.float32) / n)

def _rope_angles(pos, dim):
    inv = ROPE_THETA ** (-jnp.arange(0, dim, 2, dtype=jnp.float32) / dim)
    return pos.astype(jnp.float32)[..., None] * inv

def _apply_rope(x, ang):
    half = x.shape[-1] // 2
    cos = jnp.cos(ang).astype(x.dtype)
    sin = jnp.sin(ang).astype(x.dtype)
    x1, x2 = x[..., :half], x[..., half:]
    return jnp.concatenate([x1 * cos - x2 * sin, x2 * cos + x1 * sin], axis=-1)

def _split_cols(proj):
    out, start = [], 0
    for n in COL_SIZES:
        out.append(proj[..., start:start + n])
        start += n
    return out

def _diff_attention(q, k, v, pos, lam, slopes):
    scale = A_DH ** -0.5

    def block(args):
        qb, pb = args
        sc = jnp.einsum('bqhcd,bkhcd->bhcqk', qb, k).astype(jnp.float32) * scale
        dist = jnp.abs(pb[:, :, None] - pos[:, None, :]).astype(jnp.float32)
        sc = sc - slopes[None, :, None, None, None] * dist[:, None, None]
        p = jax.nn.softmax(sc, axis=-1)
        attn = p[:, :, 0] - lam * p[:, :, 1]
        return jnp.einsum('bhqk,bkhd->bqhd', attn.astype(v.dtype), v)

    return _from_blocks(lax.map(block, (_to_blocks(q), _to_blocks(pos))))

def _dilated_pattern(q, k, v, slopes, window, dilation):
    b, s, h, dh = q.shape
    half = window // (2 * dilation)
    pad = half * dilation
    kp = jnp.pad(k, ((0, 0), (pad, pad), (0, 0), (0, 0)))
    vp = jnp.pad(v, ((0, 0), (pad, pad), (0, 0), (0, 0)))
    offs = (jnp.arange(2 * half + 1) - half) * dilation
    bias = -slopes[:, None] * jnp.abs(offs).astype(jnp.float32)[None, :]
    scale = dh ** -0.5

    def block(args):
        qb, t0 = args
        kpos = t0 + jnp.arange(Q_BLOCK)[:, None] + offs[None, :]
        valid = (kpos >= 0) & (kpos < s)
        kb = jnp.take(kp, kpos + pad, axis=1)
        vb = jnp.take(vp, kpos + pad, axis=1)
        sc = jnp.einsum('bqhd,bqkhd->bhqk', qb, kb).astype(jnp.float32) * scale
        sc = jnp.where(valid[None, None], sc + bias[None, :, None, :], -jnp.inf)
        lse = jax.nn.logsumexp(sc, axis=-1)
        p = jnp.exp(sc - lse[..., None])
        o = jnp.einsum('bhqk,bqkhd->bqhd', p.astype(v.dtype), vb)
        return o, jnp.swapaxes(lse, 1, 2)

    starts = jnp.arange(s // Q_BLOCK, dtype=jnp.int32) * Q_BLOCK
    o, lse = lax.map(block, (_to_blocks(q), starts))
    return _from_blocks(o), _from_blocks(lse)

def _dilated_attention(q, k, v, slopes):
    outs, lses = [], []
    for window, dilation in B_PATTERNS:
        o, l = _dilated_pattern(q, k, v, slopes, window, dilation)
        outs.append(o)
        lses.append(l)
    w = jax.nn.softmax(jnp.stack(lses), axis=0)
    return jnp.sum(w[..., None].astype(q.dtype) * jnp.stack(outs), axis=0)

def _mla_attention(cq, ckv, ckr, pos, q_norm_g, w_uq, kv_norm_g, w_ukv):
    b, s, _ = cq.shape
    q = (_rms_norm(cq, q_norm_g) @ w_uq).reshape(b, s, C_HEADS, C_NOPE + C_ROPE)
    kv = (_rms_norm(ckv, kv_norm_g) @ w_ukv).reshape(b, s, C_HEADS, C_NOPE + C_DV)
    q_nope, q_rope = q[..., :C_NOPE], q[..., C_NOPE:]
    k_nope, v = kv[..., :C_NOPE], kv[..., C_NOPE:]
    ang = _rope_angles(pos, C_ROPE)
    q_rope = _apply_rope(q_rope, ang[:, :, None, :])
    k_rope = _apply_rope(ckr, ang)
    scale = (C_NOPE + C_ROPE) ** -0.5

    def block(args):
        qn, qr = args
        sc = (jnp.einsum('bqhd,bkhd->bhqk', qn, k_nope)
              + jnp.einsum('bqhr,bkr->bhqk', qr, k_rope)).astype(jnp.float32) * scale
        p = jax.nn.softmax(sc, axis=-1)
        return jnp.einsum('bhqk,bkhd->bqhd', p.astype(v.dtype), v)

    o = _from_blocks(lax.map(block, (_to_blocks(q_nope), _to_blocks(q_rope))))
    return o.reshape(b, s, C_HEADS * C_DV)

def _cross_attention(h, m, w_xq, w_xkv, w_xo):
    b, s, _ = h.shape
    q = (h @ w_xq).reshape(b, s, X_HEADS, X_DH)
    kv = (m @ w_xkv).reshape(b, m.shape[1], 2, X_HEADS, X_DH)
    k, v = kv[:, :, 0], kv[:, :, 1]
    sc = jnp.einsum('bqhd,bkhd->bhqk', q, k).astype(jnp.float32) * (X_DH ** -0.5)
    p = jax.nn.softmax(sc, axis=-1)
    o = jnp.einsum('bhqk,bkhd->bqhd', p.astype(v.dtype), v).reshape(b, s, X_HEADS * X_DH)
    return o @ w_xo

def _hier_moe(h, w_group, b_group, w_router, b_router, w1, w3, w2):
    b, s, d = h.shape
    xt = h.reshape(-1, d)
    t = xt.shape[0]
    g_prob = jax.nn.softmax((xt @ w_group + b_group).astype(jnp.float32), axis=-1)
    p_g, g_sel = lax.top_k(g_prob, 1)
    e_logits = (xt @ w_router + b_router).astype(jnp.float32).reshape(t, N_GROUPS, EXPERTS_PER_GROUP)
    e_in = jnp.take_along_axis(e_logits, g_sel[:, :, None], axis=1)[:, 0]
    top_v, top_i = lax.top_k(e_in, TOP_K)
    gate = p_g * jax.nn.softmax(top_v, axis=-1)
    eid = (g_sel * EXPERTS_PER_GROUP + top_i).reshape(-1)
    tok = jnp.repeat(jnp.arange(t, dtype=jnp.int32), TOP_K)
    wts = gate.reshape(-1)
    n = eid.shape[0]
    order = jnp.argsort(eid)
    se, stok, sw = eid[order], tok[order], wts[order]
    counts = jnp.bincount(eid, length=N_EXPERTS)
    start = jnp.cumsum(counts) - counts
    padded = (counts + EXPERT_BLOCK - 1) // EXPERT_BLOCK * EXPERT_BLOCK
    pend = jnp.cumsum(padded)
    pstart = pend - padded
    dest = pstart[se] + (jnp.arange(n) - start[se])
    n_blocks = (n + EXPERT_BLOCK - 1) // EXPERT_BLOCK + N_EXPERTS
    rows = n_blocks * EXPERT_BLOCK
    row_tok = jnp.zeros((rows,), jnp.int32).at[dest].set(stok)
    row_w = jnp.zeros((rows,), h.dtype).at[dest].set(sw.astype(h.dtype))
    blk_e = jnp.minimum(jnp.searchsorted(pend, jnp.arange(n_blocks) * EXPERT_BLOCK, side='right'),
                        N_EXPERTS - 1)
    xr = xt[row_tok].reshape(n_blocks, EXPERT_BLOCK, d)

    def expert_block(args):
        xb, e = args
        return (jax.nn.silu(xb @ w1[e]) * (xb @ w3[e])) @ w2[e]

    yr = lax.map(expert_block, (xr, blk_e)).reshape(rows, d)
    y = jax.ops.segment_sum(yr * row_w[:, None], row_tok, num_segments=t)
    return y.reshape(b, s, d)

def setup_inputs(seed: int = 0) -> dict:
    key = jax.random.key(seed)
    ks = jax.random.split(key, 32)
    f32 = jnp.float32

    def nrm(k, shape, scale):
        return jax.random.normal(k, shape, f32) * scale

    def gain(k, shape):
        return 1.0 + 0.05 * jax.random.normal(k, shape, f32)

    L, D = DEPTH, D_MODEL
    return {
        'x': nrm(ks[0], (BATCH, SEQ, D), 1.0),
        'mem': nrm(ks[1], (BATCH, MEM_TOKENS, D), 1.0),
        'positions': jnp.broadcast_to(jnp.arange(SEQ, dtype=jnp.int32), (BATCH, SEQ)),
        'mix_norm_g': gain(ks[2], (L, D)),
        'w_in': nrm(ks[3], (L, D, IN_COLS), D ** -0.5),
        'diff_lambda': nrm(ks[4], (L, 4, A_DH), 0.1),
        'diff_subln_g': gain(ks[5], (L, A_DV)),
        'mla_q_norm_g': gain(ks[6], (L, C_Q_RANK)),
        'w_uq': nrm(ks[7], (L, C_Q_RANK, C_HEADS * (C_NOPE + C_ROPE)), C_Q_RANK ** -0.5),
        'mla_kv_norm_g': gain(ks[8], (L, C_KV_RANK)),
        'w_ukv': nrm(ks[9], (L, C_KV_RANK, C_HEADS * (C_NOPE + C_DV)), C_KV_RANK ** -0.5),
        'w_branch': nrm(ks[10], (L, N_BRANCHES, BRANCH_WIDTH, D), BRANCH_WIDTH ** -0.5),
        'w_out': nrm(ks[11], (L, D, D), D ** -0.5),
        'cross_norm_g': gain(ks[12], (L, D)),
        'mem_norm_g': gain(ks[13], (L, D)),
        'w_xq': nrm(ks[14], (L, D, X_HEADS * X_DH), D ** -0.5),
        'w_xkv': nrm(ks[15], (L, D, 2 * X_HEADS * X_DH), D ** -0.5),
        'w_xo': nrm(ks[16], (L, X_HEADS * X_DH, D), (X_HEADS * X_DH) ** -0.5),
        'ffn_norm_g': gain(ks[17], (L, D)),
        'w_group': nrm(ks[18], (L, D, N_GROUPS), D ** -0.5),
        'b_group': nrm(ks[19], (L, N_GROUPS), 0.01),
        'w_router': nrm(ks[20], (L, D, N_EXPERTS), D ** -0.5),
        'b_router': nrm(ks[21], (L, N_EXPERTS), 0.01),
        'w1': nrm(ks[22], (L, N_EXPERTS, D, D_EXPERT), D ** -0.5),
        'w3': nrm(ks[23], (L, N_EXPERTS, D, D_EXPERT), D ** -0.5),
        'w2': nrm(ks[24], (L, N_EXPERTS, D_EXPERT, D), D_EXPERT ** -0.5),
        'final_norm_g': gain(ks[25], (D,)),
    }

def reference(x, mem, positions, mix_norm_g, w_in, diff_lambda, diff_subln_g,
              mla_q_norm_g, w_uq, mla_kv_norm_g, w_ukv, w_branch, w_out,
              cross_norm_g, mem_norm_g, w_xq, w_xkv, w_xo,
              ffn_norm_g, w_group, b_group, w_router, b_router, w1, w3, w2,
              final_norm_g):
    b, s, d = x.shape
    slopes_a = _alibi_slopes(A_HEADS)
    slopes_b = _alibi_slopes(B_HEADS)
    for l in range(DEPTH):
        h = _rms_norm(x, mix_norm_g[l])
        aq, ak, av, bq, bk, bv, cq, ckv, ckr, gates = _split_cols(h @ w_in[l])
        lq = diff_lambda[l].astype(jnp.float32)
        lam_init = 0.8 - 0.6 * math.exp(-0.3 * l)
        lam = jnp.exp(jnp.sum(lq[0] * lq[1])) - jnp.exp(jnp.sum(lq[2] * lq[3])) + lam_init
        oa = _diff_attention(aq.reshape(b, s, A_HEADS, 2, A_DH), ak.reshape(b, s, A_HEADS, 2, A_DH),
                             av.reshape(b, s, A_HEADS, A_DV), positions, lam, slopes_a)
        oa = (_rms_norm(oa, diff_subln_g[l]) * (1.0 - lam_init)).reshape(b, s, BRANCH_WIDTH)
        ob = _dilated_attention(bq.reshape(b, s, B_HEADS, B_DH), bk.reshape(b, s, B_HEADS, B_DH),
                                bv.reshape(b, s, B_HEADS, B_DH), slopes_b).reshape(b, s, BRANCH_WIDTH)
        oc = _mla_attention(cq, ckv, ckr, positions, mla_q_norm_g[l], w_uq[l],
                            mla_kv_norm_g[l], w_ukv[l])
        br = jnp.einsum('bsnc,ncd->bsnd', jnp.stack([oa, ob, oc], axis=2), w_branch[l])
        g = jax.nn.sigmoid(gates.reshape(b, s, N_BRANCHES, d))
        x = x + jnp.sum(g * br, axis=2) @ w_out[l]
        x = x + _cross_attention(_rms_norm(x, cross_norm_g[l]), _rms_norm(mem, mem_norm_g[l]),
                                 w_xq[l], w_xkv[l], w_xo[l])
        x = x + _hier_moe(_rms_norm(x, ffn_norm_g[l]), w_group[l], b_group[l], w_router[l],
                          b_router[l], w1[l], w3[l], w2[l])
    return _rms_norm(x, final_norm_g)


_drawn_inputs = setup_inputs


def setup_inputs(seed=0):
    import zlib

    import numpy as np

    out = dict(_drawn_inputs(seed))
    spreads = {}
    factors = {'mla_q_norm_g': 3.007, 'mla_kv_norm_g': 2.775, 'cross_norm_g': 3.116, 'b_router': 2.749}
    for name, (base, spread) in spreads.items():
        noise = np.random.default_rng([zlib.crc32(name.encode()), seed]).standard_normal(out[name].shape)
        drawn = base * np.exp(spread * noise) if base else spread * noise
        out[name] = __import__('jax').numpy.asarray(drawn.astype(out[name].dtype))
    for name, factor in factors.items():
        out[name] = (out[name] * factor).astype(out[name].dtype)
    return out
```

```python
import math
from contextlib import ExitStack

import concourse.bass as bass
from concourse import mybir

F32 = mybir.dt.float32
I32 = mybir.dt.int32
U32 = mybir.dt.uint32
ALU = mybir.AluOpType
ACT = mybir.ActivationFunctionType
AX_X = mybir.AxisListType.X

P = 128
DEPTH, D, SEQ = 2, 1024, 256
KD = D // P
TT = SEQ // P
A_HEADS, A_DH, A_DV = 4, 64, 128
B_HEADS, B_DH = 8, 64
B_PATTERNS = ((128, 1), (512, 4), (2048, 16))
C_HEADS, C_NOPE, C_ROPE, C_DV = 8, 64, 32, 64
C_Q_RANK, C_KV_RANK = 384, 256
C_DH = C_NOPE + C_ROPE
ROPE_THETA = 10000.0
X_HEADS, X_DH = 4, 64
N_BRANCHES, WIDTH = 3, 512
N_GROUPS, PER_GROUP, N_EXPERTS, D_EXPERT = 4, 8, 32, 512
EPS = 1e-6
TWO_PI = (6.28125, 0.0019350051879882812, 3.0199159795e-07)
NORM_BANKS = (3, 4, 6, 7)
SETUP_ANGLES = 24
SETUP_ZEROS = 8
ROUTE_STEPS = 37
FAR = -1e30

RING = 12
SLOT = 2048
CAP = 32
QUAD = 4
QUADS = N_EXPERTS // QUAD
PASSES = SEQ // CAP
NPB = 3

OFF_AQ, OFF_AK, OFF_AV = 0, 512, 1024
OFF_BQ, OFF_BK, OFF_BV = 1536, 2048, 2560
OFF_CQ, OFF_CKR, OFF_GATE = 3072, 3712, 3744

C_ID, C_BEFORE, C_ONES, C_SWAP, C_IOTA, C_GID, C_INV, C_LAM = 0, 128, 256, 384, 416, 448, 480, 481
C_STRIP = 488
STRIP = SEQ + P
N_CONST = C_STRIP + B_HEADS * STRIP


def slopes(n):
    return [2.0 ** (-8.0 * i / n) for i in range(1, n + 1)]


def lam_init(layer):
    return 0.8 - 0.6 * math.exp(-0.3 * layer)


def shape_constants():
    import numpy as np
    c = np.zeros((P, N_CONST), np.float32)
    r = np.arange(P)
    c[:, C_ID:C_ID + P] = r[:, None] == r[None, :]
    c[:, C_BEFORE:C_BEFORE + P] = r[:, None] < r[None, :]
    c[:, C_ONES:C_ONES + P] = 1.0
    half = C_ROPE // 2
    for i in range(half):
        c[C_NOPE + half + i, C_SWAP + i] = -1.0
        c[C_NOPE + i, C_SWAP + half + i] = 1.0
    c[:, C_IOTA:C_IOTA + CAP] = np.arange(CAP)
    c[:, C_GID:C_GID + N_EXPERTS] = np.arange(N_EXPERTS) // PER_GROUP
    inv = np.float32(ROPE_THETA) ** (-np.arange(0, C_ROPE, 2, dtype=np.float32) / np.float32(C_ROPE))
    c[C_NOPE:C_DH, C_INV] = np.concatenate([inv, inv])
    for layer in range(DEPTH):
        c[:, C_LAM + layer] = lam_init(layer)
        c[:, C_LAM + DEPTH + layer] = 1.0 - lam_init(layer)
    dist = np.abs(np.arange(STRIP)[None, :] - P - r[:, None])
    times = sum((dist % dil == 0) & (dist <= win // (2 * dil) * dil) for win, dil in B_PATTERNS)
    many = np.where(times > 0, np.log(np.maximum(times, 1)), FAR)
    for h, s in enumerate(slopes(B_HEADS)):
        c[:, C_STRIP + h * STRIP:C_STRIP + (h + 1) * STRIP] = many - s * dist
    return c


TURNS = [("xkv", 0), ("xkv", 256)] + [("in", c) for c in range(0, 3584, 256)] + [("in_last", 3584)]
TURNS += [("uq", 0), ("uq", 384), ("ukv", 0)]
T_GATE = len(TURNS)
for _pair in range(4):
    TURNS += [("in", OFF_GATE + _n * D + _pair * 256) for _n in range(N_BRANCHES)]
    TURNS += [("branch01", _pair), ("branch2", _pair)]
T_OUT = len(TURNS)
TURNS += [("out", (_half, _kg)) for _half in range(2) for _kg in range(2)]
T_XQ, T_XO = len(TURNS), len(TURNS) + 1
TURNS += [("xq", 0), ("xo", 0)]
N_MIX = len(TURNS)
EMPTY = -N_MIX % RING
Q_BASE = N_MIX + EMPTY
PER_QUAD = 2 * KD + 2 * (D_EXPERT // P)
PER_LAYER = Q_BASE + QUADS * PER_QUAD
assert PER_QUAD % RING == 0

JOBS = [("kx", 0, 1, "act"), ("vx", 1, 1, "dve")]
JOBS += [(n, 2 + i, 1, e) for i, (n, e) in enumerate(
    [("aq0", "act"), ("aq1", "dve"), ("ak0", "act"), ("ak1", "dve"), ("av0", "act"), ("av1", "dve"),
     ("bq0", "act"), ("bq1", "dve"), ("bk0", "act"), ("bk1", "dve"), ("bv0", "act"), ("bv1", "dve"),
     ("c0", "dve"), ("c1", "dve"), ("c2", "dve")])]
JOBS += [("cs", None, 0, "act"), ("cq0", 17, 0, "act"), ("cq1", 17, 1, "act"), ("cq2", 18, 0, "act"),
         ("cq3", 18, 1, "act"), ("ckr", None, 0, "dve"), ("cr0", None, 0, "dve"), ("ck0", 19, 0, "act"),
         ("ck1", 19, 0, "dve"), ("cr1", None, 0, "dve"), ("ck2", 19, 0, "act"), ("ck3", 19, 0, "act"),
         ("cr2", None, 0, "dve"), ("cv0", 19, 0, "act"), ("cr3", None, 0, "dve"), ("cv1", 19, 1, "act"),
         ("as0", None, 0, "act"), ("as1", None, 0, "act")]
JOB_NAMES = [j[0] for j in JOBS]
FILL = {0: ["bq0"], 1: ["bq1", "bk0"], 2: ["bk1"], 3: ["bv0"], 4: ["bv1"], 5: ["c0"], 6: ["c1"], 7: ["c2"],
        9: ["cs"], 11: ["cq0", "cq1"], 12: ["cq2", "cq3", "ckr"], 13: ["cr0", "ck0", "ck1"],
        14: ["cr1", "ck2"], 15: ["ck3", "cr2"], 16: ["cv0", "cr3"], 17: ["cv1"], 19: ["as0"], 20: ["as1"]}
assert JOB_NAMES[8:] == [n for i in sorted(FILL) for n in FILL[i]]
A0, B0, C0, X0, NI = 0, 8, 16, 24, 28
LAG_T, LAG_PV, LAG_OUT = 2, 3, 4


def count_before(kind, n):
    return sum(kind(j) for j in JOBS[:n + 1])


def bass_hybrid_encoder(nc, x_in, mem_in, pos_in, mix_norm_g, w_in, diff_lambda, diff_subln_g, mla_q_norm_g,
                        w_uq, mla_kv_norm_g, w_ukv, w_branch, w_out, cross_norm_g, mem_norm_g, w_xq, w_xkv,
                        w_xo, ffn_norm_g, w_group, b_group, w_router, b_router, w1, w3, w2, final_norm_g,
                        consts, out):
    ctx = ExitStack()
    with ctx:
        def sb(name, shape, dt=F32):
            return ctx.enter_context(nc.sbuf_tensor(name, shape, dt))

        def sem(name):
            return ctx.enter_context(nc.semaphore(name))

        ring = sb("ring", [P, RING, SLOT])
        con = sb("con", [P, N_CONST])
        x = sb("x", [P, TT, D])
        h = sb("h", [P, TT, D])
        hT = sb("hT", [P, KD, SEQ])
        gain = sb("gain", [P, D])
        q0 = sb("q0", [P, KD, SEQ])
        k0 = sb("k0", [P, 4, 2 * SEQ])
        v0 = sb("v0", [P, TT, 512])
        q1 = sb("q1", [P, 4, SEQ])
        k1 = sb("k1", [P, 4, 2 * SEQ])
        v1 = sb("v1", [P, TT, 512])
        kx = sb("kx", [P, 2, 2 * SEQ])
        vx = sb("vx", [P, TT, 256])
        prob = sb("prob", [P, NPB, 2, SEQ])
        probT = sb("probT", [P, 2, 2, TT, P])
        oa = sb("oa", [P, 4, SEQ])
        cT = sb("cT", [P, 5, SEQ])
        wide = sb("wide", [P, 4, SEQ])
        dist = sb("dist", [P, TT, SEQ])
        ropes = sb("ropes", [P, 2, SEQ])
        small = sb("small", [P, 64])
        gpad = sb("gpad", [P, TT, 8])
        topi = sb("topi", [P, TT, 2, 8], U32)
        flag = sb("flag", [P, 1], I32)
        gcol = sb("gcol", [P, DEPTH, 6])
        lamt = sb("lamt", [P, DEPTH])
        stat = sb("stat", [P, 16])
        mx = sb("mx", [P, NPB, 2])
        sm = sb("sm", [P, NPB, 2])
        rs = sb("rs", [P, NPB, 4])
        bank = [ctx.enter_context(nc.psum_tensor(f"bank{i}", [P, 512], F32)) for i in range(8)]

        ident = con[:, C_ID:C_ID + P]
        ones = con[:, C_ONES:C_ONES + P]
        before = con[:, C_BEFORE:C_BEFORE + P]
        iota = con[:, C_IOTA:C_IOTA + CAP]
        oBC = h[:, :, :].rearrange("p t (c n) -> p (t c) n", n=SEQ)
        kc = k0[:, :, :].rearrange("p a (b n) -> p (a b) n", n=SEQ)
        posf = q1[:, 0:2, :].rearrange("p c n -> p (c n)")[:, 0:TT + SEQ]
        posi = v1[:, :, :].bitcast(I32).rearrange("p t n -> p (t n)")[:, 0:TT + SEQ]
        angles = prob[:, 0, :, :]
        spare = oa[:, :, :].rearrange("p c n -> p (c n)")
        NR = N_GROUPS + N_EXPERTS
        logit = spare[:, 0:72].rearrange("p (t n) -> p t n", t=TT)
        rt = spare[:, 72:328].rearrange("p (t a n) -> p t a n", t=TT, a=4)
        top = spare[:, 328:392].rearrange("p (t a n) -> p t a n", t=TT, a=4)
        chosen = spare[:, 392:456].rearrange("p (t n) -> p t n", t=TT)
        place = spare[:, 456:528].rearrange("p (t n) -> p t n", t=TT)
        weight = spare[:, 528:600].rearrange("p (t n) -> p t n", t=TT)
        router_w = wide[:, :, :].rearrange("p c n -> p (c n)")[:, 0:KD * NR].rearrange("p (k n) -> p k n", k=KD)
        router_b = wide[:, :, :].rearrange("p c n -> p (c n)")[:, KD * NR:KD * NR + NR]
        xt = v0[:, :, :].rearrange("p t (c n) -> p (t c) n", n=P)
        yexp = q1[:, :, :].rearrange("p c n -> p (c n)")
        sel = v1[:, 0, 0:256].rearrange("p (t n) -> p t n", t=TT)
        selw = v1[:, 0, 256:512].rearrange("p (t n) -> p t n", t=TT)
        selwT = v1[:, 1, 0:256]
        flat = [prob[:, i, :, :].rearrange("p a n -> p (a n)") for i in range(NPB)]
        act_e, act_r, hidden = flat
        hiddenT = probT[:, 0, :, :, :].rearrange("p a b n -> p (a b) n")
        memx = q0[:, :, :].rearrange("p c n -> p (c n)").rearrange("p (t n) -> p t n", t=TT)
        memjunk = hT[:, :, :].rearrange("p c n -> p (c n)").rearrange("p (t n) -> p t n", t=TT)

        landed = [sem(f"landed{i}") for i in range(RING)]
        slot_free = sem("slot_free")
        con_in, x_in_s, pos_in_s, cols_in, lam_in = (sem(n) for n in ("con_in", "x_arrived", "pos_in", "cols_in", "lam_in"))
        gain_in, gain_used = sem("gain_in"), sem("gain_used")
        mem_arrived, router_in = sem("mem_arrived"), sem("router_in")
        setup_dve, setup_act, setup_pool, zeroed = sem("setup_dve"), sem("setup_act"), sem("setup_pool"), sem("zeroed")
        squared, rstd, normed, turned = sem("squared"), sem("rstd"), sem("normed"), sem("turned")
        hT_act, hT_dve = sem("hT_act"), sem("hT_dve")
        made = sem("made")
        copied = {"act": sem("copied_act"), "dve": sem("copied_dve")}
        layer_cols = sem("layer_cols")
        c_squared, c_rstd, c_scaled, rope_step, kr_spread = (sem("c_squared"), sem("c_rstd"), sem("c_scaled"),
                                                             sem("rope_step"), sem("kr_spread"))
        a_squared, a_rstd, a_normed = sem("a_squared"), sem("a_rstd"), sem("a_normed")
        scored, biased, maxed, exped = sem("scored"), sem("biased"), sem("maxed"), sem("exped")
        inverted, weighed = sem("inverted"), sem("weighed")
        a_scaled = sem("a_scaled")
        probs_turned, probsT_copied = sem("probs_turned"), sem("probsT_copied")
        pv_done, out_copied = sem("pv_done"), sem("out_copied")
        gate_exp, branch0, gate_step, mixed, mix_sum = (sem("gate_exp"), sem("branch0"), sem("gate_step"),
                                                        sem("mixed"), sem("mix_sum"))
        projected, x_added = sem("projected"), sem("x_added")
        qx_copied = sem("qx_copied")
        logits_made, route_step, route_ask, route_exp = (sem("logits_made"), sem("route_step"),
                                                         sem("route_ask"), sem("route_exp"))
        chosen_s, ranked, placed = sem("chosen_made"), sem("ranked"), sem("placed")
        shifted = sem("shifted")
        layer_done = sem("layer_done")
        stored, passed = sem("stored"), sem("passed")

        def round_sems(name):
            return {s: sem(f"{name}_{s}") for s in
                    ("sel_made", "selw_step", "selw_made", "gathered", "xt_act", "xt_dve", "e_made",
                     "silu_step", "hidden_made", "selw_turned", "hidden_turned", "selwT_copied",
                     "hiddenT_copied", "y_act", "y_dve", "combined", "added")}

        main_r, more_r = round_sems("main"), round_sems("more")
        more_landed = [sem(f"more_landed{i}") for i in range(RING)]
        more_free = sem("more_free")

        def real_turns(slot, upto):
            return sum(1 for j in range(upto) if j % RING == slot and not N_MIX <= j < Q_BASE)

        def wait_turn(eng, l, j):
            s = j % RING
            eng.wait_ge(landed[s], l * (16 * real_turns(s, PER_LAYER)) + 16 * real_turns(s, j + 1))

        def wait_free(eng, l, j):
            eng.wait_ge(slot_free, l * PER_LAYER + (RING + j + 1))

        N_MADE = sum(not j[2] for j in JOBS)
        N_COPIED = {e: sum(j[3] == e for j in JOBS) for e in ("act", "dve")}

        def wait_made(eng, l, name):
            n = JOB_NAMES.index(name)
            if JOBS[n][2]:
                wait_free(eng, l, JOBS[n][1])
            else:
                eng.wait_ge(made, l * N_MADE + count_before(lambda j: not j[2], n))

        def wait_copied(eng, l, name):
            n = JOB_NAMES.index(name)
            e = JOBS[n][3]
            eng.wait_ge(copied[e], l * N_COPIED[e] + count_before(lambda j: j[3] == e, n))

        def slot_k(j, k, n):
            return ring[:, j % RING, 0:k * n].rearrange("p (k n) -> p k n", k=k)

        def plain(eng):
            eng.sem_inc(passed, 1)

        def bank_n(g):
            return bank[NORM_BANKS[g]][:, :].rearrange("p (a n) -> p a n", a=2)

        block = ctx.enter_context(nc.Block())

        def mix_source(l, kind, a):
            def rows(w):
                return w.rearrange("(k p) n -> p k n", p=P)
            if kind == "in":
                return 8, 256, rows(w_in[l, :, a:a + 256])
            if kind == "in_last":
                return 8, 160, rows(w_in[l, :, a:a + 160])
            if kind == "xkv":
                return 8, 256, rows(w_xkv[l, :, a:a + 256])
            if kind == "xq":
                return 8, 256, rows(w_xq[l])
            if kind == "xo":
                return 2, 1024, rows(w_xo[l])
            if kind == "uq":
                return 3, 384, rows(w_uq[l, :, a:a + 384])
            if kind == "ukv":
                return 2, 1024, rows(w_ukv[l])
            if kind in ("branch01", "branch2"):
                src = rows(w_branch[l].rearrange("n c d -> (n c) d"))
                lo, n = (0, 8) if kind == "branch01" else (8, 4)
                return n, 256, src[:, lo:lo + n, a * 256:a * 256 + 256]
            half, kg = a
            return 4, 512, rows(w_out[l])[:, 4 * kg:4 * kg + 4, half * 512:half * 512 + 512]

        def quad_source(l, q, j):
            es = bass.ds(q * QUAD, QUAD)
            if j < 2 * KD:
                w, k = (w1 if j < KD else w3), j % KD
                return w[l][es, k * P:(k + 1) * P, :].rearrange("e p n -> p e n")
            half, k = divmod(j - 2 * KD, 4)
            return w2[l][es, k * P:(k + 1) * P, half * 512:half * 512 + 512].rearrange("e p n -> p e n")

        @block.sync
        def _(sp):
            more = sp.alloc_register("sp_more_rounds")
            sp.reg_mov(more, 0)
            sp.dma_start(con[:, :], consts).then_inc(con_in, 16)
            with sp.Fori(0, DEPTH) as l:
                for j, (kind, a) in enumerate(TURNS):
                    k, n, src = mix_source(l, kind, a)
                    sp.wait_ge(slot_free, l * PER_LAYER + (j + 1))
                    sp.dma_start(slot_k(j, k, n), src).then_inc(landed[j % RING], 16)
                with sp.Fori(0, QUADS) as q:
                    for j in range(PER_QUAD):
                        sp.wait_ge(slot_free, l * PER_LAYER + q * PER_QUAD + (Q_BASE + j + 1))
                        sp.dma_start(slot_k(j, QUAD, 512), quad_source(l, q, j)).then_inc(landed[j % RING], 16)
                sp.wait_ge(placed, l + 1)
                plain(sp)
                over = sp.value_load(flag[0:1, 0:1], min_val=0, max_val=1)
                with sp.If(over > 0):
                    sp.wait_ge(slot_free, l * PER_LAYER + (PER_LAYER + RING))
                    plain(sp)
                    with sp.Fori(0, PASSES - 1) as p:
                        with sp.Fori(0, QUADS) as q:
                            rd = sp.snap(more) + p * QUADS + q
                            for j in range(PER_QUAD):
                                sp.wait_ge(more_free, rd * PER_QUAD + (j + 1))
                                sp.dma_start(slot_k(j, QUAD, 512), quad_source(l, q, j))\
                                  .then_inc(more_landed[j % RING], 16)
                    sp.reg_add(more, more, (PASSES - 1) * QUADS)
                    sp.wait_ge(more_free, sp.snap(more) * PER_QUAD + RING)
                    plain(sp)
            for t in range(TT):
                sp.wait_ge(normed, 8 * DEPTH + t + 1)
                sp.dma_start(out[0, t * P:(t + 1) * P, :], h[:, t, :]).then_inc(stored, 16)
            sp.wait_ge(stored, 16 * TT)

        @block.gpsimd
        def _(pool):
            nc.gpsimd.dma_start(x[:, :, :], x_in[0].rearrange("(t p) n -> p t n", p=P)).then_inc(x_in_s, 16)
            nc.gpsimd.dma_start(posi[:, TT:TT + SEQ], pos_in[0:1, :].broadcast_to([P, SEQ])).then_inc(pos_in_s, 16)
            for t in range(TT):
                nc.gpsimd.dma_start(posi[:, t:t + 1], pos_in[0, t * P:(t + 1) * P].rearrange("(p a) -> p a", a=1))\
                  .then_inc(pos_in_s, 16)
            for l in range(DEPTH):
                for c in range(3):
                    nc.gpsimd.dma_start(gcol[:, l, c:c + 1], mla_q_norm_g[l, c * P:(c + 1) * P]
                                        .rearrange("(p a) -> p a", a=1)).then_inc(cols_in, 16)
                for c in range(2):
                    nc.gpsimd.dma_start(gcol[:, l, 3 + c:4 + c], mla_kv_norm_g[l, c * P:(c + 1) * P]
                                        .rearrange("(p a) -> p a", a=1)).then_inc(cols_in, 16)
                nc.gpsimd.dma_start(gcol[:, l, 5:6], diff_subln_g[l].rearrange("(p a) -> p a", a=1))\
                  .then_inc(cols_in, 16)
            nc.gpsimd.dma_start(wide[:, 0:2, :].rearrange("p a n -> p (a n)"),
                                diff_lambda.rearrange("l a d -> (l a d)").rearrange("(a n) -> a n", a=1)
                                .broadcast_to([P, DEPTH * 4 * A_DH])).then_inc(lam_in, 16)
            done = 0
            for tile, value in ([(stat[:, 8:9], EPS), (gpad[:, :, :], FAR)]
                                + [(kk[rows, :, cols], 0.0) for kk in (k0, k1, kx) for rows, cols in
                                   ((slice(0, 64), slice(SEQ, 2 * SEQ)), (slice(64, 128), slice(0, SEQ)))]):
                nc.gpsimd.memset(tile, value).then_inc(setup_pool, 1)
                done += 1
                pool.wait_ge(setup_pool, done)
            assert done == SETUP_ZEROS
            pool.sem_inc(zeroed, 1)

            def load_gain(g, l, turn):
                pool.wait_ge(gain_used, l * 4 + (turn + 1))
                plain(pool)
                nc.gpsimd.dma_start(gain[:, :], g.broadcast_to([P, D])).then_inc(gain_in, 16)

            with pool.Fori(0, DEPTH) as l:
                row = bass.ds(l, 1)
                pool.wait_ge(layer_done, l + 1)
                plain(pool)
                nc.gpsimd.dma_start(memx, mem_in[0].rearrange("(t p) n -> p t n", p=P)).then_inc(mem_arrived, 16)
                load_gain(mem_norm_g[row, :], l, 0)
                load_gain(mix_norm_g[row, :], l, 1)
                load_gain(cross_norm_g[row, :], l, 2)
                pool.wait_ge(a_normed, l + 1)
                plain(pool)
                nc.gpsimd.dma_start(router_w[:, :, 0:N_GROUPS], w_group[l].rearrange("(k p) n -> p k n", p=P))\
                  .then_inc(router_in, 16)
                nc.gpsimd.dma_start(router_w[:, :, N_GROUPS:], w_router[l].rearrange("(k p) n -> p k n", p=P))\
                  .then_inc(router_in, 16)
                nc.gpsimd.dma_start(router_b[:, 0:N_GROUPS], b_group[row, :].broadcast_to([P, N_GROUPS]))\
                  .then_inc(router_in, 16)
                nc.gpsimd.dma_start(router_b[:, N_GROUPS:], b_router[row, :].broadcast_to([P, N_EXPERTS]))\
                  .then_inc(router_in, 16)
                pool.wait_ge(scored, l * NI + X0)
                plain(pool)
                nc.gpsimd.memset(k0[0:64, :, SEQ:2 * SEQ], 0.0).then_inc(zeroed, 1)
                pool.wait_ge(zeroed, l * 2 + 2)
                plain(pool)
                nc.gpsimd.memset(k0[64:128, :, 0:SEQ], 0.0).then_inc(zeroed, 1)
                load_gain(ffn_norm_g[row, :], l, 3)
            load_gain(final_norm_g.rearrange("(a n) -> a n", a=1), DEPTH, 0)

        @block.scalar
        def _(act):
            more = act.alloc_register("act_more_rounds")
            act.reg_mov(more, 0)

            def norm(l, n, src, junk):
                if n == 1 or isinstance(l, int):
                    act.wait_ge(x_in_s, 16)
                    act.wait_ge(layer_done, l + 1)
                if n == 2:
                    act.wait_ge(x_added, l * 8 + 4)
                if n == 3:
                    act.wait_ge(x_added, l * 8 + 8)
                if n == 0 and not isinstance(l, int):
                    act.wait_ge(mem_arrived, l * 16 + 16)
                    act.wait_ge(layer_done, l + 1)
                if n == 1:
                    act.wait_ge(normed, l * 8 + 2)
                for t in range(TT):
                    nc.scalar.activation(junk[:, t, :], src[:, t, :], ACT.Square,
                                         accum_out=stat[:, t:t + 1]).then_inc(squared, 1)
                act.wait_ge(squared, l * 8 + (2 * n + 2))
                nc.scalar.activation(stat[:, 2:4], stat[:, 0:2], ACT.Ln, scale=1.0 / D, bias=stat[:, 8:9])\
                  .then_inc(rstd, 1)
                act.wait_ge(rstd, l * 8 + (2 * n + 1))
                nc.scalar.activation(stat[:, 4:6], stat[:, 2:4], ACT.Exp, scale=-0.5).then_inc(rstd, 1)

            def copy_hT(l, n):
                for g in (0, 2):
                    act.wait_ge(turned, l * 16 + (4 * n + g + 1))
                    if n == 1 and g == 0:
                        wait_made(act, l, "vx")
                    nc.scalar.activation(hT[:, 2 * g:2 * g + 2, :], bank_n(g), ACT.Copy).then_inc(hT_act, 1)

            def job(l, name):
                n = JOB_NAMES.index(name)
                wait_made(act, l, name)
                b = bank[n % 2][:, :]
                b2 = b.rearrange("p (a n) -> p a n", a=2)
                kind, i = name[:-1], name[-1]
                if name == "kx":
                    nc.scalar.activation(kx[0:64, :, 0:SEQ], b2[0:64], ACT.Copy)
                    last = nc.scalar.activation(kx[64:128, :, SEQ:2 * SEQ], b2[64:128], ACT.Copy)
                elif kind in ("aq", "bq"):
                    dst = q0 if kind == "aq" else q1
                    if name == "aq0":
                        wait_made(act, l, "vx")
                    last = nc.scalar.activation(dst[:, 2 * int(i):2 * int(i) + 2, :], b2, ACT.Copy, scale=A_DH ** -0.5)
                elif kind in ("ak", "bk"):
                    dst, c = (k0 if kind == "ak" else k1), 2 * int(i)
                    act.wait_ge(zeroed, l * 2 + 1)
                    nc.scalar.activation(dst[0:64, c:c + 2, 0:SEQ], b2[0:64], ACT.Copy)
                    last = nc.scalar.activation(dst[64:128, c:c + 2, SEQ:2 * SEQ], b2[64:128], ACT.Copy)
                elif kind in ("av", "bv"):
                    dst, c = (v0 if kind == "av" else v1), 256 * int(i)
                    last = nc.scalar.activation(dst[:, :, c:c + 256], b2, ACT.Copy)
                elif name == "cs":
                    nc.scalar.activation(wide[:, 0, :], b2[:, 0], ACT.Ln, scale=1.0 / C_Q_RANK, bias=stat[:, 8:9])
                    last = nc.scalar.activation(wide[:, 1, :], b2[:, 1], ACT.Ln, scale=1.0 / C_KV_RANK,
                                                bias=stat[:, 8:9])
                    last.then_inc(copied["act"], 1)
                    wait_copied(act, l, "cs")
                    nc.scalar.activation(wide[:, 2:4, :], wide[:, 0:2, :], ACT.Exp, scale=-0.5).then_inc(c_rstd, 1)
                    return
                elif kind == "cq":
                    c = 2 * int(i)
                    last = nc.scalar.activation(q0[0:C_DH, c:c + 2, :], b2[0:C_DH], ACT.Copy, scale=C_DH ** -0.5)
                elif kind == "ck" and name != "ckr":
                    c = 2 * int(i)
                    last = nc.scalar.activation(kc[0:C_NOPE, c:c + 2, :], b2[0:C_NOPE], ACT.Copy)
                elif kind == "cv":
                    last = nc.scalar.activation(v0[:, int(i), :], b, ACT.Copy)
                elif kind == "as":
                    c = 2 * int(i)
                    last = nc.scalar.activation(wide[:, c:c + 2, :], b2, ACT.Ln, scale=1.0 / A_DV, bias=stat[:, 8:9])
                last.then_inc(copied["act"], 1)

            def experts_round(S, wait_w1, wait_w2a, rd, look):
                def copy_xt(k):
                    act.wait_ge(S["gathered"], k)
                    nc.scalar.activation(xt[:, 0:4, :], bank[0][:, :].rearrange("p (c n) -> p c n", c=4), ACT.Copy)\
                      .then_inc(S["xt_act"], 1)
                if look is None:
                    copy_xt(rd + 1)
                wait_w1(act)
                nc.scalar.activation(act_e, bank[2][:, :], ACT.Exp, scale=-1.0).then_inc(S["e_made"], 1)
                if look is not None:
                    copy_xt(look)
                act.wait_ge(S["selw_turned"], rd + 1)
                nc.scalar.activation(selwT, bank[5][:, 0:256], ACT.Copy).then_inc(S["selwT_copied"], 1)
                act.wait_ge(S["hidden_turned"], rd + 1)
                nc.scalar.activation(hiddenT, bank[4][:, :].rearrange("p (c n) -> p c n", c=4), ACT.Copy)\
                  .then_inc(S["hiddenT_copied"], 1)
                wait_w2a(act)
                nc.scalar.activation(yexp[:, 0:512], bank[6][:, :], ACT.Copy).then_inc(S["y_act"], 1)

            act.wait_ge(setup_pool, SETUP_ZEROS)
            act.wait_ge(con_in, 16)
            act.wait_ge(setup_dve, SETUP_ANGLES)
            nc.scalar.activation(ropes[64:96, 0, :], angles[64:96, 0, :], ACT.Sin)
            nc.scalar.activation(ropes[64:96, 1, :], angles[64:96, 1, :], ACT.Sin)
            nc.scalar.activation(small[:, 4:8], small[:, 0:4], ACT.Exp).then_inc(setup_act, 1)

            with act.Fori(0, DEPTH) as l:
                norm(l, 0, memx, memjunk)
                copy_hT(l, 0)
                job(l, "kx")
                norm(l, 1, x, h)
                copy_hT(l, 1)
                for name in ("aq0", "ak0", "av0"):
                    job(l, name)

                def exps(i):
                    pb, m = i % NPB, mx[:, i % NPB, :]
                    act.wait_ge(maxed, l * NI + (i + 1))
                    plain = i >= C0
                    if i >= NPB:
                        act.wait_ge(probs_turned, l * NI + (i - NPB + 1))
                    for j in range(2):
                        src = bank[2 + i % 2][:, j * SEQ:(j + 1) * SEQ] if plain else prob[:, pb, j, :]
                        last = nc.scalar.activation(prob[:, pb, j, :], src, ACT.Exp, bias=m[:, j:j + 1],
                                                    accum_out=sm[:, pb, j:j + 1])
                    last.then_inc(exped, 1)

                def copy_probsT(i):
                    act.wait_ge(probs_turned, l * NI + (i + 1))
                    if i >= 2:
                        act.wait_ge(pv_done, l * NI + (i - 1))
                    n = 1 if i < B0 else 2
                    nc.scalar.activation(probT[:, i % 2, 0:n, :, :].rearrange("p a b n -> p (a b) n"),
                                         bank[4 + i % 2][:, 0:n * 256].rearrange("p (c n) -> p c n", n=P),
                                         ACT.Copy).then_inc(probsT_copied, 1)

                for i in range(X0 + LAG_OUT):
                    if i < X0:
                        exps(i)
                    if i == 8:
                        wait_copied(act, l, "c2")
                        act.wait_ge(scored, l * NI + B0)
                        nc.scalar.activation(q0[:, 0:5, :], cT[:, :, :], ACT.Square).then_inc(c_squared, 1)
                    if i == 18:
                        act.wait_ge(out_copied, l * (NI // 2) + 4)
                        act.wait_ge(c_scaled, l * 5 + 5)
                        nc.scalar.activation(wide[:, :, :], oa[:, :, :], ACT.Square).then_inc(a_squared, 1)
                    for name in FILL.get(i, []):
                        if JOBS[JOB_NAMES.index(name)][3] == "act":
                            if name == "cq0":
                                wait_copied(act, l, "cs")
                            if name == "cv0":
                                act.wait_ge(pv_done, l * NI + B0)
                            job(l, name)
                    if i == 20:
                        wait_copied(act, l, "as1")
                        nc.scalar.activation(wide[:, :, :], wide[:, :, :], ACT.Exp, scale=-0.5).then_inc(a_rstd, 1)
                    if LAG_T <= i < X0 + LAG_T:
                        copy_probsT(i - LAG_T)
                for pair in range(4):
                    for n in range(N_BRANCHES):
                        wait_free(act, l, T_GATE + 5 * pair + n)
                        act.wait_ge(mix_sum, l * 4 + (pair + 1))
                        nc.scalar.activation(flat[n], bank[(6 * pair + n) % 8][:, :], ACT.Exp, scale=-1.0)\
                          .then_inc(gate_exp, 1)
                norm(l, 2, x, h)
                copy_hT(l, 2)
                wait_free(act, l, T_XQ)
                nc.scalar.activation(q1[:, 0:2, :], bank[0][:, :].rearrange("p (a n) -> p a n", a=2), ACT.Copy,
                                     scale=X_DH ** -0.5).then_inc(qx_copied, 1)
                for i in range(X0, NI + LAG_T):
                    if i < NI:
                        exps(i)
                    if i >= X0 + LAG_T:
                        copy_probsT(i - LAG_T)
                norm(l, 3, x, h)
                copy_hT(l, 3)
                for t in range(TT):
                    act.wait_ge(route_ask, l * 2 + (t + 1))
                    nc.scalar.activation(small[:, 16 + 4 * t:20 + 4 * t], logit[:, t, 0:N_GROUPS], ACT.Exp,
                                         bias=small[:, 10 + 2 * t:11 + 2 * t], accum_out=small[:, 24 + 2 * t:25 + 2 * t])
                    nc.scalar.activation(small[:, 25 + 2 * t:26 + 2 * t], top[:, t, 2, 1:2], ACT.Exp,
                                         bias=small[:, 11 + 2 * t:12 + 2 * t]).then_inc(route_exp, 1)
                S = main_r
                act.wait_ge(S["gathered"], l * (QUADS + 1) + 1)
                nc.scalar.activation(xt[:, 0:4, :], bank[0][:, :].rearrange("p (c n) -> p c n", c=4), ACT.Copy)\
                  .then_inc(S["xt_act"], 1)
                with act.Fori(0, QUADS) as q:
                    base = l * PER_LAYER + q * PER_QUAD
                    experts_round(S, lambda e: e.wait_ge(slot_free, base + (Q_BASE + RING + KD)),
                                  lambda e: e.wait_ge(slot_free, base + (Q_BASE + RING + 2 * KD + 4)),
                                  l * QUADS + q, l * (QUADS + 1) + q + 2)
                act.wait_ge(placed, l + 1)
                plain(act)
                over = act.value_load(flag[0:1, 0:1], min_val=0, max_val=1)
                with act.If(over > 0):
                    with act.Fori(0, PASSES - 1) as p:
                        with act.Fori(0, QUADS) as q:
                            rd = act.snap(more) + p * QUADS + q
                            experts_round(more_r, lambda e: e.wait_ge(more_free, rd * PER_QUAD + (RING + KD)),
                                          lambda e: e.wait_ge(more_free, rd * PER_QUAD + (RING + 2 * KD + 4)), rd, None)
                    act.reg_add(more, more, (PASSES - 1) * QUADS)
            norm(DEPTH, 0, x, h)

        @block.vector
        def _(dve):
            more = dve.alloc_register("dve_more_rounds")
            dve.reg_mov(more, 0)
            more_passes = dve.alloc_register("dve_more_passes")
            dve.reg_mov(more_passes, 0)
            steps = [0]

            def then(ins):
                steps[0] += 1
                ins.then_inc(setup_dve, 1)
                dve.wait_ge(setup_dve, steps[0])

            dve.wait_ge(pos_in_s, 16 * (TT + 1))
            dve.wait_ge(con_in, 16)
            dve.wait_ge(setup_pool, SETUP_ZEROS)
            dve.wait_ge(cols_in, 16 * 6 * DEPTH)
            dve.wait_ge(lam_in, 16)
            then(nc.vector.tensor_copy(posf[:, :], posi[:, :]))
            for b in range(TT):
                then(nc.vector.tensor_scalar(dist[:, b, :], posf[:, TT:], posf[:, b:b + 1], None, ALU.subtract))
                then(nc.vector.scalar_tensor_tensor(dist[:, b, :], dist[:, b, :], -1.0, dist[:, b, :], ALU.mult, ALU.max))
            r = slice(C_NOPE, C_DH)
            ang, turns = wide[r, 2, :], wide[r, 3, :]
            then(nc.vector.tensor_scalar(ang, posf[r, TT:], con[r, C_INV:C_INV + 1], None, ALU.mult))
            for dst, quarter in ((1, 0.0), (0, 0.25)):
                w = angles[r, dst, :]
                then(nc.vector.tensor_scalar(turns, ang, 1.0 / (2 * math.pi), quarter, ALU.mult, ALU.add))
                then(nc.vector.tensor_scalar(turns, turns, 12582912.0, None, ALU.add))
                then(nc.vector.tensor_scalar(turns, turns, -12582912.0, None, ALU.add))
                then(nc.vector.scalar_tensor_tensor(w, turns, -TWO_PI[0], ang, ALU.mult, ALU.add))
                then(nc.vector.scalar_tensor_tensor(w, turns, -TWO_PI[1], w, ALU.mult, ALU.add))
                then(nc.vector.scalar_tensor_tensor(w, turns, -TWO_PI[2], w, ALU.mult, ALU.add))
                then(nc.vector.tensor_scalar(w, w, quarter * 2 * math.pi, 3.1415925, ALU.add, ALU.min))
                then(nc.vector.tensor_scalar(w, w, -3.1415925, None, ALU.max))
            lq = wide[:, 0:2, :].rearrange("p l (a b d) -> p (l a) b d", b=2, d=A_DH)
            pr = cT[:, 0, :].rearrange("p (a d) -> p a d", d=A_DH)
            then(nc.vector.tensor_tensor(pr, lq[:, :, 0, :], lq[:, :, 1, :], ALU.mult))
            then(nc.vector.tensor_reduce(small[:, 0:4], pr, AX_X, ALU.add))
            assert steps[0] == SETUP_ANGLES
            dve.wait_ge(setup_act, 1)
            ex = small[:, 4:8].rearrange("p (l a) -> p l a", a=2)
            then(nc.vector.tensor_tensor(small[:, 8:10], ex[:, :, 1], ex[:, :, 0], ALU.subtract))
            then(nc.vector.tensor_tensor(lamt[:, :], small[:, 8:10], con[:, C_LAM:C_LAM + DEPTH], ALU.subtract))
            then(nc.vector.tensor_tensor(gcol[:, :, 5], gcol[:, :, 5], con[:, C_LAM + DEPTH:C_LAM + 2 * DEPTH], ALU.mult))
            for count in (gain_used, layer_done, mix_sum, main_r["added"], more_r["added"]):
                dve.sem_inc(count, 1)

            def norm(l, n, src, dst):
                dve.wait_ge(gain_in, l * 64 + (16 * n + 16))
                dve.wait_ge(rstd, l * 8 + (2 * n + 2))
                for t in range(TT):
                    last = nc.vector.scalar_tensor_tensor(dst[:, t, :], src[:, t, :], stat[:, 4 + t:5 + t], gain[:, :],
                                                          ALU.mult, ALU.mult)
                    last.then_inc(normed, 1)
                dve.wait_ge(normed, l * 8 + (2 * n + 2))
                dve.sem_inc(gain_used, 1)

            def copy_hT(l, n):
                for g in (1, 3):
                    dve.wait_ge(turned, l * 16 + (4 * n + g + 1))
                    nc.vector.tensor_copy(hT[:, 2 * g:2 * g + 2, :], bank_n(g)).then_inc(hT_dve, 1)

            def rope(l, n, dst, src, heads):
                cos = ropes[r, 0:1, :].broadcast_to([C_ROPE, heads, SEQ])
                sin = ropes[r, 1:2, :].broadcast_to([C_ROPE, heads, SEQ])
                tmp = oBC[r, 6:6 + heads, :]
                nc.vector.tensor_tensor(tmp, src, sin, ALU.mult).then_inc(rope_step, 1)
                nc.vector.tensor_tensor(dst, dst, cos, ALU.mult).then_inc(rope_step, 1)
                dve.wait_ge(rope_step, l * 10 + (2 * n + 2))
                return nc.vector.tensor_tensor(dst, dst, tmp, ALU.add)

            def job(l, name):
                n = JOB_NAMES.index(name)
                wait_made(dve, l, name)
                b = bank[n % 2][:, :]
                b2 = b.rearrange("p (a n) -> p a n", a=2)
                kind, i = name[:-1], name[-1]
                if name == "vx":
                    last = nc.vector.tensor_copy(vx[:, :, :], b2)
                elif kind in ("aq", "bq"):
                    dst = q0 if kind == "aq" else q1
                    last = nc.vector.tensor_scalar(dst[:, 2 * int(i):2 * int(i) + 2, :], b2, A_DH ** -0.5, None, ALU.mult)
                elif kind in ("ak", "bk"):
                    dst, c = (k0 if kind == "ak" else k1), 2 * int(i)
                    dve.wait_ge(zeroed, l * 2 + 1)
                    nc.vector.tensor_copy(dst[0:64, c:c + 2, 0:SEQ], b2[0:64])
                    last = nc.vector.tensor_copy(dst[64:128, c:c + 2, SEQ:2 * SEQ], b2[64:128])
                elif kind in ("av", "bv"):
                    dst, c = (v0 if kind == "av" else v1), 256 * int(i)
                    last = nc.vector.tensor_copy(dst[:, :, c:c + 256], b2)
                elif name in ("c0", "c1"):
                    c = 2 * int(i)
                    last = nc.vector.tensor_copy(cT[:, c:c + 2, :], b2)
                elif name == "c2":
                    dve.wait_ge(scored, l * NI + B0)
                    nc.vector.tensor_copy(cT[:, 4, :], b2[:, 0, :])
                    last = nc.vector.tensor_copy(kc[r, 0, :], b2[r, 1, :])
                elif kind == "ck" and name != "ckr":
                    c = 2 * int(i)
                    last = nc.vector.tensor_copy(kc[0:C_NOPE, c:c + 2, :], b2[0:C_NOPE])
                elif kind == "cr":
                    c = 2 * int(i)
                    last = rope(l, 1 + int(i), q0[r, c:c + 2, :], b2[r], 2)
                elif name == "ckr":
                    last = rope(l, 0, kc[r, 0:1, :], b2[r, 0:1, :], 1)
                    last.then_inc(copied["dve"], 1)
                    wait_copied(dve, l, "ckr")
                    nc.vector.tensor_copy(kc[r, 1:8, :], kc[r, 0:1, :].broadcast_to([C_ROPE, 7, SEQ]))\
                      .then_inc(kr_spread, 1)
                    return
                last.then_inc(copied["dve"], 1)

            def maxima(l, i):
                pb = i % NPB
                src = bank[2 + i % 2][:, :].rearrange("p (a n) -> p a n", a=2)
                dve.wait_ge(scored, l * NI + (i + 1))
                b = i % 2
                if i >= NPB:
                    dve.wait_ge(probs_turned, l * NI + (i - NPB + 1))
                if i < B0:
                    nc.vector.scalar_tensor_tensor(prob[:, pb, :, :], dist[:, b:b + 1, :].broadcast_to([P, 2, SEQ]),
                                                   -slopes(A_HEADS)[i // 2], src, ALU.mult, ALU.add).then_inc(biased, 1)
                elif i < C0:
                    hd = 2 * ((i - B0) // 2)
                    at = C_STRIP + hd * STRIP
                    strip = con[:, at:at + 2 * STRIP].rearrange("p (a n) -> p a n", a=2)[:, :, P - b * P:P - b * P + SEQ]
                    nc.vector.tensor_tensor(prob[:, pb, :, :], src, strip, ALU.add).then_inc(biased, 1)
                if i < C0:
                    dve.wait_ge(biased, l * C0 + (i + 1))
                    src = prob[:, pb, :, :]
                nc.vector.tensor_reduce(mx[:, pb, :], src, AX_X, ALU.max, negate=True).then_inc(maxed, 1)

            def weigh(l, i):
                pb = i % NPB
                dve.wait_ge(exped, l * NI + (i + 1))
                nc.vector.reciprocal(rs[:, pb, 0:2], sm[:, pb, :]).then_inc(inverted, 1)
                dve.wait_ge(inverted, l * NI + (i + 1))
                if i < B0:
                    nc.vector.tensor_scalar(rs[:, pb, 2:3], rs[:, pb, 1:2], lamcur, None, ALU.mult).then_inc(a_scaled, 1)
                    dve.wait_ge(a_scaled, l * 16 + (2 * i + 1))
                    nc.vector.tensor_scalar(prob[:, pb, 1, :], prob[:, pb, 1, :], rs[:, pb, 2:3], None, ALU.mult)\
                      .then_inc(a_scaled, 1)
                    dve.wait_ge(a_scaled, l * 16 + (2 * i + 2))
                    nc.vector.scalar_tensor_tensor(prob[:, pb, 0, :], prob[:, pb, 0, :], rs[:, pb, 0:1],
                                                   prob[:, pb, 1, :], ALU.mult, ALU.add).then_inc(weighed, 1)
                else:
                    nc.vector.tensor_scalar(prob[:, pb, 0, :], prob[:, pb, 0, :], rs[:, pb, 0:1], None, ALU.mult)
                    nc.vector.tensor_scalar(prob[:, pb, 1, :], prob[:, pb, 1, :], rs[:, pb, 1:2], None, ALU.mult)\
                      .then_inc(weighed, 1)

            def copy_out(l, u):
                dve.wait_ge(pv_done, l * NI + (2 * u + 2))
                if u < 4:
                    dst = oa[:, u, :]
                elif u < 12:
                    dst = oBC[:, u - 4, :]
                else:
                    dst = oa[:, u - 12, :]
                nc.vector.tensor_copy(dst, bank[6 + u % 2][:, 0:SEQ]).then_inc(out_copied, 1)

            def experts_round(S, wait_w3, wait_w2b, rd, q, look, sel_next):
                def make_sel(cols):
                    nc.vector.tensor_tensor(
                        sel.rearrange("p t (e s) -> p t e s", e=QUAD),
                        iota.rearrange("p (a b s) -> p a b s", a=1, b=1).broadcast_to([P, TT, QUAD, CAP]),
                        place[:, :, cols].rearrange("p t (e s) -> p t e s", s=1).broadcast_to([P, TT, QUAD, CAP]),
                        ALU.is_equal).then_inc(S["sel_made"], 1)

                def copy_xt(k):
                    dve.wait_ge(S["gathered"], k)
                    nc.vector.tensor_copy(xt[:, 4:8, :], bank[1][:, :].rearrange("p (c n) -> p c n", c=4))\
                       .then_inc(S["xt_dve"], 1)

                if look is not None:
                    make_sel(bass.ds(q * QUAD + QUAD, QUAD))
                else:
                    make_sel(bass.ds(q * QUAD, QUAD))
                    copy_xt(rd + 1)
                here = bass.ds(q * QUAD, QUAD)
                sw = selw.rearrange("p t (e s) -> p t e s", e=QUAD)
                nc.vector.tensor_tensor(
                    sw, iota.rearrange("p (a b s) -> p a b s", a=1, b=1).broadcast_to([P, TT, QUAD, CAP]),
                    place[:, :, here].rearrange("p t (e s) -> p t e s", s=1).broadcast_to([P, TT, QUAD, CAP]),
                    ALU.is_equal).then_inc(S["selw_step"], 1)
                dve.wait_ge(S["selw_step"], rd + 1)
                nc.vector.tensor_tensor(
                    sw, sw, weight[:, :, here].rearrange("p t (e s) -> p t e s", s=1).broadcast_to([P, TT, QUAD, CAP]),
                    ALU.mult).then_inc(S["selw_made"], 1)
                dve.wait_ge(S["e_made"], rd + 1)
                nc.vector.tensor_scalar(act_e, act_e, 1.0, None, ALU.add).then_inc(S["silu_step"], 1)
                dve.wait_ge(S["silu_step"], rd * 3 + 1)
                nc.vector.reciprocal(act_r, act_e).then_inc(S["silu_step"], 1)
                dve.wait_ge(S["silu_step"], rd * 3 + 2)
                nc.vector.tensor_tensor(act_r, bank[2][:, :], act_r, ALU.mult).then_inc(S["silu_step"], 1)
                dve.wait_ge(S["silu_step"], rd * 3 + 3)
                wait_w3(dve)
                nc.vector.tensor_tensor(hidden, bank[3][:, :], act_r, ALU.mult).then_inc(S["hidden_made"], 1)
                if look is not None:
                    copy_xt(look)
                wait_w2b(dve)
                nc.vector.tensor_copy(yexp[:, 512:1024], bank[7][:, :]).then_inc(S["y_dve"], 1)
                for c in range(4):
                    t, half = divmod(c, 2)
                    dve.wait_ge(S["combined"], rd * 4 + (c + 1))
                    xs = x[:, t, half * 512:half * 512 + 512]
                    nc.vector.tensor_tensor(xs, xs, bank[(5, 2)[c % 2]][:, :], ALU.add).then_inc(S["added"], 1)

            gcur, lamcur = small[:, 40:46], small[:, 46:47]
            with dve.Fori(0, DEPTH) as l:
                row = bass.ds(l, 1)
                nc.vector.tensor_copy(gcur, gcol[:, row, :].rearrange("p a n -> p (a n)")).then_inc(layer_cols, 1)
                nc.vector.tensor_copy(lamcur, lamt[:, row]).then_inc(layer_cols, 1)
                norm(l, 0, memx, memx)
                copy_hT(l, 0)
                job(l, "vx")
                norm(l, 1, x, h)
                wait_made(dve, l, "vx")
                copy_hT(l, 1)
                for name in ("aq1", "ak1", "av1"):
                    job(l, name)
                for i in range(X0 + LAG_OUT + 1):
                    if i < X0:
                        maxima(l, i)
                    if 1 <= i <= X0:
                        if i == 1:
                            dve.wait_ge(layer_cols, l * 2 + 2)
                        weigh(l, i - 1)
                    for name in FILL.get(i, []):
                        if JOBS[JOB_NAMES.index(name)][3] == "dve":
                            job(l, name)
                    if i == 10:
                        dve.wait_ge(c_rstd, l + 1)
                        for c in range(5):
                            nc.vector.scalar_tensor_tensor(cT[:, c, :], cT[:, c, :], gcur[:, c:c + 1],
                                                           wide[:, 2 + c // 3, :], ALU.mult, ALU.mult).then_inc(c_scaled, 1)
                    if i == 21:
                        dve.wait_ge(a_rstd, l + 1)
                        nc.vector.scalar_tensor_tensor(oa[:, :, :], oa[:, :, :], gcur[:, 5:6], wide[:, :, :],
                                                       ALU.mult, ALU.mult).then_inc(a_normed, 1)
                    if i >= LAG_OUT and (i - LAG_OUT) % 2 == 1:
                        copy_out(l, (i - LAG_OUT) // 2)
                for pair in range(4):
                    for n in range(N_BRANCHES):
                        e = flat[n]
                        g = 3 * pair + n
                        dve.wait_ge(gate_exp, l * 12 + (g + 1))
                        nc.vector.tensor_scalar(e, e, 1.0, None, ALU.add).then_inc(gate_step, 1)
                        dve.wait_ge(gate_step, l * 28 + (7 * pair + 2 * n + 1))
                        nc.vector.reciprocal(e, e).then_inc(gate_step, 1)
                        dve.wait_ge(gate_step, l * 28 + (7 * pair + 2 * n + 2))
                        if n == 0:
                            dve.wait_ge(branch0, l * 4 + (pair + 1))
                        else:
                            wait_free(dve, l, T_GATE + 5 * pair + 2 + n)
                        nc.vector.tensor_tensor(e, bank[(6 * pair + 3 + n) % 8][:, :], e, ALU.mult).then_inc(mixed, 1)
                    dve.wait_ge(mixed, l * 12 + (3 * pair + 3))
                    nc.vector.tensor_tensor(flat[0], flat[0], flat[1], ALU.add).then_inc(gate_step, 1)
                    dve.wait_ge(gate_step, l * 28 + (7 * pair + 7))
                    nc.vector.tensor_tensor(q0[:, 2 * pair:2 * pair + 2, :].rearrange("p a n -> p (a n)"), flat[0],
                                            flat[2], ALU.add).then_inc(mix_sum, 1)
                for o in range(4):
                    half, t = divmod(o, 2)
                    if t == 0:
                        dve.wait_ge(projected, l * 5 + (half + 1))
                    else:
                        wait_free(dve, l, T_OUT + 2 * half + 1)
                    xs = x[:, t, half * 512:half * 512 + 512]
                    nc.vector.tensor_tensor(xs, xs, bank[o][:, :], ALU.add).then_inc(x_added, 1)
                dve.wait_ge(x_added, l * 8 + 4)
                norm(l, 2, x, h)
                copy_hT(l, 2)
                for i in range(X0, NI + LAG_OUT):
                    if i < NI:
                        maxima(l, i)
                    if X0 < i <= NI:
                        weigh(l, i - 1)
                    if i - LAG_OUT >= X0 and (i - LAG_OUT) % 2 == 1:
                        copy_out(l, (i - LAG_OUT) // 2)
                for o in range(4):
                    t, half = divmod(o, 2)
                    if o < 3:
                        dve.wait_ge(projected, l * 5 + (2 + o + 1))
                    else:
                        wait_free(dve, l, T_XO)
                    xs = x[:, t, half * 512:half * 512 + 512]
                    nc.vector.tensor_tensor(xs, xs, bank[o][:, :], ALU.add).then_inc(x_added, 1)
                dve.wait_ge(x_added, l * 8 + 8)
                norm(l, 3, x, h)
                copy_hT(l, 3)

                rstep = [0]

                def step(ins):
                    rstep[0] += 1
                    ins.then_inc(route_step, 1)
                    dve.wait_ge(route_step, l * ROUTE_STEPS + rstep[0])
                    plain(dve)

                dve.wait_ge(router_in, l * 64 + 64)
                dve.wait_ge(logits_made, l + 1)
                nc.vector.memset(place[:, :, N_EXPERTS:], -1.0)
                nc.vector.memset(weight[:, :, N_EXPERTS:], 0.0)
                step(nc.vector.tensor_tensor(logit[:, :, :],
                                             bank[0][:, 0:128].rearrange("p (t n) -> p t n", t=TT)[:, :, 0:36],
                                             router_b[:, :].rearrange("p (a n) -> p a n", a=1)
                                             .broadcast_to([P, TT, 36]), ALU.add))
                step(nc.vector.tensor_copy(gpad[:, :, 0:N_GROUPS], logit[:, :, 0:N_GROUPS]))
                for t in range(TT):
                    f = small[:, 48 + 8 * t:56 + 8 * t]
                    el = logit[:, t, N_GROUPS:]
                    step(nc.vector.max(top[:, t, 0, :], gpad[:, t, :]))
                    step(nc.vector.max_index(topi[:, t, 0, :], top[:, t, 0, :], gpad[:, t, :]))
                    step(nc.vector.tensor_copy(f[:, 0:1], topi[:, t, 0, 0:1]))
                    step(nc.vector.tensor_scalar(rt[:, t, 0, :], con[:, C_GID:C_GID + N_EXPERTS], f[:, 0:1], None,
                                                 ALU.is_equal))
                    step(nc.vector.tensor_scalar(rt[:, t, 0, :], rt[:, t, 0, :], -FAR, FAR, ALU.mult, ALU.add))
                    step(nc.vector.tensor_tensor(rt[:, t, 1, :], rt[:, t, 0, :], el, ALU.add))
                    step(nc.vector.max(top[:, t, 2, :], rt[:, t, 1, :]))
                    step(nc.vector.max_index(topi[:, t, 1, :], top[:, t, 2, :], rt[:, t, 1, :]))
                    step(nc.vector.tensor_copy(f[:, 1:3], topi[:, t, 1, 0:2]))
                    nc.vector.tensor_scalar(small[:, 10 + 2 * t:11 + 2 * t], top[:, t, 0, 0:1], -1.0, None, ALU.mult)
                    nc.vector.tensor_scalar(small[:, 11 + 2 * t:12 + 2 * t], top[:, t, 2, 0:1], -1.0, None, ALU.mult)\
                      .then_inc(route_ask, 1)
                    i1, i2 = f[:, 1:2], f[:, 2:3]
                    experts = con[:, C_IOTA:C_IOTA + N_EXPERTS]
                    step(nc.vector.tensor_scalar(rt[:, t, 2, :], experts, i1, None, ALU.is_equal))
                    step(nc.vector.tensor_scalar(rt[:, t, 3, :], experts, i2, None, ALU.is_equal))
                    nc.vector.tensor_tensor(chosen[:, t, :], rt[:, t, 2, :], rt[:, t, 3, :], ALU.add).then_inc(chosen_s, 1)
                for t in range(TT):
                    f = small[:, 48 + 8 * t:56 + 8 * t]
                    sg, q2 = small[:, 24 + 2 * t:25 + 2 * t], small[:, 25 + 2 * t:26 + 2 * t]
                    dve.wait_ge(route_exp, l * 2 + (t + 1))
                    step(nc.vector.tensor_scalar(f[:, 3:4], q2, 1.0, sg, ALU.add, ALU.mult))
                    step(nc.vector.reciprocal(f[:, 4:5], f[:, 3:4]))
                    step(nc.vector.tensor_tensor(f[:, 5:6], f[:, 4:5], q2, ALU.mult))
                    step(nc.vector.tensor_scalar(rt[:, t, 3, :], rt[:, t, 3, :], f[:, 5:6], None, ALU.mult))
                    step(nc.vector.scalar_tensor_tensor(weight[:, t, 0:N_EXPERTS], rt[:, t, 2, :], f[:, 4:5],
                                                        rt[:, t, 3, :], ALU.mult, ALU.add))
                dve.wait_ge(ranked, l + 1)
                rank = bank[1][:, 0:64].rearrange("p (t n) -> p t n", t=TT)
                step(nc.vector.scalar_tensor_tensor(place[:, :, 0:N_EXPERTS], rank, 1.0, chosen[:, :, :], ALU.add, ALU.mult))
                step(nc.vector.tensor_scalar(place[:, :, 0:N_EXPERTS], place[:, :, 0:N_EXPERTS], -1.0, None, ALU.add))
                step(nc.vector.tensor_reduce(small[:, 47:48], bank[1][:, 64:96], AX_X, ALU.max))
                nc.vector.tensor_scalar(flag[:, :], small[:, 47:48], float(CAP), None, ALU.is_gt).then_inc(placed, 1)
                assert rstep[0] == ROUTE_STEPS

                S = main_r
                nc.vector.tensor_tensor(
                    sel.rearrange("p t (e s) -> p t e s", e=QUAD),
                    iota.rearrange("p (a b s) -> p a b s", a=1, b=1).broadcast_to([P, TT, QUAD, CAP]),
                    place[:, :, 0:QUAD].rearrange("p t (e s) -> p t e s", s=1).broadcast_to([P, TT, QUAD, CAP]),
                    ALU.is_equal).then_inc(S["sel_made"], 1)
                dve.wait_ge(S["gathered"], l * (QUADS + 1) + 1)
                nc.vector.tensor_copy(xt[:, 4:8, :], bank[1][:, :].rearrange("p (c n) -> p c n", c=4))\
                   .then_inc(S["xt_dve"], 1)
                with dve.Fori(0, QUADS) as q:
                    base = l * PER_LAYER + q * PER_QUAD
                    experts_round(S, lambda e: e.wait_ge(slot_free, base + (Q_BASE + RING + 2 * KD)),
                                  lambda e: e.wait_ge(slot_free, base + (Q_BASE + RING + PER_QUAD)),
                                  l * QUADS + q, q, l * (QUADS + 1) + q + 2, None)
                dve.wait_ge(S["added"], l * (4 * QUADS) + (4 * QUADS + 1))
                dve.wait_ge(placed, l + 1)
                plain(dve)
                over = dve.value_load(flag[0:1, 0:1], min_val=0, max_val=1)
                with dve.If(over > 0):
                    with dve.Fori(0, PASSES - 1) as p:
                        nc.vector.tensor_scalar(place[:, :, 0:N_EXPERTS], place[:, :, 0:N_EXPERTS], -float(CAP), None,
                                                ALU.add).then_inc(shifted, 1)
                        with dve.Fori(0, QUADS) as q:
                            rd = dve.snap(more) + p * QUADS + q
                            dve.wait_ge(shifted, dve.snap(more_passes) + p + 1)
                            experts_round(more_r, lambda e: e.wait_ge(more_free, rd * PER_QUAD + (RING + 2 * KD)),
                                          lambda e: e.wait_ge(more_free, rd * PER_QUAD + (RING + PER_QUAD)),
                                          rd, q, None, None)
                    dve.reg_add(more, more, (PASSES - 1) * QUADS)
                    dve.reg_add(more_passes, more_passes, PASSES - 1)
                    dve.wait_ge(more_r["added"], dve.snap(more) * 4 + 1)
                    plain(dve)
                dve.sem_inc(layer_done, 1)
            norm(DEPTH, 0, x, h)

        @block.tensor
        def _(pe):
            more = pe.alloc_register("pe_more_rounds")
            pe.reg_mov(more, 0)
            pe.sem_inc(slot_free, RING)
            pe.sem_inc(more_free, RING)
            pe.wait_ge(con_in, 16)

            def turn_tokens(l, n, src):
                pe.wait_ge(normed, l * 8 + (2 * n + 2))
                for g in range(4):
                    for kk in range(2):
                        for t in range(TT):
                            k = 2 * g + kk
                            at = kk * SEQ + t * P
                            last = nc.tensor.transpose(bank[NORM_BANKS[g]][:, at:at + P], src[:, t, k * P:(k + 1) * P], ident)
                    last.then_inc(turned, 1)
                pe.wait_ge(hT_act, l * 8 + (2 * n + 2))
                pe.wait_ge(hT_dve, l * 8 + (2 * n + 2))

            def features(dst, w, cols, src, kn):
                for k in range(kn):
                    last = nc.tensor.matmul(dst, w[:, k, cols], src[:, k, :], start=k == 0, stop=k == kn - 1)
                return last

            def tokens(dst, w, src, t, kn):
                for k in range(kn):
                    last = nc.tensor.matmul(dst, src[:, k, t * P:(t + 1) * P], w[:, k], start=k == 0, stop=k == kn - 1)
                return last

            def job(l, name):
                n = JOB_NAMES.index(name)
                turn, frees = JOBS[n][1:3]
                if n >= 2:
                    wait_copied(pe, l, JOB_NAMES[n - 2])
                if turn is not None:
                    wait_turn(pe, l, turn)
                b = bank[n % 2]
                kind, i = name[:-1], name[-1]
                if name in ("kx",) or kind in ("aq", "bq", "ak", "bk") or name in ("c0", "c1"):
                    w = slot_k(turn, 8, 256)
                    for c in range(2):
                        last = features(b[:, c * SEQ:(c + 1) * SEQ], w, slice(c * P, (c + 1) * P), hT, KD)
                elif name == "vx" or kind in ("av", "bv"):
                    w = slot_k(turn, 8, 256)
                    for t in range(TT):
                        last = tokens(b[:, t * 256:(t + 1) * 256], w, hT, t, KD)
                elif name == "c2":
                    w = slot_k(turn, 8, 160)
                    features(b[:, 0:SEQ], w, slice(0, P), hT, KD)
                    last = features(b[C_NOPE:C_DH, SEQ:2 * SEQ], w, slice(P, P + C_ROPE), hT, KD)
                elif name == "cs":
                    pe.wait_ge(c_squared, l + 1)
                    for k in range(3):
                        nc.tensor.matmul(b[:, 0:SEQ], ones, q0[:, k, :], start=k == 0, stop=k == 2)
                    for k in range(2):
                        last = nc.tensor.matmul(b[:, SEQ:2 * SEQ], ones, q0[:, 3 + k, :], start=k == 0, stop=k == 1)
                elif kind == "cq":
                    pe.wait_ge(c_scaled, l * 5 + 5)
                    w = slot_k(turn, 3, 384)
                    for j in range(2):
                        at = (2 * int(i) + j) % 4 * C_DH
                        last = features(b[0:C_DH, j * SEQ:(j + 1) * SEQ], w, slice(at, at + C_DH), cT, 3)
                elif kind == "ck" and name != "ckr":
                    w = slot_k(turn, 2, 1024)
                    for j in range(2):
                        at = (2 * int(i) + j) * (C_NOPE + C_DV)
                        last = features(b[0:C_NOPE, j * SEQ:(j + 1) * SEQ], w, slice(at, at + C_NOPE), cT[:, 3:5, :], 2)
                elif kind == "cv":
                    w = slot_k(turn, 2, 1024).rearrange("p k (h n) -> p k h n", h=C_HEADS)[:, :, :, C_NOPE:]
                    last = tokens(b[:, :].rearrange("p (h n) -> p h n", h=C_HEADS), w, cT[:, 3:5, :], int(i), 2)
                elif kind == "cr":
                    wait_copied(pe, l, "cq" + i)
                    last = nc.tensor.matmul(b[C_NOPE:C_DH, :], con[0:C_DH, C_SWAP:C_SWAP + C_ROPE],
                                            q0[0:C_DH, 2 * int(i):2 * int(i) + 2, :], start=True, stop=True)
                elif name == "ckr":
                    last = nc.tensor.matmul(b[C_NOPE:C_DH, 0:SEQ], con[0:C_DH, C_SWAP:C_SWAP + C_ROPE],
                                            kc[0:C_DH, 0, :], start=True, stop=True)
                elif kind == "as":
                    pe.wait_ge(a_squared, l + 1)
                    last = nc.tensor.matmul(b[:, :], ones, wide[:, 2 * int(i):2 * int(i) + 2, :], start=True, stop=True)
                last.then_inc(slot_free if frees else made, 1)

            def scores(l, i):
                u, b = divmod(i, 2)
                needed = {A0: ("ak0", "ak1"), B0: ("bk0", "bk1"), C0: ("cr0", "ck0"), C0 + 2: ("cr1", "ck0"),
                          C0 + 4: ("cr2", "ck2"), C0 + 6: ("cr3", "ck3")}
                for name in needed.get(i, ()):
                    wait_copied(pe, l, name)
                if i == C0:
                    pe.wait_ge(kr_spread, l + 1)
                if i == X0:
                    pe.wait_ge(qx_copied, l + 1)
                if i >= 2:
                    pe.wait_ge(exped, l * NI + (i - 1))
                dst = bank[2 + i % 2]
                qs = slice(b * P, (b + 1) * P)
                if C0 <= i < X0:
                    for j in range(2):
                        hd = 2 * (u - 8) + j
                        last = nc.tensor.matmul(dst[:, j * SEQ:(j + 1) * SEQ], q0[0:C_DH, hd, qs], kc[0:C_DH, hd, :],
                                                start=True, stop=True)
                else:
                    q, k, c = (q0, k0, u) if i < B0 else (q1, k1, u - 4) if i < C0 else (q1, kx, u - 12)
                    last = nc.tensor.matmul(dst[:, :], q[:, c, qs], k[:, c, :], start=True, stop=True)
                last.then_inc(scored, 1)

            def turn_probs(l, i):
                pe.wait_ge(weighed, l * NI + (i + 1))
                if i >= 2:
                    pe.wait_ge(probsT_copied, l * NI + (i - 1))
                for j in range(1 if i < B0 else 2):
                    for c in range(TT):
                        at = (2 * j + c) * P
                        last = nc.tensor.transpose(bank[4 + i % 2][:, at:at + P], prob[:, i % NPB, j, c * P:(c + 1) * P], ident)
                last.then_inc(probs_turned, 1)

            def products(l, i):
                u, b = divmod(i, 2)
                pe.wait_ge(probsT_copied, l * NI + (i + 1))
                if i == A0:
                    wait_copied(pe, l, "av0")
                    wait_copied(pe, l, "av1")
                if i == B0:
                    wait_copied(pe, l, "bv0")
                    wait_copied(pe, l, "bv1")
                if i == C0:
                    wait_copied(pe, l, "cv1")
                if b == 0 and u >= 2:
                    pe.wait_ge(out_copied, l * (NI // 2) + (u - 1))
                dst = bank[6 + u % 2]
                qs = slice(b * P, (b + 1) * P)
                if i < B0:
                    for c in range(TT):
                        last = nc.tensor.matmul(dst[:, qs], v0[:, c, u * P:(u + 1) * P], probT[:, i % 2, 0, c, :],
                                                start=c == 0, stop=c == TT - 1)
                else:
                    v, hd = (v1, 2 * (u - 4)) if i < C0 else (v0, 2 * (u - 8)) if i < X0 else (vx, 2 * (u - 12))
                    for c in range(TT):
                        for j in range(2):
                            last = nc.tensor.matmul(dst[64 * j:64 * j + 64, qs], v[:, c, (hd + j) * 64:(hd + j + 1) * 64],
                                                    probT[:, i % 2, j, c, :], start=c == 0, stop=c == TT - 1)
                last.then_inc(pv_done, 1)

            def gather(S, k):
                pe.wait_ge(S["sel_made"], k)
                for c in range(KD):
                    for t in range(TT):
                        last = nc.tensor.matmul(bank[c // 4][:, c % 4 * P:(c % 4 + 1) * P], h[:, t, c * P:(c + 1) * P],
                                                sel[:, t, :], start=t == 0, stop=t == TT - 1)
                last.then_inc(S["gathered"], 1)

            def experts_round(S, wait, free, rd, xts, look):
                pe.wait_ge(S["xt_act"], xts)
                pe.wait_ge(S["xt_dve"], xts)
                pe.wait_ge(S["added"], rd * 4 + 1)
                for m in range(2):
                    for k in range(KD):
                        j = m * KD + k
                        wait(j)
                        w = slot_k(j, QUAD, 512)
                        for e in range(QUAD):
                            last = nc.tensor.matmul(bank[2 + m][e * CAP:(e + 1) * CAP, :], xt[:, k, e * CAP:(e + 1) * CAP],
                                                    w[:, e, :], start=k == 0, stop=k == KD - 1)
                        last.then_inc(free, 1)
                if look is not None:
                    gather(S, look)
                pe.wait_ge(S["selw_made"], rd + 1)
                for t in range(TT):
                    last = nc.tensor.transpose(bank[5][:, t * P:(t + 1) * P], selw[:, t, :], ident)
                last.then_inc(S["selw_turned"], 1)
                pe.wait_ge(S["hidden_made"], rd + 1)
                for k in range(4):
                    last = nc.tensor.transpose(bank[4][:, k * P:(k + 1) * P], hidden[:, k * P:(k + 1) * P], ident)
                last.then_inc(S["hidden_turned"], 1)
                pe.wait_ge(S["hiddenT_copied"], rd + 1)
                for half in range(2):
                    for k in range(4):
                        j = 2 * KD + 4 * half + k
                        wait(j)
                        w = slot_k(j, QUAD, 512)
                        for e in range(QUAD):
                            last = nc.tensor.matmul(bank[6 + half][e * CAP:(e + 1) * CAP, :],
                                                    hiddenT[:, k, e * CAP:(e + 1) * CAP], w[:, e, :],
                                                    start=k == 0, stop=k == 3)
                        last.then_inc(free, 1)
                pe.wait_ge(S["selwT_copied"], rd + 1)
                for c in range(4):
                    t, half = divmod(c, 2)
                    pe.wait_ge(S["y_act"] if half == 0 else S["y_dve"], rd + 1)
                    if c >= 2:
                        pe.wait_ge(S["added"], rd * 4 + c)
                    nc.tensor.matmul(bank[(5, 2)[c % 2]][:, :], selwT[:, t * P:(t + 1) * P],
                                     yexp[:, half * 512:half * 512 + 512], start=True, stop=True)\
                      .then_inc(S["combined"], 1)

            with pe.Fori(0, DEPTH) as l:
                turn_tokens(l, 0, memx)
                job(l, "kx")
                job(l, "vx")
                turn_tokens(l, 1, h)
                for name in JOB_NAMES[2:8]:
                    job(l, name)
                for i in range(X0 + LAG_PV):
                    if i < X0:
                        scores(l, i)
                    for name in FILL.get(i, []):
                        job(l, name)
                    if LAG_T <= i < X0 + LAG_T:
                        turn_probs(l, i - LAG_T)
                    if i >= LAG_PV:
                        products(l, i - LAG_PV)
                pe.wait_ge(out_copied, l * (NI // 2) + 12)
                pe.wait_ge(a_normed, l + 1)
                wait_copied(pe, l, "as1")
                srcs = (oa, oBC[:, 0:4, :], oBC[:, 4:8, :])
                for pair in range(4):
                    for m in range(2 * N_BRANCHES):
                        g = 6 * pair + m
                        if g >= 8:
                            op, om = divmod(g - 8, 6)
                            if om < 3:
                                pe.wait_ge(gate_exp, l * 12 + (3 * op + om + 1))
                            else:
                                pe.wait_ge(mixed, l * 12 + (3 * op + om - 3 + 1))
                        b = bank[g % 8]
                        n = m % 3
                        if m < 3:
                            turn = T_GATE + 5 * pair + n
                            wait_turn(pe, l, turn)
                            for c in range(2):
                                last = features(b[:, c * SEQ:(c + 1) * SEQ], slot_k(turn, 8, 256),
                                                slice(c * P, (c + 1) * P), hT, KD)
                            last.then_inc(slot_free, 1)
                        else:
                            turn = T_GATE + 5 * pair + (3 if n < 2 else 4)
                            wait_turn(pe, l, turn)
                            w = slot_k(turn, 8, 256)[:, 4 * n:4 * n + 4] if n < 2 else slot_k(turn, 4, 256)
                            for c in range(2):
                                last = features(b[:, c * SEQ:(c + 1) * SEQ], w, slice(c * P, (c + 1) * P), srcs[n], 4)
                            last.then_inc(branch0 if n == 0 else slot_free, 1)
                pe.wait_ge(mix_sum, l * 4 + 5)
                for half in range(2):
                    for kg in range(2):
                        turn = T_OUT + 2 * half + kg
                        wait_turn(pe, l, turn)
                        w = slot_k(turn, 4, 512)
                        for t in range(TT):
                            for k in range(4):
                                last = nc.tensor.matmul(bank[2 * half + t][:, :], q0[:, 4 * kg + k, t * P:(t + 1) * P],
                                                        w[:, k, :], start=kg == 0 and k == 0, stop=kg == 1 and k == 3)
                            if t == 1:
                                last.then_inc(slot_free, 1)
                            elif kg == 1:
                                last.then_inc(projected, 1)
                turn_tokens(l, 2, h)
                wait_turn(pe, l, T_XQ)
                for c in range(2):
                    last = features(bank[0][:, c * SEQ:(c + 1) * SEQ], slot_k(T_XQ, 8, 256), slice(c * P, (c + 1) * P), hT, KD)
                last.then_inc(slot_free, 1)
                for i in range(X0, NI + LAG_PV):
                    if i < NI:
                        scores(l, i)
                    if X0 + LAG_T <= i < NI + LAG_T:
                        turn_probs(l, i - LAG_T)
                    if i >= X0 + LAG_PV:
                        products(l, i - LAG_PV)
                pe.wait_ge(out_copied, l * (NI // 2) + 14)
                wait_turn(pe, l, T_XO)
                w = slot_k(T_XO, 2, 1024)
                for o in range(4):
                    t, half = divmod(o, 2)
                    for k in range(2):
                        last = nc.tensor.matmul(bank[o][:, :], oa[:, k, t * P:(t + 1) * P],
                                                w[:, k, half * 512:half * 512 + 512], start=k == 0, stop=k == 1)
                    if o < 3:
                        last.then_inc(projected, 1)
                    else:
                        last.then_inc(slot_free, 1 + EMPTY)
                turn_tokens(l, 3, h)
                pe.wait_ge(router_in, l * 64 + 64)
                for t in range(TT):
                    for k in range(KD):
                        last = nc.tensor.matmul(bank[0][:, t * 64:t * 64 + 36], hT[:, k, t * P:(t + 1) * P], router_w[:, k, :],
                                                start=k == 0, stop=k == KD - 1)
                last.then_inc(logits_made, 1)
                pe.wait_ge(chosen_s, l * 2 + 2)
                b = bank[1]
                nc.tensor.matmul(b[:, 0:32], before, chosen[:, 0, :], start=True, stop=True)
                nc.tensor.matmul(b[:, 32:64], ones, chosen[:, 0, :], start=True, stop=False)
                nc.tensor.matmul(b[:, 32:64], before, chosen[:, 1, :], start=False, stop=True)
                nc.tensor.matmul(b[:, 64:96], ones, chosen[:, 0, :], start=True, stop=False)
                nc.tensor.matmul(b[:, 64:96], ones, chosen[:, 1, :], start=False, stop=True).then_inc(ranked, 1)
                S = main_r
                gather(S, l * (QUADS + 1) + 1)
                with pe.Fori(0, QUADS) as q:
                    def wait_main(j):
                        s = j % RING
                        pe.wait_ge(landed[s], l * (16 * real_turns(s, PER_LAYER)) + q * (16 * PER_QUAD // RING)
                                   + 16 * real_turns(s, Q_BASE + j + 1))
                    experts_round(S, wait_main, slot_free, l * QUADS + q, l * (QUADS + 1) + q + 1,
                                  l * (QUADS + 1) + q + 2)
                pe.wait_ge(placed, l + 1)
                plain(pe)
                over = pe.value_load(flag[0:1, 0:1], min_val=0, max_val=1)
                with pe.If(over > 0):
                    with pe.Fori(0, PASSES - 1) as p:
                        with pe.Fori(0, QUADS) as q:
                            rd = pe.snap(more) + p * QUADS + q

                            def wait_more(j):
                                pe.wait_ge(more_landed[j % RING], rd * (16 * PER_QUAD // RING) + 16 * (j // RING + 1))
                            pe.wait_ge(main_r["xt_act"], l * (QUADS + 1) + QUADS + 1)
                            pe.wait_ge(main_r["xt_dve"], l * (QUADS + 1) + QUADS + 1)
                            gather(more_r, rd + 1)
                            experts_round(more_r, wait_more, more_free, rd, rd + 1, None)
                    pe.reg_add(more, more, (PASSES - 1) * QUADS)
                pe.wait_ge(layer_done, l + 2)


_INS = ["x", "mem", "positions", "mix_norm_g", "w_in", "diff_lambda", "diff_subln_g", "mla_q_norm_g", "w_uq",
        "mla_kv_norm_g", "w_ukv", "w_branch", "w_out", "cross_norm_g", "mem_norm_g", "w_xq", "w_xkv", "w_xo",
        "ffn_norm_g", "w_group", "b_group", "w_router", "b_router", "w1", "w3", "w2", "final_norm_g"]


def kernel(**inputs):
    import numpy as np
    import concourse.bacc as bacc
    from concourse.bass_utils import run_bass_kernel_spmd

    nc = bacc.Bacc("TRN2", target_bir_lowering=False, num_devices=1)
    arrays, args = {}, []
    for name in _INS:
        a = np.ascontiguousarray(inputs[name])
        arrays[f"in_{name}_dram"] = a
        args.append(nc.dram_tensor(f"in_{name}_dram", a.shape, mybir.dt.from_np(a.dtype), kind="ExternalInput").ap())
    c = shape_constants()
    arrays["consts_dram"] = c
    args.append(nc.dram_tensor("consts_dram", c.shape, F32, kind="ExternalInput").ap())
    args.append(nc.dram_tensor("out_dram", (1, SEQ, D), F32, kind="ExternalOutput").ap())
    bass_hybrid_encoder(nc, *args)
    r = run_bass_kernel_spmd(nc, [arrays], core_ids=[0])
    return r.results[0]["out_dram"]
```

```python
import math
from contextlib import ExitStack

import concourse.bass as bass
from concourse import mybir

F32 = mybir.dt.float32
I32 = mybir.dt.int32
U32 = mybir.dt.uint32
ALU = mybir.AluOpType
ACT = mybir.ActivationFunctionType
AX_X = mybir.AxisListType.X

P = 128
DEPTH, D, SEQ = 2, 1024, 256
KD = D // P
TT = SEQ // P
A_HEADS, A_DH, A_DV = 4, 64, 128
B_HEADS, B_DH = 8, 64
B_PATTERNS = ((128, 1), (512, 4), (2048, 16))
C_HEADS, C_NOPE, C_ROPE, C_DV = 8, 64, 32, 64
C_Q_RANK, C_KV_RANK = 384, 256
C_DH = C_NOPE + C_ROPE
ROPE_THETA = 10000.0
X_HEADS, X_DH = 4, 64
N_BRANCHES, WIDTH = 3, 512
N_GROUPS, PER_GROUP, N_EXPERTS, D_EXPERT = 4, 8, 32, 512
EPS = 1e-6
TWO_PI = (6.28125, 0.0019350051879882812, 3.0199159795e-07)
NORM_BANKS = (3, 4, 6, 7)
SETUP_ANGLES = 24
SETUP_ZEROS = 3
ROUTE_STEPS = 37
ROOT_STEPS = 10
ROOT_START = 0x5F3759DF
FAR = -1e30

RING = 12
SLOT = 2048
CAP = 32
QUAD = 4
QUADS = N_EXPERTS // QUAD
PASSES = SEQ // CAP
NPB = 3

OFF_AQ, OFF_AK, OFF_AV = 0, 512, 1024
OFF_BQ, OFF_BK, OFF_BV = 1536, 2048, 2560
OFF_CQ, OFF_CKR, OFF_GATE = 3072, 3712, 3744

C_ID, C_BEFORE, C_ONES, C_SWAP, C_IOTA, C_GID, C_INV, C_LAM = 0, 128, 256, 384, 416, 448, 480, 481
C_STRIP = 488
STRIP = SEQ + P
N_CONST = C_STRIP + B_HEADS * STRIP


def slopes(n):
    return [2.0 ** (-8.0 * i / n) for i in range(1, n + 1)]


def lam_init(layer):
    return 0.8 - 0.6 * math.exp(-0.3 * layer)


def shape_constants():
    import numpy as np
    c = np.zeros((P, N_CONST), np.float32)
    r = np.arange(P)
    c[:, C_ID:C_ID + P] = r[:, None] == r[None, :]
    c[:, C_BEFORE:C_BEFORE + P] = r[:, None] < r[None, :]
    c[:, C_ONES:C_ONES + P] = 1.0
    half = C_ROPE // 2
    for i in range(half):
        c[C_NOPE + half + i, C_SWAP + i] = -1.0
        c[C_NOPE + i, C_SWAP + half + i] = 1.0
    c[:, C_IOTA:C_IOTA + CAP] = np.arange(CAP)
    c[:, C_GID:C_GID + N_EXPERTS] = np.arange(N_EXPERTS) // PER_GROUP
    inv = np.float32(ROPE_THETA) ** (-np.arange(0, C_ROPE, 2, dtype=np.float32) / np.float32(C_ROPE))
    c[C_NOPE:C_DH, C_INV] = np.concatenate([inv, inv])
    for layer in range(DEPTH):
        c[:, C_LAM + layer] = lam_init(layer)
        c[:, C_LAM + DEPTH + layer] = 1.0 - lam_init(layer)
    dist = np.abs(np.arange(STRIP)[None, :] - P - r[:, None])
    times = sum((dist % dil == 0) & (dist <= win // (2 * dil) * dil) for win, dil in B_PATTERNS)
    many = np.where(times > 0, np.log(np.maximum(times, 1)), FAR)
    for h, s in enumerate(slopes(B_HEADS)):
        c[:, C_STRIP + h * STRIP:C_STRIP + (h + 1) * STRIP] = many - s * dist
    return c


TURNS = [("in", c) for c in range(0, 3584, 256)] + [("in_last", 3584)]
TURNS += [("uq", 0), ("uq", 384), ("ukv", 0)]
T_GATE = len(TURNS)
for _pair in range(4):
    TURNS += [("in", OFF_GATE + _n * D + _pair * 256) for _n in range(N_BRANCHES)]
    TURNS += [("branch01", _pair), ("branch2", _pair)]
T_OUT = len(TURNS)
TURNS += [("out", (_half, _kg)) for _half in range(2) for _kg in range(2)]
T_XQ, T_XO = len(TURNS), len(TURNS) + 1
TURNS += [("xq", 0), ("xo", 0)]
N_MIX = len(TURNS)
EMPTY = -N_MIX % RING
Q_BASE = N_MIX + EMPTY
PER_QUAD = 2 * KD + 2 * (D_EXPERT // P)
PER_LAYER = Q_BASE + QUADS * PER_QUAD
assert PER_QUAD % RING == 0

JOBS = [(n, i, 1, e) for i, (n, e) in enumerate(
    [("aq0", "act"), ("aq1", "dve"), ("ak0", "act"), ("ak1", "dve"), ("av0", "act"), ("av1", "dve"),
     ("bq0", "act"), ("bq1", "dve"), ("bk0", "act"), ("bk1", "dve"), ("bv0", "act"), ("bv1", "dve"),
     ("c0", "dve"), ("c1", "dve"), ("c2", "dve")])]
JOBS += [("cs", None, 0, "act"), ("cq0", 15, 0, "act"), ("cq1", 15, 1, "act"), ("cq2", 16, 0, "act"),
         ("cq3", 16, 1, "act"), ("ckr", None, 0, "dve"), ("cr0", None, 0, "dve"), ("ck0", 17, 0, "act"),
         ("ck1", 17, 0, "dve"), ("cr1", None, 0, "dve"), ("ck2", 17, 0, "act"), ("ck3", 17, 0, "act"),
         ("cr2", None, 0, "dve"), ("cv0", 17, 0, "act"), ("cr3", None, 0, "dve"), ("cv1", 17, 1, "act"),
         ("as0", None, 0, "act"), ("as1", None, 0, "act")]
JOB_NAMES = [j[0] for j in JOBS]
FILL = {0: ["bq0"], 1: ["bq1", "bk0"], 2: ["bk1"], 3: ["bv0"], 4: ["bv1"], 5: ["c0"], 6: ["c1"], 7: ["c2"],
        9: ["cs"], 11: ["cq0", "cq1"], 12: ["cq2", "cq3", "ckr"], 13: ["cr0", "ck0", "ck1"],
        14: ["cr1", "ck2"], 15: ["ck3", "cr2"], 16: ["cv0", "cr3"], 17: ["cv1"], 19: ["as0"], 20: ["as1"]}
assert JOB_NAMES[6:] == [n for i in sorted(FILL) for n in FILL[i]]
A0, B0, C0, X0, NI = 0, 8, 16, 24, 28
LAG_T, LAG_PV, LAG_OUT = 2, 3, 4


def count_before(kind, n):
    return sum(kind(j) for j in JOBS[:n + 1])


def bass_hybrid_encoder(nc, x_in, mem_in, pos_in, mix_norm_g, w_in, diff_lambda, diff_subln_g, mla_q_norm_g,
                        w_uq, mla_kv_norm_g, w_ukv, w_branch, w_out, cross_norm_g, mem_norm_g, w_xq, w_xkv,
                        w_xo, ffn_norm_g, w_group, b_group, w_router, b_router, w1, w3, w2, final_norm_g,
                        consts, out):
    ctx = ExitStack()
    with ctx:
        def sb(name, shape, dt=F32):
            return ctx.enter_context(nc.sbuf_tensor(name, shape, dt))

        def sem(name):
            return ctx.enter_context(nc.semaphore(name))

        ring = sb("ring", [P, RING, SLOT])
        con = sb("con", [P, N_CONST])
        x = sb("x", [P, TT, D])
        h = sb("h", [P, TT, D])
        hT = sb("hT", [P, KD, SEQ])
        gain = sb("gain", [P, D])
        q0 = sb("q0", [P, KD, SEQ])
        k0 = sb("k0", [P, 4, 2 * SEQ])
        v0 = sb("v0", [P, TT, 512])
        q1 = sb("q1", [P, 4, SEQ])
        k1 = sb("k1", [P, 4, 2 * SEQ])
        v1 = sb("v1", [P, TT, 512])
        kx = sb("kx", [P, 2, 2 * SEQ])
        vx = sb("vx", [P, TT, 256])
        prob = sb("prob", [P, NPB, 2, SEQ])
        probT = sb("probT", [P, 2, 2, TT, P])
        oa = sb("oa", [P, 4, SEQ])
        cT = sb("cT", [P, 5, SEQ])
        wide = sb("wide", [P, 4, SEQ])
        dist = sb("dist", [P, TT, SEQ])
        ropes = sb("ropes", [P, 2, SEQ])
        small = sb("small", [P, 64])
        gpad = sb("gpad", [P, TT, 8])
        topi = sb("topi", [P, TT, 2, 8], U32)
        flag = sb("flag", [P, 1], I32)
        gcol = sb("gcol", [P, DEPTH, 6])
        lamt = sb("lamt", [P, DEPTH])
        stat = sb("stat", [P, 16])
        root = sb("root", [P, 2 * TT, 5])
        mx = sb("mx", [P, NPB, 2])
        sm = sb("sm", [P, NPB, 2])
        rs = sb("rs", [P, NPB, 4])
        bank = [ctx.enter_context(nc.psum_tensor(f"bank{i}", [P, 512], F32)) for i in range(8)]

        ident = con[:, C_ID:C_ID + P]
        ones = con[:, C_ONES:C_ONES + P]
        before = con[:, C_BEFORE:C_BEFORE + P]
        iota = con[:, C_IOTA:C_IOTA + CAP]
        oBC = h[:, :, :].rearrange("p t (c n) -> p (t c) n", n=SEQ)
        kc = k0[:, :, :].rearrange("p a (b n) -> p (a b) n", n=SEQ)
        posf = q1[:, 0:2, :].rearrange("p c n -> p (c n)")[:, 0:TT + SEQ]
        posi = v1[:, :, :].bitcast(I32).rearrange("p t n -> p (t n)")[:, 0:TT + SEQ]
        angles = prob[:, 0, :, :]
        lam_all = v0[:, 1, :]
        spare = oa[:, :, :].rearrange("p c n -> p (c n)")
        NR = N_GROUPS + N_EXPERTS
        logit = spare[:, 0:72].rearrange("p (t n) -> p t n", t=TT)
        rt = spare[:, 72:328].rearrange("p (t a n) -> p t a n", t=TT, a=4)
        top = spare[:, 328:392].rearrange("p (t a n) -> p t a n", t=TT, a=4)
        chosen = spare[:, 392:456].rearrange("p (t n) -> p t n", t=TT)
        place = spare[:, 456:528].rearrange("p (t n) -> p t n", t=TT)
        weight = spare[:, 528:600].rearrange("p (t n) -> p t n", t=TT)
        router_w = wide[:, :, :].rearrange("p c n -> p (c n)")[:, 0:KD * NR].rearrange("p (k n) -> p k n", k=KD)
        router_b = wide[:, :, :].rearrange("p c n -> p (c n)")[:, KD * NR:KD * NR + NR]
        xt = v0[:, :, :].rearrange("p t (c n) -> p (t c) n", n=P)
        yexp = q1[:, :, :].rearrange("p c n -> p (c n)")
        sel = v1[:, 0, 0:256].rearrange("p (t n) -> p t n", t=TT)
        selw = v1[:, 0, 256:512].rearrange("p (t n) -> p t n", t=TT)
        selwT = v1[:, 1, 0:256]
        flat = [prob[:, i, :, :].rearrange("p a n -> p (a n)") for i in range(NPB)]
        act_e, act_r, hidden = flat
        hiddenT = probT[:, 0, :, :, :].rearrange("p a b n -> p (a b) n")
        wxk = k0[:, :, :].rearrange("p a n -> p (a n)").rearrange("p (k n) -> p k n", k=KD)
        wxv = k1[:, :, :].rearrange("p a n -> p (a n)").rearrange("p (k n) -> p k n", k=KD)
        mem_gain = wide[:, :, :].rearrange("p c n -> p (c n)")
        memx = q0[:, :, :].rearrange("p c n -> p (c n)").rearrange("p (t n) -> p t n", t=TT)
        memjunk = hT[:, :, :].rearrange("p c n -> p (c n)").rearrange("p (t n) -> p t n", t=TT)

        landed = [sem(f"landed{i}") for i in range(RING)]
        slot_free = sem("slot_free")
        con_in, x_in_s, pos_in_s, cols_in, lam_in = (sem(n) for n in ("con_in", "x_arrived", "pos_in", "cols_in", "lam_in"))
        strips_in, eps_set = sem("strips_in"), sem("eps_set")
        gain_in, gain_used = sem("gain_in"), sem("gain_used")
        router_in = sem("router_in")
        mem_tile_in = [sem(f"mem_tile{t}_in") for t in range(TT)]
        mem_gain_in, mem_w_in = sem("mem_gain_in"), sem("mem_w_in")
        mem_squared, mem_root_step, mem_normed, mem_turned = (sem("mem_squared"), sem("mem_root_step"),
                                                              sem("mem_normed"), sem("mem_turned"))
        memT_act, memT_dve, mem_made, kx_copied, vx_copied = (sem("memT_act"), sem("memT_dve"), sem("mem_made"),
                                                              sem("kx_copied"), sem("vx_copied"))
        setup_dve, setup_act, setup_pool, zeroed = sem("setup_dve"), sem("setup_act"), sem("setup_pool"), sem("zeroed")
        squared, root_step, normed, turned = sem("squared"), sem("root_step"), sem("normed"), sem("turned")
        hT_act, hT_dve = sem("hT_act"), sem("hT_dve")
        made = sem("made")
        copied = {"act": sem("copied_act"), "dve": sem("copied_dve")}
        layer_cols = sem("layer_cols")
        c_squared, c_rstd, c_scaled, rope_step, kr_spread = (sem("c_squared"), sem("c_rstd"), sem("c_scaled"),
                                                             sem("rope_step"), sem("kr_spread"))
        a_squared, a_rstd, a_normed = sem("a_squared"), sem("a_rstd"), sem("a_normed")
        scored, biased, maxed, exped = sem("scored"), sem("biased"), sem("maxed"), sem("exped")
        inverted, weighed = sem("inverted"), sem("weighed")
        a_scaled = sem("a_scaled")
        probs_turned, probsT_copied = sem("probs_turned"), sem("probsT_copied")
        pv_done, out_copied = sem("pv_done"), sem("out_copied")
        gate_exp, branch0, gate_step, mixed, mix_sum = (sem("gate_exp"), sem("branch0"), sem("gate_step"),
                                                        sem("mixed"), sem("mix_sum"))
        projected, x_added = sem("projected"), sem("x_added")
        qx_copied = sem("qx_copied")
        logits_made, route_step, route_ask, route_exp = (sem("logits_made"), sem("route_step"),
                                                         sem("route_ask"), sem("route_exp"))
        chosen_s, ranked, placed = sem("chosen_made"), sem("ranked"), sem("placed")
        shifted = sem("shifted")
        layer_done = sem("layer_done")
        stored, passed = sem("stored"), sem("passed")

        def round_sems(name):
            return {s: sem(f"{name}_{s}") for s in
                    ("sel_made", "selw_step", "selw_made", "gathered", "xt_act", "xt_dve", "e_made",
                     "silu_step", "hidden_made", "selw_turned", "hidden_turned", "selwT_copied",
                     "hiddenT_copied", "y_act", "y_dve", "combined", "added")}

        main_r, more_r = round_sems("main"), round_sems("more")
        more_landed = [sem(f"more_landed{i}") for i in range(RING)]
        more_free = sem("more_free")

        def real_turns(slot, upto):
            return sum(1 for j in range(upto) if j % RING == slot and not N_MIX <= j < Q_BASE)

        def wait_turn(eng, l, j):
            s = j % RING
            eng.wait_ge(landed[s], l * (16 * real_turns(s, PER_LAYER)) + 16 * real_turns(s, j + 1))

        def wait_free(eng, l, j):
            eng.wait_ge(slot_free, l * PER_LAYER + (RING + j + 1))

        N_MADE = sum(not j[2] for j in JOBS)
        N_COPIED = {e: sum(j[3] == e for j in JOBS) for e in ("act", "dve")}

        def wait_made(eng, l, name):
            n = JOB_NAMES.index(name)
            if JOBS[n][2]:
                wait_free(eng, l, JOBS[n][1])
            else:
                eng.wait_ge(made, l * N_MADE + count_before(lambda j: not j[2], n))

        def wait_copied(eng, l, name):
            n = JOB_NAMES.index(name)
            e = JOBS[n][3]
            eng.wait_ge(copied[e], l * N_COPIED[e] + count_before(lambda j: j[3] == e, n))

        def slot_k(j, k, n):
            return ring[:, j % RING, 0:k * n].rearrange("p (k n) -> p k n", k=k)

        def plain(eng):
            eng.sem_inc(passed, 1)

        HALVES = ((slice(0, 64), slice(SEQ, 2 * SEQ)), (slice(64, 128), slice(0, SEQ)))

        def one(l):
            return bass.ds(l, 1)

        def bank_n(g):
            return bank[NORM_BANKS[g]][:, :].rearrange("p (a n) -> p a n", a=2)

        block = ctx.enter_context(nc.Block())

        def mix_source(l, kind, a):
            def rows(w):
                return w.rearrange("(k p) n -> p k n", p=P)
            if kind == "in":
                return 8, 256, rows(w_in[l, :, a:a + 256])
            if kind == "in_last":
                return 8, 160, rows(w_in[l, :, a:a + 160])
            if kind == "xq":
                return 8, 256, rows(w_xq[l])
            if kind == "xo":
                return 2, 1024, rows(w_xo[l])
            if kind == "uq":
                return 3, 384, rows(w_uq[l, :, a:a + 384])
            if kind == "ukv":
                return 2, 1024, rows(w_ukv[l])
            if kind in ("branch01", "branch2"):
                src = rows(w_branch[l].rearrange("n c d -> (n c) d"))
                lo, n = (0, 8) if kind == "branch01" else (8, 4)
                return n, 256, src[:, lo:lo + n, a * 256:a * 256 + 256]
            half, kg = a
            return 4, 512, rows(w_out[l])[:, 4 * kg:4 * kg + 4, half * 512:half * 512 + 512]

        def quad_source(l, q, j):
            es = bass.ds(q * QUAD, QUAD)
            if j < 2 * KD:
                w, k = (w1 if j < KD else w3), j % KD
                return w[l][es, k * P:(k + 1) * P, :].rearrange("e p n -> p e n")
            half, k = divmod(j - 2 * KD, 4)
            return w2[l][es, k * P:(k + 1) * P, half * 512:half * 512 + 512].rearrange("e p n -> p e n")

        @block.sync
        def _(sp):
            more = sp.alloc_register("sp_more_rounds")
            sp.reg_mov(more, 0)
            sp.dma_start(posi[:, TT:TT + SEQ], pos_in[0:1, :].broadcast_to([P, SEQ])).then_inc(pos_in_s, 16)
            for t in range(TT):
                sp.dma_start(posi[:, t:t + 1], pos_in[0, t * P:(t + 1) * P].rearrange("(p a) -> p a", a=1))\
                  .then_inc(pos_in_s, 16)
            sp.dma_start(con[:, 0:C_STRIP], consts[:, 0:C_STRIP]).then_inc(con_in, 16)
            sp.dma_start(lam_all, diff_lambda.rearrange("l a d -> (l a d)").rearrange("(a n) -> a n", a=1)
                         .broadcast_to([P, DEPTH * 4 * A_DH])).then_inc(lam_in, 16)
            sp.dma_start(con[:, C_STRIP:], consts[:, C_STRIP:]).then_inc(strips_in, 16)
            with sp.Fori(0, DEPTH) as l:
                for j, (kind, a) in enumerate(TURNS):
                    k, n, src = mix_source(l, kind, a)
                    sp.wait_ge(slot_free, l * PER_LAYER + (j + 1))
                    sp.dma_start(slot_k(j, k, n), src).then_inc(landed[j % RING], 16)
                with sp.Fori(0, QUADS) as q:
                    for j in range(PER_QUAD):
                        sp.wait_ge(slot_free, l * PER_LAYER + q * PER_QUAD + (Q_BASE + j + 1))
                        sp.dma_start(slot_k(j, QUAD, 512), quad_source(l, q, j)).then_inc(landed[j % RING], 16)
                sp.wait_ge(placed, l + 1)
                plain(sp)
                over = sp.value_load(flag[0:1, 0:1], min_val=0, max_val=1)
                with sp.If(over > 0):
                    sp.wait_ge(slot_free, l * PER_LAYER + (PER_LAYER + RING))
                    plain(sp)
                    with sp.Fori(0, PASSES - 1) as p:
                        with sp.Fori(0, QUADS) as q:
                            rd = sp.snap(more) + p * QUADS + q
                            for j in range(PER_QUAD):
                                sp.wait_ge(more_free, rd * PER_QUAD + (j + 1))
                                sp.dma_start(slot_k(j, QUAD, 512), quad_source(l, q, j))\
                                  .then_inc(more_landed[j % RING], 16)
                    sp.reg_add(more, more, (PASSES - 1) * QUADS)
                    sp.wait_ge(more_free, sp.snap(more) * PER_QUAD + RING)
                    plain(sp)
            for t in range(TT):
                sp.wait_ge(normed, 6 * DEPTH + t + 1)
                sp.dma_start(out[0, t * P:(t + 1) * P, :], h[:, t, :]).then_inc(stored, 16)
            sp.wait_ge(stored, 16 * TT)

        @block.gpsimd
        def _(pool):
            nc.gpsimd.memset(stat[:, 8:9], EPS).then_inc(eps_set, 1)

            def load_mem(l):
                nc.gpsimd.dma_start(mem_gain, mem_norm_g[one(l), :].broadcast_to([P, D])).then_inc(mem_gain_in, 16)
                nc.gpsimd.dma_start(wxk, w_xkv[l, :, 0:256].rearrange("(k p) n -> p k n", p=P)).then_inc(mem_w_in, 16)
                nc.gpsimd.dma_start(wxv, w_xkv[l, :, 256:512].rearrange("(k p) n -> p k n", p=P)).then_inc(mem_w_in, 16)

            def zero_keys(l):
                pool.wait_ge(mem_made, l * 2 + 2)
                plain(pool)
                for i, (kk, rows, cols) in enumerate([(kk, rows, cols) for kk in (k0, k1) for rows, cols in HALVES]):
                    if i:
                        pool.wait_ge(zeroed, l * 4 + i)
                        plain(pool)
                    nc.gpsimd.memset(kk[rows, :, cols], 0.0).then_inc(zeroed, 1)

            load_mem(0)
            nc.gpsimd.dma_start(gain[:, :], mix_norm_g[0:1, :].broadcast_to([P, D])).then_inc(gain_in, 16)
            done = 0
            for tile, value in [(kx[rows, :, cols], 0.0) for rows, cols in HALVES] + [(gpad[:, :, :], FAR)]:
                nc.gpsimd.memset(tile, value).then_inc(setup_pool, 1)
                done += 1
                pool.wait_ge(setup_pool, done)
            assert done == SETUP_ZEROS
            for first, src in ((0, mla_q_norm_g), (3, mla_kv_norm_g), (5, diff_subln_g)):
                for l in range(DEPTH):
                    n = src.shape[1] // P
                    nc.gpsimd.dma_start(gcol[:, l, first:first + n], src[l].rearrange("(c p) -> p c", p=P),
                                        allow_slow_non_contiguous=True)\
                      .then_inc(cols_in, 16)
            zero_keys(0)

            def load_gain(g, l, turn):
                pool.wait_ge(gain_used, l * 3 + (turn + 1))
                plain(pool)
                nc.gpsimd.dma_start(gain[:, :], g.broadcast_to([P, D])).then_inc(gain_in, 16)

            with pool.Fori(0, DEPTH) as l:
                row = one(l)
                load_gain(cross_norm_g[row, :], l, 1)
                pool.wait_ge(a_normed, l + 1)
                plain(pool)
                nc.gpsimd.dma_start(router_w[:, :, 0:N_GROUPS], w_group[l].rearrange("(k p) n -> p k n", p=P))\
                  .then_inc(router_in, 16)
                nc.gpsimd.dma_start(router_w[:, :, N_GROUPS:], w_router[l].rearrange("(k p) n -> p k n", p=P))\
                  .then_inc(router_in, 16)
                nc.gpsimd.dma_start(router_b[:, 0:N_GROUPS], b_group[row, :].broadcast_to([P, N_GROUPS]))\
                  .then_inc(router_in, 16)
                nc.gpsimd.dma_start(router_b[:, N_GROUPS:], b_router[row, :].broadcast_to([P, N_EXPERTS]))\
                  .then_inc(router_in, 16)
                load_gain(ffn_norm_g[row, :], l, 2)
                with pool.If(l < DEPTH - 1):
                    following = nc.s_assert_within(pool.snap(l) + 1, 1, DEPTH - 1, skip_runtime_bounds_check_because=
                                                   "the branch is taken below the last layer only")
                    load_gain(mix_norm_g[one(following), :], following, 0)
                    pool.wait_ge(chosen_s, l * 2 + 2)
                    plain(pool)
                    load_mem(following)
                    zero_keys(following)
            load_gain(final_norm_g.rearrange("(a n) -> a n", a=1), DEPTH, 0)

        @block.scalar
        def _(act):
            more = act.alloc_register("act_more_rounds")
            act.reg_mov(more, 0)

            def norm(l, n, src, junk):
                if n == 0:
                    act.wait_ge(x_in_s, 16)
                    act.wait_ge(layer_done, l + 1)
                if n == 1:
                    act.wait_ge(x_added, l * 8 + 4)
                if n == 2:
                    act.wait_ge(x_added, l * 8 + 8)
                for t in range(TT):
                    nc.scalar.activation(junk[:, t, :], src[:, t, :], ACT.Square,
                                         accum_out=stat[:, t:t + 1]).then_inc(squared, 1)

            def copy_hT(l, n):
                for g in (0, 2):
                    act.wait_ge(turned, l * 12 + (4 * n + g + 1))
                    nc.scalar.activation(hT[:, 2 * g:2 * g + 2, :], bank_n(g), ACT.Copy).then_inc(hT_act, 1)

            def mem_stage(l):
                for t in range(TT):
                    act.wait_ge(mem_tile_in[t], l * 16 + 16)
                    nc.scalar.activation(memjunk[:, t, :], memx[:, t, :], ACT.Square,
                                         accum_out=stat[:, 9 + t:10 + t]).then_inc(mem_squared, 1)
                for g in (0, 2):
                    act.wait_ge(mem_turned, l * 4 + (g + 1))
                    nc.scalar.activation(hT[:, 2 * g:2 * g + 2, :], bank_n(g), ACT.Copy).then_inc(memT_act, 1)
                act.wait_ge(mem_made, l * 2 + 1)
                b2 = bank[0][:, :].rearrange("p (a n) -> p a n", a=2)
                nc.scalar.activation(kx[0:64, :, 0:SEQ], b2[0:64], ACT.Copy)
                nc.scalar.activation(kx[64:128, :, SEQ:2 * SEQ], b2[64:128], ACT.Copy).then_inc(kx_copied, 1)

            def job(l, name):
                n = JOB_NAMES.index(name)
                wait_made(act, l, name)
                b = bank[n % 2][:, :]
                b2 = b.rearrange("p (a n) -> p a n", a=2)
                kind, i = name[:-1], name[-1]
                if kind in ("aq", "bq"):
                    dst = q0 if kind == "aq" else q1
                    last = nc.scalar.activation(dst[:, 2 * int(i):2 * int(i) + 2, :], b2, ACT.Copy, scale=A_DH ** -0.5)
                elif kind in ("ak", "bk"):
                    dst, c = (k0 if kind == "ak" else k1), 2 * int(i)
                    act.wait_ge(zeroed, l * 4 + 4)
                    nc.scalar.activation(dst[0:64, c:c + 2, 0:SEQ], b2[0:64], ACT.Copy)
                    last = nc.scalar.activation(dst[64:128, c:c + 2, SEQ:2 * SEQ], b2[64:128], ACT.Copy)
                elif kind in ("av", "bv"):
                    dst, c = (v0 if kind == "av" else v1), 256 * int(i)
                    last = nc.scalar.activation(dst[:, :, c:c + 256], b2, ACT.Copy)
                elif name == "cs":
                    nc.scalar.activation(wide[:, 0, :], b2[:, 0], ACT.Ln, scale=1.0 / C_Q_RANK, bias=stat[:, 8:9])
                    last = nc.scalar.activation(wide[:, 1, :], b2[:, 1], ACT.Ln, scale=1.0 / C_KV_RANK,
                                                bias=stat[:, 8:9])
                    last.then_inc(copied["act"], 1)
                    wait_copied(act, l, "cs")
                    nc.scalar.activation(wide[:, 2:4, :], wide[:, 0:2, :], ACT.Exp, scale=-0.5).then_inc(c_rstd, 1)
                    return
                elif kind == "cq":
                    c = 2 * int(i)
                    last = nc.scalar.activation(q0[0:C_DH, c:c + 2, :], b2[0:C_DH], ACT.Copy, scale=C_DH ** -0.5)
                elif kind == "ck" and name != "ckr":
                    c = 2 * int(i)
                    last = nc.scalar.activation(kc[0:C_NOPE, c:c + 2, :], b2[0:C_NOPE], ACT.Copy)
                elif kind == "cv":
                    last = nc.scalar.activation(v0[:, int(i), :], b, ACT.Copy)
                elif kind == "as":
                    c = 2 * int(i)
                    last = nc.scalar.activation(wide[:, c:c + 2, :], b2, ACT.Ln, scale=1.0 / A_DV, bias=stat[:, 8:9])
                last.then_inc(copied["act"], 1)

            def experts_round(S, wait_w1, wait_w2a, rd, look):
                def copy_xt(k):
                    act.wait_ge(S["gathered"], k)
                    nc.scalar.activation(xt[:, 0:4, :], bank[0][:, :].rearrange("p (c n) -> p c n", c=4), ACT.Copy)\
                      .then_inc(S["xt_act"], 1)
                if look is None:
                    copy_xt(rd + 1)
                wait_w1(act)
                nc.scalar.activation(act_e, bank[2][:, :], ACT.Exp, scale=-1.0).then_inc(S["e_made"], 1)
                if look is not None:
                    copy_xt(look)
                act.wait_ge(S["selw_turned"], rd + 1)
                nc.scalar.activation(selwT, bank[5][:, 0:256], ACT.Copy).then_inc(S["selwT_copied"], 1)
                act.wait_ge(S["hidden_turned"], rd + 1)
                nc.scalar.activation(hiddenT, bank[4][:, :].rearrange("p (c n) -> p c n", c=4), ACT.Copy)\
                  .then_inc(S["hiddenT_copied"], 1)
                wait_w2a(act)
                nc.scalar.activation(yexp[:, 0:512], bank[6][:, :], ACT.Copy).then_inc(S["y_act"], 1)

            def load_mem():
                for t in range(TT):
                    act.dma_start(memx[:, t, :], mem_in[0, t * P:(t + 1) * P, :]).then_inc(mem_tile_in[t], 16)

            load_mem()
            act.dma_start(x[:, :, :], x_in[0].rearrange("(t p) n -> p t n", p=P)).then_inc(x_in_s, 16)
            act.wait_ge(eps_set, 1)
            act.wait_ge(setup_pool, SETUP_ZEROS)
            mem_stage(0)
            act.wait_ge(setup_dve, SETUP_ANGLES)
            nc.scalar.activation(ropes[64:96, 0, :], angles[64:96, 0, :], ACT.Sin)
            nc.scalar.activation(ropes[64:96, 1, :], angles[64:96, 1, :], ACT.Sin)
            nc.scalar.activation(small[:, 4:8], small[:, 0:4], ACT.Exp).then_inc(setup_act, 1)

            with act.Fori(0, DEPTH) as l:
                norm(l, 0, x, h)
                copy_hT(l, 0)
                for name in ("aq0", "ak0", "av0"):
                    job(l, name)

                def exps(i):
                    pb, m = i % NPB, mx[:, i % NPB, :]
                    act.wait_ge(maxed, l * NI + (i + 1))
                    plain = i >= C0
                    if i >= NPB:
                        act.wait_ge(probs_turned, l * NI + (i - NPB + 1))
                    for j in range(2):
                        src = bank[2 + i % 2][:, j * SEQ:(j + 1) * SEQ] if plain else prob[:, pb, j, :]
                        last = nc.scalar.activation(prob[:, pb, j, :], src, ACT.Exp, bias=m[:, j:j + 1],
                                                    accum_out=sm[:, pb, j:j + 1])
                    last.then_inc(exped, 1)

                def copy_probsT(i):
                    act.wait_ge(probs_turned, l * NI + (i + 1))
                    if i >= 2:
                        act.wait_ge(pv_done, l * NI + (i - 1))
                    n = 1 if i < B0 else 2
                    nc.scalar.activation(probT[:, i % 2, 0:n, :, :].rearrange("p a b n -> p (a b) n"),
                                         bank[4 + i % 2][:, 0:n * 256].rearrange("p (c n) -> p c n", n=P),
                                         ACT.Copy).then_inc(probsT_copied, 1)

                for i in range(X0 + LAG_OUT):
                    if i < X0:
                        exps(i)
                    if i == 8:
                        wait_copied(act, l, "c2")
                        act.wait_ge(scored, l * NI + B0)
                        nc.scalar.activation(q0[:, 0:5, :], cT[:, :, :], ACT.Square).then_inc(c_squared, 1)
                    if i == 18:
                        act.wait_ge(out_copied, l * (NI // 2) + 4)
                        act.wait_ge(c_scaled, l * 5 + 5)
                        nc.scalar.activation(wide[:, :, :], oa[:, :, :], ACT.Square).then_inc(a_squared, 1)
                    for name in FILL.get(i, []):
                        if JOBS[JOB_NAMES.index(name)][3] == "act":
                            if name == "cq0":
                                wait_copied(act, l, "cs")
                            if name == "cv0":
                                act.wait_ge(pv_done, l * NI + B0)
                            job(l, name)
                    if i == 20:
                        wait_copied(act, l, "as1")
                        nc.scalar.activation(wide[:, :, :], wide[:, :, :], ACT.Exp, scale=-0.5).then_inc(a_rstd, 1)
                    if LAG_T <= i < X0 + LAG_T:
                        copy_probsT(i - LAG_T)
                for pair in range(4):
                    for n in range(N_BRANCHES):
                        wait_free(act, l, T_GATE + 5 * pair + n)
                        act.wait_ge(mix_sum, l * 4 + (pair + 1))
                        nc.scalar.activation(flat[n], bank[(6 * pair + n) % 8][:, :], ACT.Exp, scale=-1.0)\
                          .then_inc(gate_exp, 1)
                norm(l, 1, x, h)
                copy_hT(l, 1)
                wait_free(act, l, T_XQ)
                nc.scalar.activation(q1[:, 0:2, :], bank[0][:, :].rearrange("p (a n) -> p a n", a=2), ACT.Copy,
                                     scale=X_DH ** -0.5).then_inc(qx_copied, 1)
                for i in range(X0, NI + LAG_T):
                    if i < NI:
                        exps(i)
                    if i >= X0 + LAG_T:
                        copy_probsT(i - LAG_T)
                norm(l, 2, x, h)
                copy_hT(l, 2)
                for t in range(TT):
                    act.wait_ge(route_ask, l * 2 + (t + 1))
                    nc.scalar.activation(small[:, 16 + 4 * t:20 + 4 * t], logit[:, t, 0:N_GROUPS], ACT.Exp,
                                         bias=small[:, 10 + 2 * t:11 + 2 * t], accum_out=small[:, 24 + 2 * t:25 + 2 * t])
                    nc.scalar.activation(small[:, 25 + 2 * t:26 + 2 * t], top[:, t, 2, 1:2], ACT.Exp,
                                         bias=small[:, 11 + 2 * t:12 + 2 * t]).then_inc(route_exp, 1)
                S = main_r
                act.wait_ge(S["gathered"], l * (QUADS + 1) + 1)
                nc.scalar.activation(xt[:, 0:4, :], bank[0][:, :].rearrange("p (c n) -> p c n", c=4), ACT.Copy)\
                  .then_inc(S["xt_act"], 1)

                with act.If(l < DEPTH - 1):
                    load_mem()

                def main_round(q):
                    base = l * PER_LAYER + q * PER_QUAD
                    experts_round(S, lambda e: e.wait_ge(slot_free, base + (Q_BASE + RING + KD)),
                                  lambda e: e.wait_ge(slot_free, base + (Q_BASE + RING + 2 * KD + 4)),
                                  l * QUADS + q, l * (QUADS + 1) + q + 2)

                with act.Fori(0, QUADS - 1) as q:
                    main_round(q)
                with act.If(l < DEPTH - 1):
                    mem_stage(act.snap(l) + 1)
                main_round(QUADS - 1)
                act.wait_ge(placed, l + 1)
                plain(act)
                over = act.value_load(flag[0:1, 0:1], min_val=0, max_val=1)
                with act.If(over > 0):
                    with act.Fori(0, PASSES - 1) as p:
                        with act.Fori(0, QUADS) as q:
                            rd = act.snap(more) + p * QUADS + q
                            experts_round(more_r, lambda e: e.wait_ge(more_free, rd * PER_QUAD + (RING + KD)),
                                          lambda e: e.wait_ge(more_free, rd * PER_QUAD + (RING + 2 * KD + 4)), rd, None)
                    act.reg_add(more, more, (PASSES - 1) * QUADS)
            norm(DEPTH, 0, x, h)

        @block.vector
        def _(dve):
            more = dve.alloc_register("dve_more_rounds")
            dve.reg_mov(more, 0)
            more_passes = dve.alloc_register("dve_more_passes")
            dve.reg_mov(more_passes, 0)
            steps = [0]

            def then(ins):
                steps[0] += 1
                ins.then_inc(setup_dve, 1)
                dve.wait_ge(setup_dve, steps[0])


            def rsqrt(row, totals, step, count):
                def at(t, c):
                    return root[:, row + t, c:c + 1]

                def bits(t, c):
                    return at(t, c).bitcast(I32)
                for t in range(TT):
                    nc.vector.tensor_scalar(at(t, 0), totals[:, t:t + 1], 1.0 / D, EPS, ALU.mult, ALU.add)\
                      .then_inc(step, 1)
                for t in range(TT):
                    nc.vector.tensor_scalar(at(t, 1), totals[:, t:t + 1], -0.5 / D, -0.5 * EPS, ALU.mult, ALU.add)\
                      .then_inc(step, 1)
                dve.wait_ge(step, count + TT)
                for t in range(TT):
                    nc.vector.tensor_scalar(bits(t, 2), bits(t, 0), 1, None, ALU.logical_shift_right).then_inc(step, 1)
                dve.wait_ge(step, count + 3 * TT)
                for t in range(TT):
                    nc.vector.tensor_scalar(bits(t, 3), bits(t, 2), -1, ROOT_START, ALU.mult, ALU.add).then_inc(step, 1)
                for i in range(3):
                    dve.wait_ge(step, count + (4 + 2 * i) * TT)
                    for t in range(TT):
                        nc.vector.scalar_tensor_tensor(at(t, 4), at(t, 3), at(t, 1), at(t, 3), ALU.mult, ALU.mult)\
                          .then_inc(step, 1)
                    dve.wait_ge(step, count + (5 + 2 * i) * TT)
                    for t in range(TT):
                        nc.vector.scalar_tensor_tensor(at(t, 3), at(t, 4), 1.5, at(t, 3), ALU.add, ALU.mult)\
                          .then_inc(step, 1)
                dve.wait_ge(step, count + TT * ROOT_STEPS)

            def mem_norm(l):
                dve.wait_ge(mem_squared, l * TT + TT)
                rsqrt(TT, stat[:, 9:9 + TT], mem_root_step, l * (TT * ROOT_STEPS))
                dve.wait_ge(mem_gain_in, l * 16 + 16)
                for t in range(TT):
                    nc.vector.scalar_tensor_tensor(memx[:, t, :], memx[:, t, :], root[:, TT + t, 3:4], mem_gain,
                                                   ALU.mult, ALU.mult).then_inc(mem_normed, 1)
                for g in (1, 3):
                    dve.wait_ge(mem_turned, l * 4 + (g + 1))
                    nc.vector.tensor_copy(hT[:, 2 * g:2 * g + 2, :], bank_n(g)).then_inc(memT_dve, 1)

            def mem_values(l):
                dve.wait_ge(mem_made, l * 2 + 2)
                nc.vector.tensor_copy(vx[:, :, :], bank[1][:, :].rearrange("p (a n) -> p a n", a=2))\
                   .then_inc(vx_copied, 1)

            mem_norm(0)
            dve.wait_ge(pos_in_s, 16 * (TT + 1))
            dve.wait_ge(con_in, 16)
            dve.wait_ge(lam_in, 16)
            then(nc.vector.tensor_copy(posf[:, :], posi[:, :]))
            for b in range(TT):
                then(nc.vector.tensor_scalar(dist[:, b, :], posf[:, TT:], posf[:, b:b + 1], None, ALU.subtract))
                then(nc.vector.scalar_tensor_tensor(dist[:, b, :], dist[:, b, :], -1.0, dist[:, b, :], ALU.mult, ALU.max))
            r = slice(C_NOPE, C_DH)
            ang, turns = v0[r, 0, 0:SEQ], v0[r, 0, SEQ:2 * SEQ]
            then(nc.vector.tensor_scalar(ang, posf[r, TT:], con[r, C_INV:C_INV + 1], None, ALU.mult))
            for dst, quarter in ((1, 0.0), (0, 0.25)):
                w = angles[r, dst, :]
                then(nc.vector.tensor_scalar(turns, ang, 1.0 / (2 * math.pi), quarter, ALU.mult, ALU.add))
                then(nc.vector.tensor_scalar(turns, turns, 12582912.0, None, ALU.add))
                then(nc.vector.tensor_scalar(turns, turns, -12582912.0, None, ALU.add))
                then(nc.vector.scalar_tensor_tensor(w, turns, -TWO_PI[0], ang, ALU.mult, ALU.add))
                then(nc.vector.scalar_tensor_tensor(w, turns, -TWO_PI[1], w, ALU.mult, ALU.add))
                then(nc.vector.scalar_tensor_tensor(w, turns, -TWO_PI[2], w, ALU.mult, ALU.add))
                then(nc.vector.tensor_scalar(w, w, quarter * 2 * math.pi, 3.1415925, ALU.add, ALU.min))
                then(nc.vector.tensor_scalar(w, w, -3.1415925, None, ALU.max))
            lq = lam_all.rearrange("p (a b d) -> p a b d", b=2, d=A_DH)
            pr = cT[:, 0, :].rearrange("p (a d) -> p a d", d=A_DH)
            then(nc.vector.tensor_tensor(pr, lq[:, :, 0, :], lq[:, :, 1, :], ALU.mult))
            then(nc.vector.tensor_reduce(small[:, 0:4], pr, AX_X, ALU.add))
            assert steps[0] == SETUP_ANGLES

            mem_values(0)
            dve.wait_ge(setup_act, 1)
            ex = small[:, 4:8].rearrange("p (l a) -> p l a", a=2)
            then(nc.vector.tensor_tensor(small[:, 8:10], ex[:, :, 1], ex[:, :, 0], ALU.subtract))
            then(nc.vector.tensor_tensor(lamt[:, :], small[:, 8:10], con[:, C_LAM:C_LAM + DEPTH], ALU.subtract))
            for count in (gain_used, layer_done, mix_sum, main_r["added"], more_r["added"]):
                dve.sem_inc(count, 1)

            def norm(l, n, src, dst):
                dve.wait_ge(squared, l * 6 + (2 * n + 2))
                rsqrt(0, stat[:, 0:TT], root_step, l * (3 * TT * ROOT_STEPS) + n * TT * ROOT_STEPS)
                dve.wait_ge(gain_in, l * 48 + (16 * n + 16))
                for t in range(TT):
                    nc.vector.scalar_tensor_tensor(dst[:, t, :], src[:, t, :], root[:, t, 3:4], gain[:, :],
                                                   ALU.mult, ALU.mult).then_inc(normed, 1)
                dve.wait_ge(normed, l * 6 + (2 * n + 2))
                dve.sem_inc(gain_used, 1)

            def copy_hT(l, n):
                for g in (1, 3):
                    dve.wait_ge(turned, l * 12 + (4 * n + g + 1))
                    nc.vector.tensor_copy(hT[:, 2 * g:2 * g + 2, :], bank_n(g)).then_inc(hT_dve, 1)

            def rope(l, n, dst, src, heads):
                cos = ropes[r, 0:1, :].broadcast_to([C_ROPE, heads, SEQ])
                sin = ropes[r, 1:2, :].broadcast_to([C_ROPE, heads, SEQ])
                tmp = oBC[r, 6:6 + heads, :]
                nc.vector.tensor_tensor(tmp, src, sin, ALU.mult).then_inc(rope_step, 1)
                nc.vector.tensor_tensor(dst, dst, cos, ALU.mult).then_inc(rope_step, 1)
                dve.wait_ge(rope_step, l * 10 + (2 * n + 2))
                return nc.vector.tensor_tensor(dst, dst, tmp, ALU.add)

            def job(l, name):
                n = JOB_NAMES.index(name)
                wait_made(dve, l, name)
                b = bank[n % 2][:, :]
                b2 = b.rearrange("p (a n) -> p a n", a=2)
                kind, i = name[:-1], name[-1]
                if kind in ("aq", "bq"):
                    dst = q0 if kind == "aq" else q1
                    last = nc.vector.tensor_scalar(dst[:, 2 * int(i):2 * int(i) + 2, :], b2, A_DH ** -0.5, None, ALU.mult)
                elif kind in ("ak", "bk"):
                    dst, c = (k0 if kind == "ak" else k1), 2 * int(i)
                    dve.wait_ge(zeroed, l * 4 + 4)
                    nc.vector.tensor_copy(dst[0:64, c:c + 2, 0:SEQ], b2[0:64])
                    last = nc.vector.tensor_copy(dst[64:128, c:c + 2, SEQ:2 * SEQ], b2[64:128])
                elif kind in ("av", "bv"):
                    dst, c = (v0 if kind == "av" else v1), 256 * int(i)
                    last = nc.vector.tensor_copy(dst[:, :, c:c + 256], b2)
                elif name in ("c0", "c1"):
                    c = 2 * int(i)
                    last = nc.vector.tensor_copy(cT[:, c:c + 2, :], b2)
                elif name == "c2":
                    dve.wait_ge(scored, l * NI + B0)
                    nc.vector.tensor_copy(cT[:, 4, :], b2[:, 0, :])
                    last = nc.vector.tensor_copy(kc[r, 0, :], b2[r, 1, :])
                elif kind == "ck" and name != "ckr":
                    c = 2 * int(i)
                    last = nc.vector.tensor_copy(kc[0:C_NOPE, c:c + 2, :], b2[0:C_NOPE])
                elif kind == "cr":
                    c = 2 * int(i)
                    last = rope(l, 1 + int(i), q0[r, c:c + 2, :], b2[r], 2)
                elif name == "ckr":
                    last = rope(l, 0, kc[r, 0:1, :], b2[r, 0:1, :], 1)
                    last.then_inc(copied["dve"], 1)
                    wait_copied(dve, l, "ckr")
                    nc.vector.tensor_copy(kc[r, 1:8, :], kc[r, 0:1, :].broadcast_to([C_ROPE, 7, SEQ]))\
                      .then_inc(kr_spread, 1)
                    return
                last.then_inc(copied["dve"], 1)

            def maxima(l, i):
                pb = i % NPB
                src = bank[2 + i % 2][:, :].rearrange("p (a n) -> p a n", a=2)
                dve.wait_ge(scored, l * NI + (i + 1))
                b = i % 2
                if i >= NPB:
                    dve.wait_ge(probs_turned, l * NI + (i - NPB + 1))
                if i < B0:
                    nc.vector.scalar_tensor_tensor(prob[:, pb, :, :], dist[:, b:b + 1, :].broadcast_to([P, 2, SEQ]),
                                                   -slopes(A_HEADS)[i // 2], src, ALU.mult, ALU.add).then_inc(biased, 1)
                elif i < C0:
                    hd = 2 * ((i - B0) // 2)
                    at = C_STRIP + hd * STRIP
                    if i == B0:
                        dve.wait_ge(strips_in, 16)
                    strip = con[:, at:at + 2 * STRIP].rearrange("p (a n) -> p a n", a=2)[:, :, P - b * P:P - b * P + SEQ]
                    nc.vector.tensor_tensor(prob[:, pb, :, :], src, strip, ALU.add).then_inc(biased, 1)
                if i < C0:
                    dve.wait_ge(biased, l * C0 + (i + 1))
                    src = prob[:, pb, :, :]
                nc.vector.tensor_reduce(mx[:, pb, :], src, AX_X, ALU.max, negate=True).then_inc(maxed, 1)

            def weigh(l, i):
                pb = i % NPB
                dve.wait_ge(exped, l * NI + (i + 1))
                nc.vector.reciprocal(rs[:, pb, 0:2], sm[:, pb, :]).then_inc(inverted, 1)
                dve.wait_ge(inverted, l * NI + (i + 1))
                if i < B0:
                    nc.vector.tensor_scalar(rs[:, pb, 2:3], rs[:, pb, 1:2], lamcur, None, ALU.mult).then_inc(a_scaled, 1)
                    dve.wait_ge(a_scaled, l * 16 + (2 * i + 1))
                    nc.vector.tensor_scalar(prob[:, pb, 1, :], prob[:, pb, 1, :], rs[:, pb, 2:3], None, ALU.mult)\
                      .then_inc(a_scaled, 1)
                    dve.wait_ge(a_scaled, l * 16 + (2 * i + 2))
                    nc.vector.scalar_tensor_tensor(prob[:, pb, 0, :], prob[:, pb, 0, :], rs[:, pb, 0:1],
                                                   prob[:, pb, 1, :], ALU.mult, ALU.add).then_inc(weighed, 1)
                else:
                    nc.vector.tensor_scalar(prob[:, pb, 0, :], prob[:, pb, 0, :], rs[:, pb, 0:1], None, ALU.mult)
                    nc.vector.tensor_scalar(prob[:, pb, 1, :], prob[:, pb, 1, :], rs[:, pb, 1:2], None, ALU.mult)\
                      .then_inc(weighed, 1)

            def copy_out(l, u):
                dve.wait_ge(pv_done, l * NI + (2 * u + 2))
                if u < 4:
                    dst = oa[:, u, :]
                elif u < 12:
                    dst = oBC[:, u - 4, :]
                else:
                    dst = oa[:, u - 12, :]
                nc.vector.tensor_copy(dst, bank[6 + u % 2][:, 0:SEQ]).then_inc(out_copied, 1)

            def experts_round(S, wait_w3, wait_w2b, rd, q, look, sel_next):
                def make_sel(cols):
                    nc.vector.tensor_tensor(
                        sel.rearrange("p t (e s) -> p t e s", e=QUAD),
                        iota.rearrange("p (a b s) -> p a b s", a=1, b=1).broadcast_to([P, TT, QUAD, CAP]),
                        place[:, :, cols].rearrange("p t (e s) -> p t e s", s=1).broadcast_to([P, TT, QUAD, CAP]),
                        ALU.is_equal).then_inc(S["sel_made"], 1)

                def copy_xt(k):
                    dve.wait_ge(S["gathered"], k)
                    nc.vector.tensor_copy(xt[:, 4:8, :], bank[1][:, :].rearrange("p (c n) -> p c n", c=4))\
                       .then_inc(S["xt_dve"], 1)

                if look is not None:
                    make_sel(bass.ds(q * QUAD + QUAD, QUAD))
                else:
                    make_sel(bass.ds(q * QUAD, QUAD))
                    copy_xt(rd + 1)
                here = bass.ds(q * QUAD, QUAD)
                sw = selw.rearrange("p t (e s) -> p t e s", e=QUAD)
                nc.vector.tensor_tensor(
                    sw, iota.rearrange("p (a b s) -> p a b s", a=1, b=1).broadcast_to([P, TT, QUAD, CAP]),
                    place[:, :, here].rearrange("p t (e s) -> p t e s", s=1).broadcast_to([P, TT, QUAD, CAP]),
                    ALU.is_equal).then_inc(S["selw_step"], 1)
                dve.wait_ge(S["selw_step"], rd + 1)
                nc.vector.tensor_tensor(
                    sw, sw, weight[:, :, here].rearrange("p t (e s) -> p t e s", s=1).broadcast_to([P, TT, QUAD, CAP]),
                    ALU.mult).then_inc(S["selw_made"], 1)
                dve.wait_ge(S["e_made"], rd + 1)
                nc.vector.tensor_scalar(act_e, act_e, 1.0, None, ALU.add).then_inc(S["silu_step"], 1)
                dve.wait_ge(S["silu_step"], rd * 3 + 1)
                nc.vector.reciprocal(act_r, act_e).then_inc(S["silu_step"], 1)
                dve.wait_ge(S["silu_step"], rd * 3 + 2)
                nc.vector.tensor_tensor(act_r, bank[2][:, :], act_r, ALU.mult).then_inc(S["silu_step"], 1)
                dve.wait_ge(S["silu_step"], rd * 3 + 3)
                wait_w3(dve)
                nc.vector.tensor_tensor(hidden, bank[3][:, :], act_r, ALU.mult).then_inc(S["hidden_made"], 1)
                if look is not None:
                    copy_xt(look)
                wait_w2b(dve)
                nc.vector.tensor_copy(yexp[:, 512:1024], bank[7][:, :]).then_inc(S["y_dve"], 1)
                for c in range(4):
                    t, half = divmod(c, 2)
                    dve.wait_ge(S["combined"], rd * 4 + (c + 1))
                    xs = x[:, t, half * 512:half * 512 + 512]
                    nc.vector.tensor_tensor(xs, xs, bank[(5, 2)[c % 2]][:, :], ALU.add).then_inc(S["added"], 1)

            gcur, lamcur = small[:, 40:46], small[:, 46:47]
            with dve.Fori(0, DEPTH) as l:
                row = bass.ds(l, 1)
                nc.vector.tensor_copy(lamcur, lamt[:, row]).then_inc(layer_cols, 1)
                norm(l, 0, x, h)
                copy_hT(l, 0)
                for name in ("aq1", "ak1", "av1"):
                    job(l, name)
                for i in range(X0 + LAG_OUT + 1):
                    if i < X0:
                        maxima(l, i)
                    if 1 <= i <= X0:
                        if i == 1:
                            dve.wait_ge(layer_cols, l * 3 + 1)
                        weigh(l, i - 1)
                    for name in FILL.get(i, []):
                        if JOBS[JOB_NAMES.index(name)][3] == "dve":
                            job(l, name)
                    if i == 10:
                        dve.wait_ge(cols_in, 16 * 3 * DEPTH)
                        nc.vector.tensor_copy(gcur[:, 0:5], gcol[:, row, 0:5].rearrange("p a n -> p (a n)"))\
                          .then_inc(layer_cols, 1)
                        nc.vector.tensor_tensor(gcur[:, 5:6], gcol[:, row, 5], con[:, bass.ds(l + C_LAM + DEPTH, 1)],
                                                ALU.mult).then_inc(layer_cols, 1)
                        dve.wait_ge(layer_cols, l * 3 + 3)
                        dve.wait_ge(c_rstd, l + 1)
                        for c in range(5):
                            nc.vector.scalar_tensor_tensor(cT[:, c, :], cT[:, c, :], gcur[:, c:c + 1],
                                                           wide[:, 2 + c // 3, :], ALU.mult, ALU.mult).then_inc(c_scaled, 1)
                    if i == 21:
                        dve.wait_ge(a_rstd, l + 1)
                        nc.vector.scalar_tensor_tensor(oa[:, :, :], oa[:, :, :], gcur[:, 5:6], wide[:, :, :],
                                                       ALU.mult, ALU.mult).then_inc(a_normed, 1)
                    if i >= LAG_OUT and (i - LAG_OUT) % 2 == 1:
                        copy_out(l, (i - LAG_OUT) // 2)
                for pair in range(4):
                    for n in range(N_BRANCHES):
                        e = flat[n]
                        g = 3 * pair + n
                        dve.wait_ge(gate_exp, l * 12 + (g + 1))
                        nc.vector.tensor_scalar(e, e, 1.0, None, ALU.add).then_inc(gate_step, 1)
                        dve.wait_ge(gate_step, l * 28 + (7 * pair + 2 * n + 1))
                        nc.vector.reciprocal(e, e).then_inc(gate_step, 1)
                        dve.wait_ge(gate_step, l * 28 + (7 * pair + 2 * n + 2))
                        if n == 0:
                            dve.wait_ge(branch0, l * 4 + (pair + 1))
                        else:
                            wait_free(dve, l, T_GATE + 5 * pair + 2 + n)
                        nc.vector.tensor_tensor(e, bank[(6 * pair + 3 + n) % 8][:, :], e, ALU.mult).then_inc(mixed, 1)
                    dve.wait_ge(mixed, l * 12 + (3 * pair + 3))
                    nc.vector.tensor_tensor(flat[0], flat[0], flat[1], ALU.add).then_inc(gate_step, 1)
                    dve.wait_ge(gate_step, l * 28 + (7 * pair + 7))
                    nc.vector.tensor_tensor(q0[:, 2 * pair:2 * pair + 2, :].rearrange("p a n -> p (a n)"), flat[0],
                                            flat[2], ALU.add).then_inc(mix_sum, 1)
                for o in range(4):
                    half, t = divmod(o, 2)
                    if t == 0:
                        dve.wait_ge(projected, l * 5 + (half + 1))
                    else:
                        wait_free(dve, l, T_OUT + 2 * half + 1)
                    xs = x[:, t, half * 512:half * 512 + 512]
                    nc.vector.tensor_tensor(xs, xs, bank[o][:, :], ALU.add).then_inc(x_added, 1)
                dve.wait_ge(x_added, l * 8 + 4)
                norm(l, 1, x, h)
                copy_hT(l, 1)
                for i in range(X0, NI + LAG_OUT):
                    if i < NI:
                        maxima(l, i)
                    if X0 < i <= NI:
                        weigh(l, i - 1)
                    if i - LAG_OUT >= X0 and (i - LAG_OUT) % 2 == 1:
                        copy_out(l, (i - LAG_OUT) // 2)
                for o in range(4):
                    t, half = divmod(o, 2)
                    if o < 3:
                        dve.wait_ge(projected, l * 5 + (2 + o + 1))
                    else:
                        wait_free(dve, l, T_XO)
                    xs = x[:, t, half * 512:half * 512 + 512]
                    nc.vector.tensor_tensor(xs, xs, bank[o][:, :], ALU.add).then_inc(x_added, 1)
                dve.wait_ge(x_added, l * 8 + 8)
                norm(l, 2, x, h)
                copy_hT(l, 2)

                rstep = [0]

                def step(ins):
                    rstep[0] += 1
                    ins.then_inc(route_step, 1)
                    dve.wait_ge(route_step, l * ROUTE_STEPS + rstep[0])
                    plain(dve)

                dve.wait_ge(router_in, l * 64 + 64)
                dve.wait_ge(logits_made, l + 1)
                nc.vector.memset(place[:, :, N_EXPERTS:], -1.0)
                nc.vector.memset(weight[:, :, N_EXPERTS:], 0.0)
                step(nc.vector.tensor_tensor(logit[:, :, :],
                                             bank[0][:, 0:128].rearrange("p (t n) -> p t n", t=TT)[:, :, 0:36],
                                             router_b[:, :].rearrange("p (a n) -> p a n", a=1)
                                             .broadcast_to([P, TT, 36]), ALU.add))
                step(nc.vector.tensor_copy(gpad[:, :, 0:N_GROUPS], logit[:, :, 0:N_GROUPS]))
                for t in range(TT):
                    f = small[:, 48 + 8 * t:56 + 8 * t]
                    el = logit[:, t, N_GROUPS:]
                    step(nc.vector.max(top[:, t, 0, :], gpad[:, t, :]))
                    step(nc.vector.max_index(topi[:, t, 0, :], top[:, t, 0, :], gpad[:, t, :]))
                    step(nc.vector.tensor_copy(f[:, 0:1], topi[:, t, 0, 0:1]))
                    step(nc.vector.tensor_scalar(rt[:, t, 0, :], con[:, C_GID:C_GID + N_EXPERTS], f[:, 0:1], None,
                                                 ALU.is_equal))
                    step(nc.vector.tensor_scalar(rt[:, t, 0, :], rt[:, t, 0, :], -FAR, FAR, ALU.mult, ALU.add))
                    step(nc.vector.tensor_tensor(rt[:, t, 1, :], rt[:, t, 0, :], el, ALU.add))
                    step(nc.vector.max(top[:, t, 2, :], rt[:, t, 1, :]))
                    step(nc.vector.max_index(topi[:, t, 1, :], top[:, t, 2, :], rt[:, t, 1, :]))
                    step(nc.vector.tensor_copy(f[:, 1:3], topi[:, t, 1, 0:2]))
                    nc.vector.tensor_scalar(small[:, 10 + 2 * t:11 + 2 * t], top[:, t, 0, 0:1], -1.0, None, ALU.mult)
                    nc.vector.tensor_scalar(small[:, 11 + 2 * t:12 + 2 * t], top[:, t, 2, 0:1], -1.0, None, ALU.mult)\
                      .then_inc(route_ask, 1)
                    i1, i2 = f[:, 1:2], f[:, 2:3]
                    experts = con[:, C_IOTA:C_IOTA + N_EXPERTS]
                    step(nc.vector.tensor_scalar(rt[:, t, 2, :], experts, i1, None, ALU.is_equal))
                    step(nc.vector.tensor_scalar(rt[:, t, 3, :], experts, i2, None, ALU.is_equal))
                    nc.vector.tensor_tensor(chosen[:, t, :], rt[:, t, 2, :], rt[:, t, 3, :], ALU.add).then_inc(chosen_s, 1)
                for t in range(TT):
                    f = small[:, 48 + 8 * t:56 + 8 * t]
                    sg, q2 = small[:, 24 + 2 * t:25 + 2 * t], small[:, 25 + 2 * t:26 + 2 * t]
                    dve.wait_ge(route_exp, l * 2 + (t + 1))
                    step(nc.vector.tensor_scalar(f[:, 3:4], q2, 1.0, sg, ALU.add, ALU.mult))
                    step(nc.vector.reciprocal(f[:, 4:5], f[:, 3:4]))
                    step(nc.vector.tensor_tensor(f[:, 5:6], f[:, 4:5], q2, ALU.mult))
                    step(nc.vector.tensor_scalar(rt[:, t, 3, :], rt[:, t, 3, :], f[:, 5:6], None, ALU.mult))
                    step(nc.vector.scalar_tensor_tensor(weight[:, t, 0:N_EXPERTS], rt[:, t, 2, :], f[:, 4:5],
                                                        rt[:, t, 3, :], ALU.mult, ALU.add))
                dve.wait_ge(ranked, l + 1)
                rank = bank[1][:, 0:64].rearrange("p (t n) -> p t n", t=TT)
                step(nc.vector.scalar_tensor_tensor(place[:, :, 0:N_EXPERTS], rank, 1.0, chosen[:, :, :], ALU.add, ALU.mult))
                step(nc.vector.tensor_scalar(place[:, :, 0:N_EXPERTS], place[:, :, 0:N_EXPERTS], -1.0, None, ALU.add))
                step(nc.vector.tensor_reduce(small[:, 47:48], bank[1][:, 64:96], AX_X, ALU.max))
                nc.vector.tensor_scalar(flag[:, :], small[:, 47:48], float(CAP), None, ALU.is_gt).then_inc(placed, 1)
                assert rstep[0] == ROUTE_STEPS

                S = main_r
                nc.vector.tensor_tensor(
                    sel.rearrange("p t (e s) -> p t e s", e=QUAD),
                    iota.rearrange("p (a b s) -> p a b s", a=1, b=1).broadcast_to([P, TT, QUAD, CAP]),
                    place[:, :, 0:QUAD].rearrange("p t (e s) -> p t e s", s=1).broadcast_to([P, TT, QUAD, CAP]),
                    ALU.is_equal).then_inc(S["sel_made"], 1)
                dve.wait_ge(S["gathered"], l * (QUADS + 1) + 1)
                nc.vector.tensor_copy(xt[:, 4:8, :], bank[1][:, :].rearrange("p (c n) -> p c n", c=4))\
                   .then_inc(S["xt_dve"], 1)

                def main_round(q):
                    base = l * PER_LAYER + q * PER_QUAD
                    experts_round(S, lambda e: e.wait_ge(slot_free, base + (Q_BASE + RING + 2 * KD)),
                                  lambda e: e.wait_ge(slot_free, base + (Q_BASE + RING + PER_QUAD)),
                                  l * QUADS + q, q, l * (QUADS + 1) + q + 2, None)

                with dve.Fori(0, QUADS - 1) as q:
                    main_round(q)
                with dve.If(l < DEPTH - 1):
                    mem_norm(dve.snap(l) + 1)
                    mem_values(dve.snap(l) + 1)
                main_round(QUADS - 1)
                dve.wait_ge(S["added"], l * (4 * QUADS) + (4 * QUADS + 1))
                dve.wait_ge(placed, l + 1)
                plain(dve)
                over = dve.value_load(flag[0:1, 0:1], min_val=0, max_val=1)
                with dve.If(over > 0):
                    with dve.Fori(0, PASSES - 1) as p:
                        nc.vector.tensor_scalar(place[:, :, 0:N_EXPERTS], place[:, :, 0:N_EXPERTS], -float(CAP), None,
                                                ALU.add).then_inc(shifted, 1)
                        with dve.Fori(0, QUADS) as q:
                            rd = dve.snap(more) + p * QUADS + q
                            dve.wait_ge(shifted, dve.snap(more_passes) + p + 1)
                            experts_round(more_r, lambda e: e.wait_ge(more_free, rd * PER_QUAD + (RING + 2 * KD)),
                                          lambda e: e.wait_ge(more_free, rd * PER_QUAD + (RING + PER_QUAD)),
                                          rd, q, None, None)
                    dve.reg_add(more, more, (PASSES - 1) * QUADS)
                    dve.reg_add(more_passes, more_passes, PASSES - 1)
                    dve.wait_ge(more_r["added"], dve.snap(more) * 4 + 1)
                    plain(dve)
                dve.sem_inc(layer_done, 1)
            norm(DEPTH, 0, x, h)

        @block.tensor
        def _(pe):
            more = pe.alloc_register("pe_more_rounds")
            pe.reg_mov(more, 0)
            pe.sem_inc(slot_free, RING)
            pe.sem_inc(more_free, RING)
            pe.wait_ge(con_in, 16)

            def turn_tokens(l, n, src):
                for t in range(TT):
                    pe.wait_ge(normed, l * 6 + (2 * n + t + 1))
                    for g in range(4):
                        for kk in range(2):
                            k = 2 * g + kk
                            at = kk * SEQ + t * P
                            last = nc.tensor.transpose(bank[NORM_BANKS[g]][:, at:at + P], src[:, t, k * P:(k + 1) * P], ident)
                        if t == TT - 1:
                            last.then_inc(turned, 1)
                pe.wait_ge(hT_act, l * 6 + (2 * n + 2))
                pe.wait_ge(hT_dve, l * 6 + (2 * n + 2))

            def features(dst, w, cols, src, kn):
                for k in range(kn):
                    last = nc.tensor.matmul(dst, w[:, k, cols], src[:, k, :], start=k == 0, stop=k == kn - 1)
                return last

            def tokens(dst, w, src, t, kn):
                for k in range(kn):
                    last = nc.tensor.matmul(dst, src[:, k, t * P:(t + 1) * P], w[:, k], start=k == 0, stop=k == kn - 1)
                return last

            def job(l, name):
                n = JOB_NAMES.index(name)
                turn, frees = JOBS[n][1:3]
                if n >= 2:
                    wait_copied(pe, l, JOB_NAMES[n - 2])
                if turn is not None:
                    wait_turn(pe, l, turn)
                b = bank[n % 2]
                kind, i = name[:-1], name[-1]
                if kind in ("aq", "bq", "ak", "bk") or name in ("c0", "c1"):
                    w = slot_k(turn, 8, 256)
                    for c in range(2):
                        last = features(b[:, c * SEQ:(c + 1) * SEQ], w, slice(c * P, (c + 1) * P), hT, KD)
                elif kind in ("av", "bv"):
                    w = slot_k(turn, 8, 256)
                    for t in range(TT):
                        last = tokens(b[:, t * 256:(t + 1) * 256], w, hT, t, KD)
                elif name == "c2":
                    w = slot_k(turn, 8, 160)
                    features(b[:, 0:SEQ], w, slice(0, P), hT, KD)
                    last = features(b[C_NOPE:C_DH, SEQ:2 * SEQ], w, slice(P, P + C_ROPE), hT, KD)
                elif name == "cs":
                    pe.wait_ge(c_squared, l + 1)
                    for k in range(3):
                        nc.tensor.matmul(b[:, 0:SEQ], ones, q0[:, k, :], start=k == 0, stop=k == 2)
                    for k in range(2):
                        last = nc.tensor.matmul(b[:, SEQ:2 * SEQ], ones, q0[:, 3 + k, :], start=k == 0, stop=k == 1)
                elif kind == "cq":
                    pe.wait_ge(c_scaled, l * 5 + 5)
                    w = slot_k(turn, 3, 384)
                    for j in range(2):
                        at = (2 * int(i) + j) % 4 * C_DH
                        last = features(b[0:C_DH, j * SEQ:(j + 1) * SEQ], w, slice(at, at + C_DH), cT, 3)
                elif kind == "ck" and name != "ckr":
                    w = slot_k(turn, 2, 1024)
                    for j in range(2):
                        at = (2 * int(i) + j) * (C_NOPE + C_DV)
                        last = features(b[0:C_NOPE, j * SEQ:(j + 1) * SEQ], w, slice(at, at + C_NOPE), cT[:, 3:5, :], 2)
                elif kind == "cv":
                    w = slot_k(turn, 2, 1024).rearrange("p k (h n) -> p k h n", h=C_HEADS)[:, :, :, C_NOPE:]
                    last = tokens(b[:, :].rearrange("p (h n) -> p h n", h=C_HEADS), w, cT[:, 3:5, :], int(i), 2)
                elif kind == "cr":
                    wait_copied(pe, l, "cq" + i)
                    last = nc.tensor.matmul(b[C_NOPE:C_DH, :], con[0:C_DH, C_SWAP:C_SWAP + C_ROPE],
                                            q0[0:C_DH, 2 * int(i):2 * int(i) + 2, :], start=True, stop=True)
                elif name == "ckr":
                    last = nc.tensor.matmul(b[C_NOPE:C_DH, 0:SEQ], con[0:C_DH, C_SWAP:C_SWAP + C_ROPE],
                                            kc[0:C_DH, 0, :], start=True, stop=True)
                elif kind == "as":
                    pe.wait_ge(a_squared, l + 1)
                    last = nc.tensor.matmul(b[:, :], ones, wide[:, 2 * int(i):2 * int(i) + 2, :], start=True, stop=True)
                last.then_inc(slot_free if frees else made, 1)

            def mem_stage(l):
                for t in range(TT):
                    pe.wait_ge(mem_normed, l * 2 + (t + 1))
                    for g in range(4):
                        for kk in range(2):
                            k = 2 * g + kk
                            at = kk * SEQ + t * P
                            last = nc.tensor.transpose(bank[NORM_BANKS[g]][:, at:at + P],
                                                       memx[:, t, k * P:(k + 1) * P], ident)
                        if t == TT - 1:
                            last.then_inc(mem_turned, 1)
                pe.wait_ge(memT_act, l * 2 + 2)
                pe.wait_ge(memT_dve, l * 2 + 2)
                pe.wait_ge(mem_w_in, l * 32 + 32)
                for c in range(2):
                    last = features(bank[0][:, c * SEQ:(c + 1) * SEQ], wxk, slice(c * P, (c + 1) * P), hT, KD)
                last.then_inc(mem_made, 1)
                for t in range(TT):
                    last = tokens(bank[1][:, t * 256:(t + 1) * 256], wxv, hT, t, KD)
                last.then_inc(mem_made, 1)

            def scores(l, i):
                u, b = divmod(i, 2)
                needed = {A0: ("ak0", "ak1"), B0: ("bk0", "bk1"), C0: ("cr0", "ck0"), C0 + 2: ("cr1", "ck0"),
                          C0 + 4: ("cr2", "ck2"), C0 + 6: ("cr3", "ck3")}
                for name in needed.get(i, ()):
                    wait_copied(pe, l, name)
                if i == C0:
                    pe.wait_ge(kr_spread, l + 1)
                if i == X0:
                    pe.wait_ge(qx_copied, l + 1)
                if i >= 2:
                    pe.wait_ge(exped, l * NI + (i - 1))
                dst = bank[2 + i % 2]
                qs = slice(b * P, (b + 1) * P)
                if C0 <= i < X0:
                    for j in range(2):
                        hd = 2 * (u - 8) + j
                        last = nc.tensor.matmul(dst[:, j * SEQ:(j + 1) * SEQ], q0[0:C_DH, hd, qs], kc[0:C_DH, hd, :],
                                                start=True, stop=True)
                else:
                    q, k, c = (q0, k0, u) if i < B0 else (q1, k1, u - 4) if i < C0 else (q1, kx, u - 12)
                    last = nc.tensor.matmul(dst[:, :], q[:, c, qs], k[:, c, :], start=True, stop=True)
                last.then_inc(scored, 1)

            def turn_probs(l, i):
                pe.wait_ge(weighed, l * NI + (i + 1))
                if i >= 2:
                    pe.wait_ge(probsT_copied, l * NI + (i - 1))
                for j in range(1 if i < B0 else 2):
                    for c in range(TT):
                        at = (2 * j + c) * P
                        last = nc.tensor.transpose(bank[4 + i % 2][:, at:at + P], prob[:, i % NPB, j, c * P:(c + 1) * P], ident)
                last.then_inc(probs_turned, 1)

            def products(l, i):
                u, b = divmod(i, 2)
                pe.wait_ge(probsT_copied, l * NI + (i + 1))
                if i == A0:
                    wait_copied(pe, l, "av0")
                    wait_copied(pe, l, "av1")
                if i == B0:
                    wait_copied(pe, l, "bv0")
                    wait_copied(pe, l, "bv1")
                if i == C0:
                    wait_copied(pe, l, "cv1")
                if b == 0 and u >= 2:
                    pe.wait_ge(out_copied, l * (NI // 2) + (u - 1))
                dst = bank[6 + u % 2]
                qs = slice(b * P, (b + 1) * P)
                if i < B0:
                    for c in range(TT):
                        last = nc.tensor.matmul(dst[:, qs], v0[:, c, u * P:(u + 1) * P], probT[:, i % 2, 0, c, :],
                                                start=c == 0, stop=c == TT - 1)
                else:
                    v, hd = (v1, 2 * (u - 4)) if i < C0 else (v0, 2 * (u - 8)) if i < X0 else (vx, 2 * (u - 12))
                    for c in range(TT):
                        for j in range(2):
                            last = nc.tensor.matmul(dst[64 * j:64 * j + 64, qs], v[:, c, (hd + j) * 64:(hd + j + 1) * 64],
                                                    probT[:, i % 2, j, c, :], start=c == 0, stop=c == TT - 1)
                last.then_inc(pv_done, 1)

            def gather(S, k):
                pe.wait_ge(S["sel_made"], k)
                for c in range(KD):
                    for t in range(TT):
                        last = nc.tensor.matmul(bank[c // 4][:, c % 4 * P:(c % 4 + 1) * P], h[:, t, c * P:(c + 1) * P],
                                                sel[:, t, :], start=t == 0, stop=t == TT - 1)
                last.then_inc(S["gathered"], 1)

            def experts_round(S, wait, free, rd, xts, look):
                pe.wait_ge(S["xt_act"], xts)
                pe.wait_ge(S["xt_dve"], xts)
                pe.wait_ge(S["added"], rd * 4 + 1)
                for m in range(2):
                    for k in range(KD):
                        j = m * KD + k
                        wait(j)
                        w = slot_k(j, QUAD, 512)
                        for e in range(QUAD):
                            last = nc.tensor.matmul(bank[2 + m][e * CAP:(e + 1) * CAP, :], xt[:, k, e * CAP:(e + 1) * CAP],
                                                    w[:, e, :], start=k == 0, stop=k == KD - 1)
                        last.then_inc(free, 1)
                if look is not None:
                    gather(S, look)
                pe.wait_ge(S["selw_made"], rd + 1)
                for t in range(TT):
                    last = nc.tensor.transpose(bank[5][:, t * P:(t + 1) * P], selw[:, t, :], ident)
                last.then_inc(S["selw_turned"], 1)
                pe.wait_ge(S["hidden_made"], rd + 1)
                for k in range(4):
                    last = nc.tensor.transpose(bank[4][:, k * P:(k + 1) * P], hidden[:, k * P:(k + 1) * P], ident)
                last.then_inc(S["hidden_turned"], 1)
                pe.wait_ge(S["hiddenT_copied"], rd + 1)
                for half in range(2):
                    for k in range(4):
                        j = 2 * KD + 4 * half + k
                        wait(j)
                        w = slot_k(j, QUAD, 512)
                        for e in range(QUAD):
                            last = nc.tensor.matmul(bank[6 + half][e * CAP:(e + 1) * CAP, :],
                                                    hiddenT[:, k, e * CAP:(e + 1) * CAP], w[:, e, :],
                                                    start=k == 0, stop=k == 3)
                        last.then_inc(free, 1)
                pe.wait_ge(S["selwT_copied"], rd + 1)
                for c in range(4):
                    t, half = divmod(c, 2)
                    pe.wait_ge(S["y_act"] if half == 0 else S["y_dve"], rd + 1)
                    if c >= 2:
                        pe.wait_ge(S["added"], rd * 4 + c)
                    nc.tensor.matmul(bank[(5, 2)[c % 2]][:, :], selwT[:, t * P:(t + 1) * P],
                                     yexp[:, half * 512:half * 512 + 512], start=True, stop=True)\
                      .then_inc(S["combined"], 1)

            mem_stage(0)
            with pe.Fori(0, DEPTH) as l:
                turn_tokens(l, 0, h)
                pe.wait_ge(kx_copied, l + 1)
                pe.wait_ge(vx_copied, l + 1)
                for name in JOB_NAMES[0:6]:
                    job(l, name)
                for i in range(X0 + LAG_PV):
                    if i < X0:
                        scores(l, i)
                    for name in FILL.get(i, []):
                        job(l, name)
                    if LAG_T <= i < X0 + LAG_T:
                        turn_probs(l, i - LAG_T)
                    if i >= LAG_PV:
                        products(l, i - LAG_PV)
                pe.wait_ge(out_copied, l * (NI // 2) + 12)
                pe.wait_ge(a_normed, l + 1)
                wait_copied(pe, l, "as1")
                srcs = (oa, oBC[:, 0:4, :], oBC[:, 4:8, :])
                for pair in range(4):
                    for m in range(2 * N_BRANCHES):
                        g = 6 * pair + m
                        if g >= 8:
                            op, om = divmod(g - 8, 6)
                            if om < 3:
                                pe.wait_ge(gate_exp, l * 12 + (3 * op + om + 1))
                            else:
                                pe.wait_ge(mixed, l * 12 + (3 * op + om - 3 + 1))
                        b = bank[g % 8]
                        n = m % 3
                        if m < 3:
                            turn = T_GATE + 5 * pair + n
                            wait_turn(pe, l, turn)
                            for c in range(2):
                                last = features(b[:, c * SEQ:(c + 1) * SEQ], slot_k(turn, 8, 256),
                                                slice(c * P, (c + 1) * P), hT, KD)
                            last.then_inc(slot_free, 1)
                        else:
                            turn = T_GATE + 5 * pair + (3 if n < 2 else 4)
                            wait_turn(pe, l, turn)
                            w = slot_k(turn, 8, 256)[:, 4 * n:4 * n + 4] if n < 2 else slot_k(turn, 4, 256)
                            for c in range(2):
                                last = features(b[:, c * SEQ:(c + 1) * SEQ], w, slice(c * P, (c + 1) * P), srcs[n], 4)
                            last.then_inc(branch0 if n == 0 else slot_free, 1)
                pe.wait_ge(mix_sum, l * 4 + 5)
                for half in range(2):
                    for kg in range(2):
                        turn = T_OUT + 2 * half + kg
                        wait_turn(pe, l, turn)
                        w = slot_k(turn, 4, 512)
                        for t in range(TT):
                            for k in range(4):
                                last = nc.tensor.matmul(bank[2 * half + t][:, :], q0[:, 4 * kg + k, t * P:(t + 1) * P],
                                                        w[:, k, :], start=kg == 0 and k == 0, stop=kg == 1 and k == 3)
                            if t == 1:
                                last.then_inc(slot_free, 1)
                            elif kg == 1:
                                last.then_inc(projected, 1)
                turn_tokens(l, 1, h)
                wait_turn(pe, l, T_XQ)
                for c in range(2):
                    last = features(bank[0][:, c * SEQ:(c + 1) * SEQ], slot_k(T_XQ, 8, 256), slice(c * P, (c + 1) * P), hT, KD)
                last.then_inc(slot_free, 1)
                for i in range(X0, NI + LAG_PV):
                    if i < NI:
                        scores(l, i)
                    if X0 + LAG_T <= i < NI + LAG_T:
                        turn_probs(l, i - LAG_T)
                    if i >= X0 + LAG_PV:
                        products(l, i - LAG_PV)
                pe.wait_ge(out_copied, l * (NI // 2) + 14)
                wait_turn(pe, l, T_XO)
                w = slot_k(T_XO, 2, 1024)
                for o in range(4):
                    t, half = divmod(o, 2)
                    for k in range(2):
                        last = nc.tensor.matmul(bank[o][:, :], oa[:, k, t * P:(t + 1) * P],
                                                w[:, k, half * 512:half * 512 + 512], start=k == 0, stop=k == 1)
                    if o < 3:
                        last.then_inc(projected, 1)
                    else:
                        last.then_inc(slot_free, 1 + EMPTY)
                turn_tokens(l, 2, h)
                pe.wait_ge(router_in, l * 64 + 64)
                for t in range(TT):
                    for k in range(KD):
                        last = nc.tensor.matmul(bank[0][:, t * 64:t * 64 + 36], hT[:, k, t * P:(t + 1) * P], router_w[:, k, :],
                                                start=k == 0, stop=k == KD - 1)
                last.then_inc(logits_made, 1)
                pe.wait_ge(chosen_s, l * 2 + 2)
                b = bank[1]
                nc.tensor.matmul(b[:, 0:32], before, chosen[:, 0, :], start=True, stop=True)
                nc.tensor.matmul(b[:, 32:64], ones, chosen[:, 0, :], start=True, stop=False)
                nc.tensor.matmul(b[:, 32:64], before, chosen[:, 1, :], start=False, stop=True)
                nc.tensor.matmul(b[:, 64:96], ones, chosen[:, 0, :], start=True, stop=False)
                nc.tensor.matmul(b[:, 64:96], ones, chosen[:, 1, :], start=False, stop=True).then_inc(ranked, 1)
                S = main_r
                gather(S, l * (QUADS + 1) + 1)

                def main_round(q):
                    def wait_main(j):
                        s = j % RING
                        pe.wait_ge(landed[s], l * (16 * real_turns(s, PER_LAYER)) + q * (16 * PER_QUAD // RING)
                                   + 16 * real_turns(s, Q_BASE + j + 1))
                    experts_round(S, wait_main, slot_free, l * QUADS + q, l * (QUADS + 1) + q + 1,
                                  l * (QUADS + 1) + q + 2)

                with pe.Fori(0, QUADS - 1) as q:
                    main_round(q)
                with pe.If(l < DEPTH - 1):
                    pe.wait_ge(S["xt_act"], l * (QUADS + 1) + QUADS)
                    pe.wait_ge(S["xt_dve"], l * (QUADS + 1) + QUADS)
                    mem_stage(pe.snap(l) + 1)
                    pe.wait_ge(kx_copied, pe.snap(l) + 2)
                    pe.wait_ge(vx_copied, pe.snap(l) + 2)
                main_round(QUADS - 1)
                pe.wait_ge(placed, l + 1)
                plain(pe)
                over = pe.value_load(flag[0:1, 0:1], min_val=0, max_val=1)
                with pe.If(over > 0):
                    with pe.Fori(0, PASSES - 1) as p:
                        with pe.Fori(0, QUADS) as q:
                            rd = pe.snap(more) + p * QUADS + q

                            def wait_more(j):
                                pe.wait_ge(more_landed[j % RING], rd * (16 * PER_QUAD // RING) + 16 * (j // RING + 1))
                            pe.wait_ge(main_r["xt_act"], l * (QUADS + 1) + QUADS + 1)
                            pe.wait_ge(main_r["xt_dve"], l * (QUADS + 1) + QUADS + 1)
                            gather(more_r, rd + 1)
                            experts_round(more_r, wait_more, more_free, rd, rd + 1, None)
                    pe.reg_add(more, more, (PASSES - 1) * QUADS)
                pe.wait_ge(layer_done, l + 2)


_INS = ["x", "mem", "positions", "mix_norm_g", "w_in", "diff_lambda", "diff_subln_g", "mla_q_norm_g", "w_uq",
        "mla_kv_norm_g", "w_ukv", "w_branch", "w_out", "cross_norm_g", "mem_norm_g", "w_xq", "w_xkv", "w_xo",
        "ffn_norm_g", "w_group", "b_group", "w_router", "b_router", "w1", "w3", "w2", "final_norm_g"]


def kernel(**inputs):
    import numpy as np
    import concourse.bacc as bacc
    from concourse.bass_utils import run_bass_kernel_spmd

    nc = bacc.Bacc("TRN2", target_bir_lowering=False, num_devices=1)
    arrays, args = {}, []
    for name in _INS:
        a = np.ascontiguousarray(inputs[name])
        arrays[f"in_{name}_dram"] = a
        args.append(nc.dram_tensor(f"in_{name}_dram", a.shape, mybir.dt.from_np(a.dtype), kind="ExternalInput").ap())
    c = shape_constants()
    arrays["consts_dram"] = c
    args.append(nc.dram_tensor("consts_dram", c.shape, F32, kind="ExternalInput").ap())
    args.append(nc.dram_tensor("out_dram", (1, SEQ, D), F32, kind="ExternalOutput").ap())
    bass_hybrid_encoder(nc, *args)
    r = run_bass_kernel_spmd(nc, [arrays], core_ids=[0])
    return r.results[0]["out_dram"]
```

```python
import math
from contextlib import ExitStack

import concourse.bass as bass
from concourse import mybir

F32 = mybir.dt.float32
I32 = mybir.dt.int32
U32 = mybir.dt.uint32
ALU = mybir.AluOpType
ACT = mybir.ActivationFunctionType
AX_X = mybir.AxisListType.X

P = 128
DEPTH, D, SEQ = 2, 1024, 256
KD = D // P
TT = SEQ // P
A_HEADS, A_DH, A_DV = 4, 64, 128
B_HEADS, B_DH = 8, 64
B_PATTERNS = ((128, 1), (512, 4), (2048, 16))
C_HEADS, C_NOPE, C_ROPE, C_DV = 8, 64, 32, 64
C_Q_RANK, C_KV_RANK = 384, 256
C_DH = C_NOPE + C_ROPE
ROPE_THETA = 10000.0
X_HEADS, X_DH = 4, 64
N_BRANCHES, WIDTH = 3, 512
N_GROUPS, PER_GROUP, N_EXPERTS, D_EXPERT = 4, 8, 32, 512
EPS = 1e-6
TWO_PI = (6.28125, 0.0019350051879882812, 3.0199159795e-07)
NORM_BANKS = (3, 4, 6, 7)
SUM_BANKS = (0, 1, 2, 5)
SETUP_ANGLES = 24
ROUTE_STEPS = 31
ROOT_STEPS = 10
ROOT_START = 0x5F3759DF
FAR = -1e30

RING = 12
SLOT = 2048
CAP = 32
QUAD = 4
QUADS = N_EXPERTS // QUAD
PASSES = SEQ // CAP
NPB = 3

OFF_AQ, OFF_AK, OFF_AV = 0, 512, 1024
OFF_BQ, OFF_BK, OFF_BV = 1536, 2048, 2560
OFF_CQ, OFF_CKR, OFF_GATE = 3072, 3712, 3744

C_ID, C_BEFORE, C_ONES, C_SWAP, C_IOTA, C_GID, C_INV, C_LAM = 0, 128, 256, 384, 416, 449, 481, 482
C_STRIP = 488
STRIP = SEQ + P
N_CONST = C_STRIP + B_HEADS * STRIP


def slopes(n):
    return [2.0 ** (-8.0 * i / n) for i in range(1, n + 1)]


def lam_init(layer):
    return 0.8 - 0.6 * math.exp(-0.3 * layer)


def shape_constants():
    import numpy as np
    c = np.zeros((P, N_CONST), np.float32)
    r = np.arange(P)
    c[:, C_ID:C_ID + P] = r[:, None] == r[None, :]
    c[:, C_BEFORE:C_BEFORE + P] = r[:, None] < r[None, :]
    c[:, C_ONES:C_ONES + P] = 1.0
    half = C_ROPE // 2
    for i in range(half):
        c[C_NOPE + half + i, C_SWAP + i] = -1.0
        c[C_NOPE + i, C_SWAP + half + i] = 1.0
    c[:, C_IOTA:C_IOTA + N_EXPERTS + 1] = np.arange(N_EXPERTS + 1)
    c[:, C_GID:C_GID + N_EXPERTS] = np.arange(N_EXPERTS) // PER_GROUP
    inv = np.float32(ROPE_THETA) ** (-np.arange(0, C_ROPE, 2, dtype=np.float32) / np.float32(C_ROPE))
    c[C_NOPE:C_DH, C_INV] = np.concatenate([inv, inv])
    for layer in range(DEPTH):
        c[:, C_LAM + layer] = lam_init(layer)
        c[:, C_LAM + DEPTH + layer] = 1.0 - lam_init(layer)
    dist = np.abs(np.arange(STRIP)[None, :] - P - r[:, None])
    times = sum((dist % dil == 0) & (dist <= win // (2 * dil) * dil) for win, dil in B_PATTERNS)
    many = np.where(times > 0, np.log(np.maximum(times, 1)), FAR)
    for h, s in enumerate(slopes(B_HEADS)):
        c[:, C_STRIP + h * STRIP:C_STRIP + (h + 1) * STRIP] = many - s * dist
    return c


TURNS = [("in", c) for c in range(0, OFF_BV, 256)] + [("in", c) for c in range(OFF_CQ, 3584, 256)]
TURNS += [("in_last", 3584), ("in", OFF_BV), ("in", OFF_BV + 256), ("uq", 0), ("uq", 384), ("ukv", 0)]
EARLY = 4
GATES = [(_pair, _n) for _pair in range(4) for _n in range(N_BRANCHES)]
T_GATE, T_BRANCH, LATE, PRODUCTS = {}, {}, [], []


def add_gate(gate):
    T_GATE[gate] = len(TURNS)
    TURNS.append(("in", OFF_GATE + gate[1] * D + gate[0] * 256))


for _gate in GATES[:EARLY]:
    add_gate(_gate)
for _pair in range(4):
    for _gate in GATES[max(EARLY, 3 * _pair):3 * _pair + 3]:
        add_gate(_gate)
        LATE.append(_gate)
        PRODUCTS.append(("gate",) + _gate)
    for _n in range(N_BRANCHES):
        T_BRANCH[_pair, _n] = len(TURNS) + _n // 2
        PRODUCTS.append(("branch", _pair, _n))
    TURNS += [("branch01", _pair), ("branch2", _pair)]
T_OUT = len(TURNS)
TURNS += [("out", (_half, _kg)) for _half in range(2) for _kg in range(2)]
EXTRA = 7
EMPTY = -(len(TURNS) + 2 - EXTRA) % RING
TURNS += EMPTY * [("empty", 0)]
T_XQ, T_XO = len(TURNS), len(TURNS) + 1
TURNS += [("xq", 0), ("xo", 0)]
Q_BASE = len(TURNS) - EXTRA
PER_QUAD = 2 * KD + 2 * (D_EXPERT // P)
PER_LAYER = Q_BASE + QUADS * PER_QUAD
assert PER_QUAD % RING == 0 and Q_BASE % RING == 0

JOBS = [(n, i, 1, e) for i, (n, e) in enumerate(
    [("aq0", "act"), ("aq1", "dve"), ("ak0", "act"), ("ak1", "dve"), ("av0", "act"), ("av1", "dve"),
     ("bq0", "act"), ("bq1", "dve"), ("bk0", "act"), ("bk1", "dve"), ("c0", "dve"), ("c1", "dve"), ("c2", "dve")])]
JOBS += [("bv0", 13, 1, "act"), ("cs", None, 0, "act"), ("bv1", 14, 1, "dve"),
         ("cq0", 15, 0, "act"), ("cq1", 15, 1, "act"), ("cq2", 16, 0, "act"),
         ("cq3", 16, 1, "act"), ("ckr", None, 0, "dve"), ("ck0", 17, 0, "act"),
         ("ck1", 17, 0, "dve"), ("cr0", None, 0, "dve"), ("cr1", None, 0, "dve"), ("ck2", 17, 0, "dve"), ("ck3", 17, 0, "act"),
         ("cr2", None, 0, "dve"), ("cv0", 17, 0, "dve"), ("cr3", None, 0, "dve"), ("cv1", 17, 1, "dve"),
         ("as0", None, 0, "act"), ("as1", None, 0, "act")]
JOBS[-2:-2] = [("g0", T_GATE[GATES[0]], 1, "act")]
JOBS += [(f"g{_i}", T_GATE[GATES[_i]], 1, "act") for _i in range(1, EARLY)]
JOB_NAMES = [j[0] for j in JOBS]
FILL = {0: ["av0"], 1: ["av1", "bq0"], 2: ["bq1"], 3: ["bk0"], 4: ["bk1"], 5: ["c0"], 6: ["c1"], 7: ["c2"],
        8: ["bv0"], 9: ["cs"], 10: ["bv1"], 11: ["cq0", "cq1"], 12: ["cq2", "cq3", "ckr"], 13: ["ck0", "ck1", "cr0"],
        14: ["cr1", "ck2"], 15: ["ck3", "cr2"], 16: ["cv0", "cr3"], 17: ["cv1"], 18: ["g0"], 19: ["as0", "as1"],
        20: ["g1"], 22: ["g2"], 24: ["g3"]}
assert JOB_NAMES[4:] == [n for i in sorted(FILL) for n in FILL[i]]
A0, B0, C0, X0, NI = 0, 8, 16, 24, 28
LAG_T, LAG_PV, LAG_OUT = 2, 3, 4


def count_before(kind, n):
    return sum(kind(j) for j in JOBS[:n + 1])


def bass_hybrid_encoder(nc, x_in, mem_in, pos_in, mix_norm_g, w_in, diff_lambda, diff_subln_g, mla_q_norm_g,
                        w_uq, mla_kv_norm_g, w_ukv, w_branch, w_out, cross_norm_g, mem_norm_g, w_xq, w_xkv,
                        w_xo, ffn_norm_g, w_group, b_group, w_router, b_router, w1, w3, w2, final_norm_g,
                        consts, out):
    ctx = ExitStack()
    with ctx:
        def sb(name, shape, dt=F32):
            return ctx.enter_context(nc.sbuf_tensor(name, shape, dt))

        def sem(name):
            return ctx.enter_context(nc.semaphore(name))

        ring = sb("ring", [P, RING, SLOT])
        con = sb("con", [P, C_STRIP])
        shared = sb("shared", [P, B_HEADS * STRIP + 5 * SEQ])
        strips = shared[:, 0:B_HEADS * STRIP]
        cT = shared[:, B_HEADS * STRIP:].rearrange("p (c n) -> p c n", n=SEQ)
        x = sb("x", [P, TT, D])
        h = sb("h", [P, TT, D])
        hT = sb("hT", [P, KD, SEQ])
        gain = sb("gain", [P, D])
        q0 = sb("q0", [P, KD, SEQ])
        k0 = sb("k0", [P, 4, 2 * SEQ])
        v0 = sb("v0", [P, TT, 512])
        q1 = sb("q1", [P, 4, SEQ])
        k1 = sb("k1", [P, 4, 2 * SEQ])
        v1 = sb("v1", [P, TT, 512])
        kx_wide = sb("kx_wide", [P, 2, 4 * SEQ])
        kx = kx_wide[:, 0, :].rearrange("p (a n) -> p a n", a=2)
        vx = sb("vx", [P, TT, 256])
        prob = sb("prob", [P, NPB, 2, SEQ])
        probT = sb("probT", [P, 2, 2, TT, P])
        oa = sb("oa", [P, 4, SEQ])
        wide = kx_wide[:, 1, :].rearrange("p (a n) -> p a n", a=4)
        dist = sb("dist", [P, TT, SEQ])
        ropes = sb("ropes", [P, 2, SEQ])
        small = sb("small", [P, 64])
        gpad = sb("gpad", [P, TT, 8])
        topi = sb("topi", [P, TT, 2, 8], U32)
        flag = sb("flag", [P, 1], I32)
        gcol = sb("gcol", [P, DEPTH, 6])
        lamt = sb("lamt", [P, DEPTH])
        stat = sb("stat", [P, 16])
        root = sb("root", [P, 2 * TT, 5])
        mx = sb("mx", [P, NPB, 2])
        sm = sb("sm", [P, NPB, 2])
        rs = sb("rs", [P, NPB, 4])
        bank = [ctx.enter_context(nc.psum_tensor(f"bank{i}", [P, 512], F32)) for i in range(8)]

        ident = con[:, C_ID:C_ID + P]
        ones = con[:, C_ONES:C_ONES + P]
        before = con[:, C_BEFORE:C_BEFORE + P]
        places = con[:, C_IOTA + 1:C_IOTA + 1 + CAP]
        oBC = h[:, :, :].rearrange("p t (c n) -> p (t c) n", n=SEQ)
        kc = k0[:, :, :].rearrange("p a (b n) -> p (a b) n", n=SEQ)
        posf = q1[:, 0:2, :].rearrange("p c n -> p (c n)")[:, 0:TT + SEQ]
        posi = v1[:, :, :].bitcast(I32).rearrange("p t n -> p (t n)")[:, 0:TT + SEQ]
        angles = prob[:, 0, :, :]
        lam_all = v0[:, 1, :]
        spare = oa[:, :, :].rearrange("p c n -> p (c n)")
        NR = N_GROUPS + N_EXPERTS
        logit = spare[:, 0:72].rearrange("p (t n) -> p t n", t=TT)
        rt = spare[:, 72:328].rearrange("p (t a n) -> p t a n", t=TT, a=4)
        top = spare[:, 328:392].rearrange("p (t a n) -> p t a n", t=TT, a=4)
        chosen = spare[:, 392:456].rearrange("p (t n) -> p t n", t=TT)
        place = spare[:, 456:528].rearrange("p (t n) -> p t n", t=TT)
        weight = spare[:, 528:600].rearrange("p (t n) -> p t n", t=TT)
        router_w = wide[:, :, :].rearrange("p c n -> p (c n)")[:, 0:KD * NR].rearrange("p (k n) -> p k n", k=KD)
        router_b = wide[:, :, :].rearrange("p c n -> p (c n)")[:, KD * NR:KD * NR + NR]
        xt = v0[:, :, :].rearrange("p t (c n) -> p (t c) n", n=P)
        yexp = q1[:, :, :].rearrange("p c n -> p (c n)")
        sel = v1[:, 0, 0:256].rearrange("p (t n) -> p t n", t=TT)
        selw = v1[:, 0, 256:512].rearrange("p (t n) -> p t n", t=TT)
        selwT = v1[:, 1, 0:256]
        flat = [prob[:, i, :, :].rearrange("p a n -> p (a n)") for i in range(NPB)]
        act_e, act_r, hidden = flat
        hiddenT = probT[:, 0, :, :, :].rearrange("p a b n -> p (a b) n")
        wxk = k0[:, :, :].rearrange("p a n -> p (a n)").rearrange("p (k n) -> p k n", k=KD)
        wxv = k1[:, :, :].rearrange("p a n -> p (a n)").rearrange("p (k n) -> p k n", k=KD)
        extras = (wxk, wxv, q0[:, :, :].rearrange("p a n -> p (a n)").rearrange("p (k n) -> p k n", k=KD))
        extras = [e.rearrange("p (e a) n -> p e (a n)", e=QUAD) for e in extras]
        extras += [shared[:, i * SLOT:(i + 1) * SLOT].rearrange("p (e n) -> p e n", e=QUAD) for i in range(2)]
        extras += [hT[:, :, :].rearrange("p (e a) n -> p e (a n)", e=QUAD),
                   kx_wide[:, :, :].rearrange("p b (a n) -> p (b a) n", a=2)]
        mem_gain = wide[:, :, :].rearrange("p c n -> p (c n)")
        memx = q0[:, :, :].rearrange("p c n -> p (c n)").rearrange("p (t n) -> p t n", t=TT)
        memjunk = hT[:, :, :].rearrange("p c n -> p (c n)").rearrange("p (t n) -> p t n", t=TT)

        landed = [sem(f"landed{i}") for i in range(RING)]
        slot_free = sem("slot_free")
        extra_in = [sem(f"extra{i}_in") for i in range(EXTRA)]
        con_in, x_in_s, pos_in_s, cols_in, lam_in = (sem(n) for n in ("con_in", "x_arrived", "pos_in", "cols_in", "lam_in"))
        kx_zeroed = sem("kx_zeroed")
        strips_in, eps_set = sem("strips_in"), sem("eps_set")
        gain_in, gain_used = sem("gain_in"), sem("gain_used")
        router_in = sem("router_in")
        mem_tile_in = [sem(f"mem_tile{t}_in") for t in range(TT)]
        mem_gain_in, mem_w_in = sem("mem_gain_in"), sem("mem_w_in")
        mem_squared, mem_root_step, mem_normed, mem_turned = (sem("mem_squared"), sem("mem_root_step"),
                                                              sem("mem_normed"), sem("mem_turned"))
        memT_act, memT_dve, mem_made, kx_copied, vx_copied = (sem("memT_act"), sem("memT_dve"), sem("mem_made"),
                                                              sem("kx_copied"), sem("vx_copied"))
        setup_dve, setup_act, setup_pool, zeroed = sem("setup_dve"), sem("setup_act"), sem("setup_pool"), sem("zeroed")
        squared, root_step, normed, turned = sem("squared"), sem("root_step"), sem("normed"), sem("turned")
        hT_act, hT_dve = sem("hT_act"), sem("hT_dve")
        made = sem("made")
        copied = {"act": sem("copied_act"), "dve": sem("copied_dve")}
        layer_cols = sem("layer_cols")
        c_squared, c_rstd, c_scaled, rope_step, kr_spread = (sem("c_squared"), sem("c_rstd"), sem("c_scaled"),
                                                             sem("rope_step"), sem("kr_spread"))
        a_squared, a_rstd, a_normed = sem("a_squared"), sem("a_rstd"), sem("a_normed")
        scored, biased, maxed, exped = sem("scored"), sem("biased"), sem("maxed"), sem("exped")
        inverted, weighed = sem("inverted"), sem("weighed")
        a_scaled = sem("a_scaled")
        probs_turned, probsT_copied = sem("probs_turned"), sem("probsT_copied")
        pv_done, out_copied = sem("pv_done"), sem("out_copied")
        gate_exp, branch0, gate_step, mixed, mix_sum = (sem("gate_exp"), sem("branch0"), sem("gate_step"),
                                                        sem("mixed"), sem("mix_sum"))
        projected, x_added = sem("projected"), sem("x_added")
        qx_copied = sem("qx_copied")
        logits_made, route_step, route_ask, route_exp = (sem("logits_made"), sem("route_step"),
                                                         sem("route_ask"), sem("route_exp"))
        chosen_s, ranked, placed = sem("chosen_made"), sem("ranked"), sem("placed")
        shifted = sem("shifted")
        layer_done = sem("layer_done")
        stored, passed = sem("stored"), sem("passed")

        def round_sems(name):
            return {s: sem(f"{name}_{s}") for s in
                    ("sel_made", "selw_step", "selw_made", "gathered", "xt_act", "xt_dve", "e_made",
                     "silu_step", "hidden_made", "selw_turned", "hidden_turned", "selwT_copied",
                     "hiddenT_copied", "y_act", "y_dve", "combined", "added")}

        main_r, more_r = round_sems("main"), round_sems("more")
        more_landed = [sem(f"more_landed{i}") for i in range(RING)]
        more_free = sem("more_free")

        def real_turns(slot, upto):
            return sum(1 for j in range(upto) if j % RING == slot and
                       (j >= len(TURNS) or TURNS[j][0] != "empty"))

        def wait_turn(eng, l, j):
            s = j % RING
            eng.wait_ge(landed[s], l * (16 * real_turns(s, PER_LAYER)) + 16 * real_turns(s, j + 1))

        def wait_free(eng, l, j):
            eng.wait_ge(slot_free, l * PER_LAYER + (RING + j + 1))

        N_MADE = sum(not j[2] for j in JOBS)
        N_COPIED = {e: sum(j[3] == e for j in JOBS) for e in ("act", "dve")}

        def wait_made(eng, l, name):
            n = JOB_NAMES.index(name)
            if JOBS[n][2]:
                wait_free(eng, l, JOBS[n][1])
            else:
                eng.wait_ge(made, l * N_MADE + count_before(lambda j: not j[2], n))

        def wait_copied(eng, l, name):
            n = JOB_NAMES.index(name)
            e = JOBS[n][3]
            eng.wait_ge(copied[e], l * N_COPIED[e] + count_before(lambda j: j[3] == e, n))

        def slot_k(j, k, n):
            return ring[:, j % RING, 0:k * n].rearrange("p (k n) -> p k n", k=k)

        def plain(eng):
            eng.sem_inc(passed, 1)

        def quad_at(q, j):
            return Q_BASE + j + (EXTRA if isinstance(q, int) and q == 0 and j < KD else 0)

        HALVES = ((slice(0, 64), slice(SEQ, 2 * SEQ)), (slice(64, 128), slice(0, SEQ)))

        def one(l):
            return bass.ds(l, 1)

        def bank_n(g):
            return bank[NORM_BANKS[g]][:, :].rearrange("p (a n) -> p a n", a=2)

        block = ctx.enter_context(nc.Block())

        def mix_source(l, kind, a):
            def rows(w):
                return w.rearrange("(k p) n -> p k n", p=P)
            if kind == "in":
                return 8, 256, rows(w_in[l, :, a:a + 256])
            if kind == "in_last":
                return 8, 160, rows(w_in[l, :, a:a + 160])
            if kind == "xq":
                return 8, 256, rows(w_xq[l])
            if kind == "xo":
                return 2, 1024, rows(w_xo[l])
            if kind == "uq":
                return 3, 384, rows(w_uq[l, :, a:a + 384])
            if kind == "ukv":
                return 2, 1024, rows(w_ukv[l])
            if kind in ("branch01", "branch2"):
                src = rows(w_branch[l].rearrange("n c d -> (n c) d"))
                lo, n = (0, 8) if kind == "branch01" else (8, 4)
                return n, 256, src[:, lo:lo + n, a * 256:a * 256 + 256]
            half, kg = a
            return 4, 512, rows(w_out[l])[:, 4 * kg:4 * kg + 4, half * 512:half * 512 + 512]

        def quad_source(l, q, j):
            es = bass.ds(q * QUAD, QUAD)
            if j < 2 * KD:
                w, k = (w1 if j < KD else w3), j % KD
                return w[l][es, k * P:(k + 1) * P, :].rearrange("e p n -> p e n")
            half, k = divmod(j - 2 * KD, 4)
            return w2[l][es, k * P:(k + 1) * P, half * 512:half * 512 + 512].rearrange("e p n -> p e n")

        @block.sync
        def _(sp):
            more = sp.alloc_register("sp_more_rounds")
            sp.reg_mov(more, 0)
            sp.dma_start(posi[:, TT:TT + SEQ], pos_in[0:1, :].broadcast_to([P, SEQ])).then_inc(pos_in_s, 16)
            for t in range(TT):
                sp.dma_start(posi[:, t:t + 1], pos_in[0, t * P:(t + 1) * P].rearrange("(p a) -> p a", a=1))\
                  .then_inc(pos_in_s, 16)
            sp.dma_start(con[:, :], consts[:, 0:C_STRIP]).then_inc(con_in, 16)
            sp.dma_start(lam_all, diff_lambda.rearrange("l a d -> (l a d)").rearrange("(a n) -> a n", a=1)
                         .broadcast_to([P, DEPTH * 4 * A_DH])).then_inc(lam_in, 16)
            with sp.Fori(0, DEPTH) as l:
                for j, (kind, a) in enumerate(TURNS):
                    if kind == "empty":
                        continue
                    if j == RING:
                        sp.dma_start(strips, consts[:, C_STRIP:]).then_inc(strips_in, 16)
                    if j == T_XQ:
                        sp.wait_ge(scored, l * NI + X0)
                        sp.dma_start(extras[0], quad_source(l, 0, KD + 0)).then_inc(extra_in[0], 16)
                        sp.wait_ge(mix_sum, l * 4 + 3)
                        sp.dma_start(extras[1], quad_source(l, 0, KD + 1)).then_inc(extra_in[1], 16)
                        sp.wait_ge(biased, l * C0 + C0)
                        wait_copied(sp, l, "cv1")
                        for i in (3, 4):
                            sp.dma_start(extras[i], quad_source(l, 0, KD + i)).then_inc(extra_in[i], 16)
                    k, n, src = mix_source(l, kind, a)
                    sp.wait_ge(slot_free, l * PER_LAYER + (j + 1))
                    sp.dma_start(slot_k(j, k, n), src).then_inc(landed[j % RING], 16)
                wait_free(sp, l, T_OUT + 3)
                sp.dma_start(extras[2], quad_source(l, 0, KD + 2)).then_inc(extra_in[2], 16)

                def quad_turns(q, first, last=PER_QUAD):
                    for j in range(first, last):
                        at = quad_at(q, j)
                        sp.wait_ge(slot_free, l * PER_LAYER + q * PER_QUAD + (at + 1))
                        sp.dma_start(slot_k(at, QUAD, 512), quad_source(l, q, j)).then_inc(landed[at % RING], 16)

                quad_turns(0, 0, KD)
                quad_turns(0, KD + EXTRA, EXTRA + RING)
                sp.wait_ge(logits_made, l + 1)
                plain(sp)
                sp.dma_start(extras[5], quad_source(l, 0, KD + 5)).then_inc(extra_in[5], 16)
                sp.wait_ge(chosen_s, l + 1)
                plain(sp)
                sp.dma_start(extras[6], quad_source(l, 0, KD + 6)).then_inc(extra_in[6], 16)
                quad_turns(0, EXTRA + RING)
                with sp.Fori(1, QUADS) as q:
                    quad_turns(q, 0)
                sp.wait_ge(placed, l + 1)
                plain(sp)
                over = sp.value_load(flag[0:1, 0:1], min_val=0, max_val=1)
                with sp.If(over > 0):
                    sp.wait_ge(slot_free, l * PER_LAYER + (PER_LAYER + RING))
                    plain(sp)
                    with sp.Fori(0, PASSES - 1) as p:
                        with sp.Fori(0, QUADS) as q:
                            rd = sp.snap(more) + p * QUADS + q
                            for j in range(PER_QUAD):
                                sp.wait_ge(more_free, rd * PER_QUAD + (j + 1))
                                sp.dma_start(slot_k(j, QUAD, 512), quad_source(l, q, j))\
                                  .then_inc(more_landed[j % RING], 16)
                    sp.reg_add(more, more, (PASSES - 1) * QUADS)
                    sp.wait_ge(more_free, sp.snap(more) * PER_QUAD + RING)
                    plain(sp)
            for t in range(TT):
                sp.wait_ge(normed, 6 * DEPTH + t + 1)
                sp.dma_start(out[0, t * P:(t + 1) * P, :], h[:, t, :]).then_inc(stored, 16)
            sp.wait_ge(stored, 16 * TT)

        @block.gpsimd
        def _(pool):
            nc.gpsimd.memset(stat[:, 8:9], EPS).then_inc(eps_set, 1)

            def load_mem(l):
                nc.gpsimd.dma_start(mem_gain, mem_norm_g[one(l), :].broadcast_to([P, D])).then_inc(mem_gain_in, 16)
                nc.gpsimd.dma_start(wxk, w_xkv[l, :, 0:256].rearrange("(k p) n -> p k n", p=P)).then_inc(mem_w_in, 16)
                nc.gpsimd.dma_start(wxv, w_xkv[l, :, 256:512].rearrange("(k p) n -> p k n", p=P)).then_inc(mem_w_in, 16)

            def zero_keys(l):
                pool.wait_ge(mem_made, l * 2 + 2)
                plain(pool)
                for i, (kk, rows, cols) in enumerate([(kk, rows, cols) for kk in (k0, k1) for rows, cols in HALVES]):
                    if i:
                        pool.wait_ge(zeroed, l * 4 + i)
                        plain(pool)
                    nc.gpsimd.memset(kk[rows, :, cols], 0.0).then_inc(zeroed, 1)

            def zero_mem_keys(l):
                for i, (rows, cols) in enumerate(HALVES):
                    if i:
                        pool.wait_ge(kx_zeroed, l * 2 + 1)
                        plain(pool)
                    nc.gpsimd.memset(kx[rows, :, cols], 0.0).then_inc(kx_zeroed, 1)

            load_mem(0)
            nc.gpsimd.dma_start(gain[:, :], mix_norm_g[0:1, :].broadcast_to([P, D])).then_inc(gain_in, 16)
            nc.gpsimd.memset(gpad[:, :, :], FAR).then_inc(setup_pool, 1)
            pool.wait_ge(setup_pool, 1)
            zero_mem_keys(0)
            for first, src in ((0, mla_q_norm_g), (3, mla_kv_norm_g), (5, diff_subln_g)):
                for l in range(DEPTH):
                    n = src.shape[1] // P
                    nc.gpsimd.dma_start(gcol[:, l, first:first + n], src[l].rearrange("(c p) -> p c", p=P),
                                        allow_slow_non_contiguous=True)\
                      .then_inc(cols_in, 16)
            zero_keys(0)

            def load_gain(g, l, turn):
                pool.wait_ge(gain_used, l * 3 + (turn + 1))
                plain(pool)
                nc.gpsimd.dma_start(gain[:, :], g.broadcast_to([P, D])).then_inc(gain_in, 16)

            with pool.Fori(0, DEPTH) as l:
                row = one(l)
                load_gain(cross_norm_g[row, :], l, 1)
                wait_copied(pool, l, "ckr")
                plain(pool)
                r = slice(C_NOPE, C_DH)
                nc.gpsimd.tensor_copy(kc[r, 1:8, :], kc[r, 0:1, :].broadcast_to([C_ROPE, 7, SEQ])).then_inc(kr_spread, 1)
                pool.wait_ge(a_normed, l + 1)
                plain(pool)
                nc.gpsimd.dma_start(router_w[:, :, 0:N_GROUPS], w_group[l].rearrange("(k p) n -> p k n", p=P))\
                  .then_inc(router_in, 16)
                nc.gpsimd.dma_start(router_w[:, :, N_GROUPS:], w_router[l].rearrange("(k p) n -> p k n", p=P))\
                  .then_inc(router_in, 16)
                nc.gpsimd.dma_start(router_b[:, 0:N_GROUPS], b_group[row, :].broadcast_to([P, N_GROUPS]))\
                  .then_inc(router_in, 16)
                nc.gpsimd.dma_start(router_b[:, N_GROUPS:], b_router[row, :].broadcast_to([P, N_EXPERTS]))\
                  .then_inc(router_in, 16)
                load_gain(ffn_norm_g[row, :], l, 2)
                with pool.If(l < DEPTH - 1):
                    following = nc.s_assert_within(pool.snap(l) + 1, 1, DEPTH - 1, skip_runtime_bounds_check_because=
                                                   "the branch is taken below the last layer only")
                    load_gain(mix_norm_g[one(following), :], following, 0)
                    pool.wait_ge(chosen_s, l + 1)
                    plain(pool)
                    pool.wait_ge(slot_free, l * PER_LAYER + (Q_BASE + RING + 2 * KD))
                    plain(pool)
                    load_mem(following)
                    zero_mem_keys(following)
                    zero_keys(following)
            load_gain(final_norm_g.rearrange("(a n) -> a n", a=1), DEPTH, 0)

        @block.scalar
        def _(act):
            more = act.alloc_register("act_more_rounds")
            act.reg_mov(more, 0)

            def norm(l, n, src, junk):
                if n == 0 and isinstance(l, int):
                    act.wait_ge(x_in_s, 16)
                elif n == 0:
                    act.wait_ge(layer_done, l + 1)
                for t in range(TT):
                    if n == 1:
                        act.wait_ge(x_added, l * 8 + (2 * t + 2))
                    if n == 2:
                        act.wait_ge(x_added, l * 8 + (2 * t + 6))
                    nc.scalar.activation(junk[:, t, :], src[:, t, :], ACT.Square,
                                         accum_out=stat[:, t:t + 1]).then_inc(squared, 1)

            def copy_hT(l, n):
                for g in (0, 2):
                    act.wait_ge(turned, l * 12 + (4 * n + g + 1))
                    nc.scalar.activation(hT[:, 2 * g:2 * g + 2, :], bank_n(g), ACT.Copy).then_inc(hT_act, 1)

            def mem_squares(l):
                for t in range(TT):
                    act.wait_ge(mem_tile_in[t], l * 16 + 16)
                    nc.scalar.activation(memjunk[:, t, :], memx[:, t, :], ACT.Square,
                                         accum_out=stat[:, 9 + t:10 + t]).then_inc(mem_squared, 1)
                for g in (0, 2):
                    act.wait_ge(mem_turned, l * 4 + (g + 1))
                    nc.scalar.activation(hT[:, 2 * g:2 * g + 2, :], bank_n(g), ACT.Copy).then_inc(memT_act, 1)

            def mem_keys(l):
                act.wait_ge(kx_zeroed, l * 2 + 2)
                act.wait_ge(mem_made, l * 2 + 1)
                b2 = bank[0][:, :].rearrange("p (a n) -> p a n", a=2)
                nc.scalar.activation(kx[0:64, :, 0:SEQ], b2[0:64], ACT.Copy)
                nc.scalar.activation(kx[64:128, :, SEQ:2 * SEQ], b2[64:128], ACT.Copy).then_inc(kx_copied, 1)

            def job(l, name):
                n = JOB_NAMES.index(name)
                wait_made(act, l, name)
                b = bank[n % 2][:, :]
                b2 = b.rearrange("p (a n) -> p a n", a=2)
                kind, i = name[:-1], name[-1]
                if kind in ("aq", "bq"):
                    dst = q0 if kind == "aq" else q1
                    last = nc.scalar.activation(dst[:, 2 * int(i):2 * int(i) + 2, :], b2, ACT.Copy, scale=A_DH ** -0.5)
                elif kind in ("ak", "bk"):
                    dst, c = (k0 if kind == "ak" else k1), 2 * int(i)
                    act.wait_ge(zeroed, l * 4 + 4)
                    nc.scalar.activation(dst[0:64, c:c + 2, 0:SEQ], b2[0:64], ACT.Copy)
                    last = nc.scalar.activation(dst[64:128, c:c + 2, SEQ:2 * SEQ], b2[64:128], ACT.Copy)
                elif kind in ("av", "bv"):
                    dst, c = (v0 if kind == "av" else v1), 256 * int(i)
                    last = nc.scalar.activation(dst[:, :, c:c + 256], b2, ACT.Copy)
                elif name == "cs":
                    nc.scalar.activation(wide[:, 0, :], b2[:, 0], ACT.Ln, scale=1.0 / C_Q_RANK, bias=stat[:, 8:9])
                    last = nc.scalar.activation(wide[:, 1, :], b2[:, 1], ACT.Ln, scale=1.0 / C_KV_RANK,
                                                bias=stat[:, 8:9])
                    last.then_inc(copied["act"], 1)
                    wait_copied(act, l, "cs")
                    nc.scalar.activation(wide[:, 2:4, :], wide[:, 0:2, :], ACT.Exp, scale=-0.5).then_inc(c_rstd, 1)
                    return
                elif kind == "cq":
                    c = 2 * int(i)
                    last = nc.scalar.activation(q0[0:C_DH, c:c + 2, :], b2[0:C_DH], ACT.Copy, scale=C_DH ** -0.5)
                elif kind == "ck" and name != "ckr":
                    c = 2 * int(i)
                    last = nc.scalar.activation(kc[0:C_NOPE, c:c + 2, :], b2[0:C_NOPE], ACT.Copy)
                elif kind == "cv":
                    last = nc.scalar.activation(v0[:, int(i), :], b, ACT.Copy)
                elif kind == "g":
                    act.wait_ge(scored, l * NI + C0)
                    last = nc.scalar.activation(k1[:, int(i), :], b, ACT.Exp, scale=-1.0)
                elif kind == "as":
                    c = 2 * int(i)
                    last = nc.scalar.activation(wide[:, c:c + 2, :], b2, ACT.Ln, scale=1.0 / A_DV, bias=stat[:, 8:9])
                last.then_inc(copied["act"], 1)

            def experts_round(S, wait_w1, wait_w2a, rd, look):
                def copy_xt(k):
                    act.wait_ge(S["gathered"], k * 2 - 1)
                    nc.scalar.activation(xt[:, 0:4, :], bank[0][:, :].rearrange("p (c n) -> p c n", c=4), ACT.Copy)\
                      .then_inc(S["xt_act"], 1)
                if look is None:
                    copy_xt(rd + 1)
                wait_w1(act)
                nc.scalar.activation(act_e, bank[2][:, :], ACT.Exp, scale=-1.0).then_inc(S["e_made"], 1)
                if look is not None:
                    copy_xt(look)
                act.wait_ge(S["selw_turned"], rd + 1)
                nc.scalar.activation(selwT, bank[5][:, 0:256], ACT.Copy).then_inc(S["selwT_copied"], 1)
                act.wait_ge(S["hidden_turned"], rd + 1)
                nc.scalar.activation(hiddenT, bank[4][:, :].rearrange("p (c n) -> p c n", c=4), ACT.Copy)\
                  .then_inc(S["hiddenT_copied"], 1)
                wait_w2a(act)
                nc.scalar.activation(yexp[:, 0:512], bank[6][:, :], ACT.Copy).then_inc(S["y_act"], 1)

            def load_mem():
                for t in range(TT):
                    act.dma_start(memx[:, t, :], mem_in[0, t * P:(t + 1) * P, :]).then_inc(mem_tile_in[t], 16)

            load_mem()
            act.dma_start(x[:, :, :], x_in[0].rearrange("(t p) n -> p t n", p=P)).then_inc(x_in_s, 16)
            act.wait_ge(eps_set, 1)
            mem_squares(0)
            norm(0, 0, x, h)
            act.wait_ge(setup_dve, SETUP_ANGLES)
            nc.scalar.activation(ropes[64:96, 0, :], angles[64:96, 0, :], ACT.Sin)
            nc.scalar.activation(ropes[64:96, 1, :], angles[64:96, 1, :], ACT.Sin)
            nc.scalar.activation(small[:, 4:8], small[:, 0:4], ACT.Exp).then_inc(setup_act, 1)
            mem_keys(0)

            with act.Fori(0, DEPTH) as l:
                copy_hT(l, 0)
                for name in ("aq0", "ak0"):
                    job(l, name)

                def exps(i):
                    pb, m = i % NPB, mx[:, i % NPB, :]
                    act.wait_ge(maxed, l * NI + (i + 1))
                    plain = i >= C0
                    if i >= NPB:
                        act.wait_ge(probs_turned, l * NI + (i - NPB + 1))
                    for j in range(2):
                        src = bank[2 + i % 2][:, j * SEQ:(j + 1) * SEQ] if plain else prob[:, pb, j, :]
                        last = nc.scalar.activation(prob[:, pb, j, :], src, ACT.Exp, bias=m[:, j:j + 1],
                                                    accum_out=sm[:, pb, j:j + 1])
                    last.then_inc(exped, 1)

                def copy_probsT(i):
                    act.wait_ge(probs_turned, l * NI + (i + 1))
                    if i >= 2:
                        act.wait_ge(pv_done, l * NI + (i - 1))
                    n = 1 if i < B0 else 2
                    nc.scalar.activation(probT[:, i % 2, 0:n, :, :].rearrange("p a b n -> p (a b) n"),
                                         bank[4 + i % 2][:, 0:n * 256].rearrange("p (c n) -> p c n", n=P),
                                         ACT.Copy).then_inc(probsT_copied, 1)

                for i in range(X0 + LAG_OUT):
                    if i < X0:
                        exps(i)
                    if i == 8:
                        wait_copied(act, l, "c2")
                        act.wait_ge(scored, l * NI + B0)
                        nc.scalar.activation(q0[:, 0:5, :], cT[:, :, :], ACT.Square).then_inc(c_squared, 1)
                    if i == 18:
                        act.wait_ge(out_copied, l * (NI // 2) + 4)
                        act.wait_ge(c_scaled, l * 5 + 5)
                        nc.scalar.activation(wide[:, :, :], oa[:, :, :], ACT.Square).then_inc(a_squared, 1)
                    for name in FILL.get(i, []):
                        if JOBS[JOB_NAMES.index(name)][3] == "act":
                            if name == "cq0":
                                wait_copied(act, l, "cs")
                            job(l, name)
                    if i == 19:
                        wait_copied(act, l, "as1")
                        nc.scalar.activation(wide[:, :, :], wide[:, :, :], ACT.Exp, scale=-0.5).then_inc(a_rstd, 1)
                    if LAG_T <= i < X0 + LAG_T:
                        copy_probsT(i - LAG_T)
                for pair, n in LATE:
                    wait_free(act, l, T_GATE[pair, n])
                    if pair >= 2:
                        act.wait_ge(mix_sum, l * 4 + (pair + 1))
                    nc.scalar.activation(flat[n], bank[PRODUCTS.index(("gate", pair, n)) % 8][:, :], ACT.Exp,
                                         scale=-1.0).then_inc(gate_exp, 1)
                norm(l, 1, x, h)
                copy_hT(l, 1)
                wait_free(act, l, T_XQ)
                nc.scalar.activation(q1[:, 0:2, :], bank[0][:, :].rearrange("p (a n) -> p a n", a=2), ACT.Copy,
                                     scale=X_DH ** -0.5).then_inc(qx_copied, 1)
                for i in range(X0, NI + LAG_T):
                    if i < NI:
                        exps(i)
                    if i >= X0 + LAG_T:
                        copy_probsT(i - LAG_T)
                norm(l, 2, x, h)
                copy_hT(l, 2)
                act.wait_ge(route_ask, l + 1)
                for t in range(TT):
                    nc.scalar.activation(small[:, 16 + 4 * t:20 + 4 * t], logit[:, t, 0:N_GROUPS], ACT.Exp,
                                         bias=small[:, 10 + t:11 + t], accum_out=small[:, 24 + 2 * t:25 + 2 * t])
                    nc.scalar.activation(small[:, 25 + 2 * t:26 + 2 * t], top[:, t, 2, 1:2], ACT.Exp,
                                         bias=small[:, 12 + t:13 + t]).then_inc(route_exp, 1)
                S = main_r
                act.wait_ge(S["gathered"], l * (2 * QUADS + 2) + 1)
                nc.scalar.activation(xt[:, 0:4, :], bank[0][:, :].rearrange("p (c n) -> p c n", c=4), ACT.Copy)\
                  .then_inc(S["xt_act"], 1)


                def main_round(q):
                    base = l * PER_LAYER + q * PER_QUAD
                    experts_round(S, lambda e: e.wait_ge(slot_free, base + (quad_at(q, KD - 1) + 1 + RING)),
                                  lambda e: e.wait_ge(slot_free, base + (Q_BASE + RING + 2 * KD + 4)),
                                  l * QUADS + q, l * (QUADS + 1) + q + 2)

                main_round(0)
                with act.If(l < DEPTH - 1):
                    act.wait_ge(slot_free, l * PER_LAYER + (Q_BASE + RING + 2 * KD))
                    load_mem()
                with act.Fori(1, QUADS - 1) as q:
                    main_round(q)
                with act.If(l < DEPTH - 1):
                    mem_squares(act.snap(l) + 1)
                    mem_keys(act.snap(l) + 1)
                main_round(QUADS - 1)
                act.wait_ge(placed, l + 1)
                plain(act)
                over = act.value_load(flag[0:1, 0:1], min_val=0, max_val=1)
                with act.If(over > 0):
                    with act.Fori(0, PASSES - 1) as p:
                        with act.Fori(0, QUADS) as q:
                            rd = act.snap(more) + p * QUADS + q
                            experts_round(more_r, lambda e: e.wait_ge(more_free, rd * PER_QUAD + (RING + KD)),
                                          lambda e: e.wait_ge(more_free, rd * PER_QUAD + (RING + 2 * KD + 4)), rd, None)
                    act.reg_add(more, more, (PASSES - 1) * QUADS)
                norm(act.snap(l) + 1, 0, x, h)

        @block.vector
        def _(dve):
            more = dve.alloc_register("dve_more_rounds")
            dve.reg_mov(more, 0)
            more_passes = dve.alloc_register("dve_more_passes")
            dve.reg_mov(more_passes, 0)
            steps = [0]

            def then(ins):
                steps[0] += 1
                ins.then_inc(setup_dve, 1)
                dve.wait_ge(setup_dve, steps[0])


            def rsqrt(tiles, row, totals, step, count):
                def at(t, c):
                    return root[:, row + t, c:c + 1]

                def bits(t, c):
                    return at(t, c).bitcast(I32)
                for t in tiles:
                    nc.vector.tensor_scalar(at(t, 0), totals[:, t:t + 1], 1.0 / D, EPS, ALU.mult, ALU.add)\
                      .then_inc(step, 1)
                for t in tiles:
                    nc.vector.tensor_scalar(at(t, 1), totals[:, t:t + 1], -0.5 / D, -0.5 * EPS, ALU.mult, ALU.add)\
                      .then_inc(step, 1)
                dve.wait_ge(step, count + len(tiles))
                for t in tiles:
                    nc.vector.tensor_scalar(bits(t, 2), bits(t, 0), 1, None, ALU.logical_shift_right).then_inc(step, 1)
                dve.wait_ge(step, count + 3 * len(tiles))
                for t in tiles:
                    nc.vector.tensor_scalar(bits(t, 3), bits(t, 2), -1, ROOT_START, ALU.mult, ALU.add).then_inc(step, 1)
                for i in range(3):
                    dve.wait_ge(step, count + (4 + 2 * i) * len(tiles))
                    for t in tiles:
                        nc.vector.scalar_tensor_tensor(at(t, 4), at(t, 3), at(t, 1), at(t, 3), ALU.mult, ALU.mult)\
                          .then_inc(step, 1)
                    dve.wait_ge(step, count + (5 + 2 * i) * len(tiles))
                    for t in tiles:
                        nc.vector.scalar_tensor_tensor(at(t, 3), at(t, 4), 1.5, at(t, 3), ALU.add, ALU.mult)\
                          .then_inc(step, 1)
                dve.wait_ge(step, count + len(tiles) * ROOT_STEPS)

            def mem_norm(l):
                dve.wait_ge(mem_squared, l * TT + TT)
                rsqrt(range(TT), TT, stat[:, 9:9 + TT], mem_root_step, l * (TT * ROOT_STEPS))
                dve.wait_ge(mem_gain_in, l * 16 + 16)
                for t in range(TT):
                    nc.vector.scalar_tensor_tensor(memx[:, t, :], memx[:, t, :], root[:, TT + t, 3:4], mem_gain,
                                                   ALU.mult, ALU.mult).then_inc(mem_normed, 1)
                for g in (1, 3):
                    dve.wait_ge(mem_turned, l * 4 + (g + 1))
                    nc.vector.tensor_copy(hT[:, 2 * g:2 * g + 2, :], bank_n(g)).then_inc(memT_dve, 1)

            def mem_values(l):
                dve.wait_ge(mem_made, l * 2 + 2)
                nc.vector.tensor_copy(vx[:, :, :], bank[1][:, :].rearrange("p (a n) -> p a n", a=2))\
                   .then_inc(vx_copied, 1)

            def norm(l, n, src, dst, tiles=range(TT)):
                dve.wait_ge(squared, l * 6 + (2 * n + tiles[-1] + 1))
                rsqrt(tiles, 0, stat[:, 0:TT], root_step, l * (3 * TT * ROOT_STEPS) + (n * TT + tiles[0]) * ROOT_STEPS)
                if tiles[0] == 0:
                    dve.wait_ge(gain_in, l * 48 + (16 * n + 16))
                for t in tiles:
                    nc.vector.scalar_tensor_tensor(dst[:, t, :], src[:, t, :], root[:, t, 3:4], gain[:, :],
                                                   ALU.mult, ALU.mult).then_inc(normed, 1)
                if tiles[-1] == TT - 1:
                    dve.wait_ge(normed, l * 6 + (2 * n + 2))
                    dve.sem_inc(gain_used, 1)

            mem_norm(0)
            dve.wait_ge(pos_in_s, 16 * (TT + 1))
            dve.wait_ge(con_in, 16)
            dve.wait_ge(lam_in, 16)
            then(nc.vector.tensor_copy(posf[:, :], posi[:, :]))
            for b in range(TT):
                then(nc.vector.tensor_scalar(dist[:, b, :], posf[:, TT:], posf[:, b:b + 1], None, ALU.subtract))
                then(nc.vector.scalar_tensor_tensor(dist[:, b, :], dist[:, b, :], -1.0, dist[:, b, :], ALU.mult, ALU.max))
            r = slice(C_NOPE, C_DH)
            ang, turns = v0[r, 0, 0:SEQ], v0[r, 0, SEQ:2 * SEQ]
            then(nc.vector.tensor_scalar(ang, posf[r, TT:], con[r, C_INV:C_INV + 1], None, ALU.mult))
            for dst, quarter in ((1, 0.0), (0, 0.25)):
                w = angles[r, dst, :]
                then(nc.vector.tensor_scalar(turns, ang, 1.0 / (2 * math.pi), quarter, ALU.mult, ALU.add))
                then(nc.vector.tensor_scalar(turns, turns, 12582912.0, None, ALU.add))
                then(nc.vector.tensor_scalar(turns, turns, -12582912.0, None, ALU.add))
                then(nc.vector.scalar_tensor_tensor(w, turns, -TWO_PI[0], ang, ALU.mult, ALU.add))
                then(nc.vector.scalar_tensor_tensor(w, turns, -TWO_PI[1], w, ALU.mult, ALU.add))
                then(nc.vector.scalar_tensor_tensor(w, turns, -TWO_PI[2], w, ALU.mult, ALU.add))
                then(nc.vector.tensor_scalar(w, w, quarter * 2 * math.pi, 3.1415925, ALU.add, ALU.min))
                then(nc.vector.tensor_scalar(w, w, -3.1415925, None, ALU.max))
            lq = lam_all.rearrange("p (a b d) -> p a b d", b=2, d=A_DH)
            pr = cT[:, 0, :].rearrange("p (a d) -> p a d", d=A_DH)
            then(nc.vector.tensor_tensor(pr, lq[:, :, 0, :], lq[:, :, 1, :], ALU.mult))
            then(nc.vector.tensor_reduce(small[:, 0:4], pr, AX_X, ALU.add))
            assert steps[0] == SETUP_ANGLES

            norm(0, 0, x, h)
            mem_values(0)
            dve.wait_ge(setup_act, 1)
            ex = small[:, 4:8].rearrange("p (l a) -> p l a", a=2)
            then(nc.vector.tensor_tensor(small[:, 8:10], ex[:, :, 1], ex[:, :, 0], ALU.subtract))
            then(nc.vector.tensor_tensor(lamt[:, :], small[:, 8:10], con[:, C_LAM:C_LAM + DEPTH], ALU.subtract))
            for count in (gain_used, layer_done, mix_sum, main_r["added"], more_r["added"]):
                dve.sem_inc(count, 1)

            def copy_hT(l, n):
                for g in (1, 3):
                    dve.wait_ge(turned, l * 12 + (4 * n + g + 1))
                    nc.vector.tensor_copy(hT[:, 2 * g:2 * g + 2, :], bank_n(g)).then_inc(hT_dve, 1)

            def rope(l, n, dst, src, heads):
                cos = ropes[r, 0:1, :].broadcast_to([C_ROPE, heads, SEQ])
                sin = ropes[r, 1:2, :].broadcast_to([C_ROPE, heads, SEQ])
                tmp = oBC[r, 6:6 + heads, :]
                nc.vector.tensor_tensor(tmp, src, sin, ALU.mult).then_inc(rope_step, 1)
                nc.vector.tensor_tensor(dst, dst, cos, ALU.mult).then_inc(rope_step, 1)
                dve.wait_ge(rope_step, l * 10 + (2 * n + 2))
                return nc.vector.tensor_tensor(dst, dst, tmp, ALU.add)

            def job(l, name):
                n = JOB_NAMES.index(name)
                wait_made(dve, l, name)
                b = bank[n % 2][:, :]
                b2 = b.rearrange("p (a n) -> p a n", a=2)
                kind, i = name[:-1], name[-1]
                if kind in ("aq", "bq"):
                    dst = q0 if kind == "aq" else q1
                    last = nc.vector.tensor_scalar(dst[:, 2 * int(i):2 * int(i) + 2, :], b2, A_DH ** -0.5, None, ALU.mult)
                elif kind in ("ak", "bk"):
                    dst, c = (k0 if kind == "ak" else k1), 2 * int(i)
                    dve.wait_ge(zeroed, l * 4 + 4)
                    nc.vector.tensor_copy(dst[0:64, c:c + 2, 0:SEQ], b2[0:64])
                    last = nc.vector.tensor_copy(dst[64:128, c:c + 2, SEQ:2 * SEQ], b2[64:128])
                elif kind in ("av", "bv"):
                    dst, c = (v0 if kind == "av" else v1), 256 * int(i)
                    last = nc.vector.tensor_copy(dst[:, :, c:c + 256], b2)
                elif name in ("c0", "c1"):
                    c = 2 * int(i)
                    last = nc.vector.tensor_copy(cT[:, c:c + 2, :], b2)
                elif name == "c2":
                    dve.wait_ge(scored, l * NI + B0)
                    nc.vector.tensor_copy(cT[:, 4, :], b2[:, 0, :])
                    last = nc.vector.tensor_copy(kc[r, 0, :], b2[r, 1, :])
                elif kind == "ck" and name != "ckr":
                    c = 2 * int(i)
                    last = nc.vector.tensor_copy(kc[0:C_NOPE, c:c + 2, :], b2[0:C_NOPE])
                elif kind == "cv":
                    dve.wait_ge(pv_done, l * NI + B0)
                    last = nc.vector.tensor_copy(v0[:, int(i), :], b)
                elif kind == "cr":
                    c = 2 * int(i)
                    last = rope(l, 1 + int(i), q0[r, c:c + 2, :], b2[r], 2)
                elif name == "ckr":
                    last = rope(l, 0, kc[r, 0:1, :], b2[r, 0:1, :], 1)
                last.then_inc(copied["dve"], 1)

            def maxima(l, i):
                pb = i % NPB
                src = bank[2 + i % 2][:, :].rearrange("p (a n) -> p a n", a=2)
                dve.wait_ge(scored, l * NI + (i + 1))
                b = i % 2
                if i >= NPB:
                    dve.wait_ge(probs_turned, l * NI + (i - NPB + 1))
                if i < B0:
                    nc.vector.scalar_tensor_tensor(prob[:, pb, :, :], dist[:, b:b + 1, :].broadcast_to([P, 2, SEQ]),
                                                   -slopes(A_HEADS)[i // 2], src, ALU.mult, ALU.add).then_inc(biased, 1)
                elif i < C0:
                    hd = 2 * ((i - B0) // 2)
                    at = hd * STRIP
                    if i == B0:
                        dve.wait_ge(strips_in, l * 16 + 16)
                    strip = strips[:, at:at + 2 * STRIP].rearrange("p (a n) -> p a n", a=2)[:, :, P - b * P:P - b * P + SEQ]
                    nc.vector.tensor_tensor(prob[:, pb, :, :], src, strip, ALU.add).then_inc(biased, 1)
                if i < C0:
                    dve.wait_ge(biased, l * C0 + (i + 1))
                    src = prob[:, pb, :, :]
                nc.vector.tensor_reduce(mx[:, pb, :], src, AX_X, ALU.max, negate=True).then_inc(maxed, 1)

            def weigh(l, i):
                pb = i % NPB
                dve.wait_ge(exped, l * NI + (i + 1))
                nc.vector.reciprocal(rs[:, pb, 0:2], sm[:, pb, :]).then_inc(inverted, 1)
                dve.wait_ge(inverted, l * NI + (i + 1))
                if i < B0:
                    nc.vector.tensor_scalar(rs[:, pb, 2:3], rs[:, pb, 1:2], lamcur, None, ALU.mult).then_inc(a_scaled, 1)
                    dve.wait_ge(a_scaled, l * 16 + (2 * i + 1))
                    nc.vector.tensor_scalar(prob[:, pb, 1, :], prob[:, pb, 1, :], rs[:, pb, 2:3], None, ALU.mult)\
                      .then_inc(a_scaled, 1)
                    dve.wait_ge(a_scaled, l * 16 + (2 * i + 2))
                    nc.vector.scalar_tensor_tensor(prob[:, pb, 0, :], prob[:, pb, 0, :], rs[:, pb, 0:1],
                                                   prob[:, pb, 1, :], ALU.mult, ALU.add).then_inc(weighed, 1)
                else:
                    nc.vector.tensor_scalar(prob[:, pb, 0, :], prob[:, pb, 0, :], rs[:, pb, 0:1], None, ALU.mult)
                    nc.vector.tensor_scalar(prob[:, pb, 1, :], prob[:, pb, 1, :], rs[:, pb, 1:2], None, ALU.mult)\
                      .then_inc(weighed, 1)

            def copy_out(l, u):
                dve.wait_ge(pv_done, l * NI + (2 * u + 2))
                if u < 4:
                    dst = oa[:, u, :]
                elif u < 12:
                    dst = oBC[:, u - 4, :]
                else:
                    dst = oa[:, u - 12, :]
                nc.vector.tensor_copy(dst, bank[6 + u % 2][:, 0:SEQ]).then_inc(out_copied, 1)

            def experts_round(S, wait_w3, wait_w2b, rd, q, look, sel_next):
                def make_sel(cols):
                    nc.vector.tensor_tensor(
                        sel.rearrange("p t (e s) -> p t e s", e=QUAD),
                        places.rearrange("p (a b s) -> p a b s", a=1, b=1).broadcast_to([P, TT, QUAD, CAP]),
                        place[:, :, cols].rearrange("p t (e s) -> p t e s", s=1).broadcast_to([P, TT, QUAD, CAP]),
                        ALU.is_equal).then_inc(S["sel_made"], 1)

                def copy_xt(k):
                    dve.wait_ge(S["gathered"], k * 2)
                    nc.vector.tensor_copy(xt[:, 4:8, :], bank[1][:, :].rearrange("p (c n) -> p c n", c=4))\
                       .then_inc(S["xt_dve"], 1)

                if look is not None:
                    make_sel(bass.ds(q * QUAD + QUAD, QUAD))
                else:
                    make_sel(bass.ds(q * QUAD, QUAD))
                    copy_xt(rd + 1)
                here = bass.ds(q * QUAD, QUAD)
                sw = selw.rearrange("p t (e s) -> p t e s", e=QUAD)
                nc.vector.tensor_tensor(
                    sw, places.rearrange("p (a b s) -> p a b s", a=1, b=1).broadcast_to([P, TT, QUAD, CAP]),
                    place[:, :, here].rearrange("p t (e s) -> p t e s", s=1).broadcast_to([P, TT, QUAD, CAP]),
                    ALU.is_equal).then_inc(S["selw_step"], 1)
                dve.wait_ge(S["selw_step"], rd + 1)
                nc.vector.tensor_tensor(
                    sw, sw, weight[:, :, here].rearrange("p t (e s) -> p t e s", s=1).broadcast_to([P, TT, QUAD, CAP]),
                    ALU.mult).then_inc(S["selw_made"], 1)
                dve.wait_ge(S["e_made"], rd + 1)
                nc.vector.tensor_scalar(act_e, act_e, 1.0, None, ALU.add).then_inc(S["silu_step"], 1)
                dve.wait_ge(S["silu_step"], rd * 3 + 1)
                nc.vector.reciprocal(act_r, act_e).then_inc(S["silu_step"], 1)
                dve.wait_ge(S["silu_step"], rd * 3 + 2)
                nc.vector.tensor_tensor(act_r, bank[2][:, :], act_r, ALU.mult).then_inc(S["silu_step"], 1)
                dve.wait_ge(S["silu_step"], rd * 3 + 3)
                wait_w3(dve)
                nc.vector.tensor_tensor(hidden, bank[3][:, :], act_r, ALU.mult).then_inc(S["hidden_made"], 1)
                if look is not None:
                    copy_xt(look)
                for c in range(4):
                    half, t = divmod(c, 2)
                    if c == 2:
                        wait_w2b(dve)
                        nc.vector.tensor_copy(yexp[:, 512:1024], bank[7][:, :]).then_inc(S["y_dve"], 1)
                    dve.wait_ge(S["combined"], rd * 4 + (c + 1))
                    xs = x[:, t, half * 512:half * 512 + 512]
                    nc.vector.tensor_tensor(xs, xs, bank[(5, 2)[c % 2]][:, :], ALU.add).then_inc(S["added"], 1)

            gcur, lamcur = small[:, 40:46], small[:, 46:47]
            with dve.Fori(0, DEPTH) as l:
                row = bass.ds(l, 1)
                nc.vector.tensor_copy(lamcur, lamt[:, row]).then_inc(layer_cols, 1)
                copy_hT(l, 0)
                for name in ("aq1", "ak1"):
                    job(l, name)
                for i in range(X0 + LAG_OUT + 1):
                    if i < X0:
                        maxima(l, i)
                    if 1 <= i <= X0:
                        if i == 1:
                            dve.wait_ge(layer_cols, l * 3 + 1)
                        weigh(l, i - 1)
                    for name in FILL.get(i, []):
                        if JOBS[JOB_NAMES.index(name)][3] == "dve":
                            job(l, name)
                    if i == 10:
                        dve.wait_ge(cols_in, 16 * 3 * DEPTH)
                        nc.vector.tensor_copy(gcur[:, 0:5], gcol[:, row, 0:5].rearrange("p a n -> p (a n)"))\
                          .then_inc(layer_cols, 1)
                        nc.vector.tensor_tensor(gcur[:, 5:6], gcol[:, row, 5], con[:, bass.ds(l + C_LAM + DEPTH, 1)],
                                                ALU.mult).then_inc(layer_cols, 1)
                        dve.wait_ge(layer_cols, l * 3 + 3)
                        dve.wait_ge(c_rstd, l + 1)
                        for c in range(5):
                            nc.vector.scalar_tensor_tensor(cT[:, c, :], cT[:, c, :], gcur[:, c:c + 1],
                                                           wide[:, 2 + c // 3, :], ALU.mult, ALU.mult).then_inc(c_scaled, 1)
                    if i == 21:
                        dve.wait_ge(a_rstd, l + 1)
                        nc.vector.scalar_tensor_tensor(oa[:, :, :], oa[:, :, :], gcur[:, 5:6], wide[:, :, :],
                                                       ALU.mult, ALU.mult).then_inc(a_normed, 1)
                    if i >= LAG_OUT and (i - LAG_OUT) % 2 == 1:
                        copy_out(l, (i - LAG_OUT) // 2)
                for pair in range(4):
                    es = [k1[:, 3 * pair + n, :] if 3 * pair + n < EARLY else flat[n] for n in range(N_BRANCHES)]
                    for n, e in enumerate(es):
                        if (pair, n) in LATE:
                            dve.wait_ge(gate_exp, l * len(LATE) + (LATE.index((pair, n)) + 1))
                        else:
                            wait_copied(dve, l, f"g{GATES.index((pair, n))}")
                        nc.vector.tensor_scalar(e, e, 1.0, None, ALU.add).then_inc(gate_step, 1)
                        dve.wait_ge(gate_step, l * 28 + (7 * pair + 2 * n + 1))
                        nc.vector.reciprocal(e, e).then_inc(gate_step, 1)
                    for n, e in enumerate(es):
                        dve.wait_ge(gate_step, l * 28 + (7 * pair + 2 * n + 2))
                        if n == 0:
                            dve.wait_ge(branch0, l * 4 + (pair + 1))
                        else:
                            wait_free(dve, l, T_BRANCH[pair, n])
                        nc.vector.tensor_tensor(e, bank[PRODUCTS.index(("branch", pair, n)) % 8][:, :], e, ALU.mult)\
                          .then_inc(mixed, 1)
                        if n == 1:
                            dve.wait_ge(mixed, l * 12 + (3 * pair + 2))
                            nc.vector.tensor_tensor(es[0], es[0], es[1], ALU.add).then_inc(gate_step, 1)
                    dve.wait_ge(mixed, l * 12 + (3 * pair + 3))
                    dve.wait_ge(gate_step, l * 28 + (7 * pair + 7))
                    nc.vector.tensor_tensor(q0[:, 2 * pair:2 * pair + 2, :].rearrange("p a n -> p (a n)"), es[0],
                                            es[2], ALU.add).then_inc(mix_sum, 1)
                for o in range(4):
                    t, half = divmod(o, 2)
                    if t == 0:
                        dve.wait_ge(projected, l * 5 + (half + 1))
                    else:
                        wait_free(dve, l, T_OUT + 2 * half + 1)
                    xs = x[:, t, half * 512:half * 512 + 512]
                    nc.vector.tensor_tensor(xs, xs, bank[SUM_BANKS[o]][:, :], ALU.add).then_inc(x_added, 1)
                    if half == 1:
                        dve.wait_ge(x_added, l * 8 + (2 * t + 2))
                        norm(l, 1, x, h, (t,))
                copy_hT(l, 1)
                for i in range(X0, NI + LAG_OUT):
                    if i < NI:
                        maxima(l, i)
                    if X0 < i <= NI:
                        weigh(l, i - 1)
                    if i - LAG_OUT >= X0 and (i - LAG_OUT) % 2 == 1:
                        copy_out(l, (i - LAG_OUT) // 2)
                for o in range(4):
                    t, half = divmod(o, 2)
                    if o < 3:
                        dve.wait_ge(projected, l * 5 + (2 + o + 1))
                    else:
                        wait_free(dve, l, T_XO)
                    xs = x[:, t, half * 512:half * 512 + 512]
                    nc.vector.tensor_tensor(xs, xs, bank[SUM_BANKS[o]][:, :], ALU.add).then_inc(x_added, 1)
                    if half == 1:
                        dve.wait_ge(x_added, l * 8 + (2 * t + 6))
                        norm(l, 2, x, h, (t,))
                copy_hT(l, 2)

                rstep = [0]

                def step(*instructions):
                    for ins in instructions:
                        rstep[0] += 1
                        ins.then_inc(route_step, 1)
                    dve.wait_ge(route_step, l * ROUTE_STEPS + rstep[0])
                    plain(dve)

                tiles = range(TT)
                f = small[:, 48:64].rearrange("p (t c) -> p t c", t=TT)
                dve.wait_ge(setup_pool, 1)
                dve.wait_ge(router_in, l * 64 + 64)
                dve.wait_ge(logits_made, l + 1)
                nc.vector.memset(place[:, :, N_EXPERTS:], 0.0)
                nc.vector.memset(weight[:, :, N_EXPERTS:], 0.0)
                raw = bank[0][:, 0:128].rearrange("p (t n) -> p t n", t=TT)
                bias = router_b[:, :].rearrange("p (a n) -> p a n", a=1)
                step(nc.vector.tensor_tensor(gpad[:, :, 0:N_GROUPS], raw[:, :, 0:N_GROUPS],
                                             bias[:, :, 0:N_GROUPS].broadcast_to([P, TT, N_GROUPS]), ALU.add),
                     nc.vector.tensor_tensor(logit[:, :, :], raw[:, :, 0:NR], bias.broadcast_to([P, TT, NR]), ALU.add))
                step(*[nc.vector.max(top[:, t, 0, :], gpad[:, t, :]) for t in tiles])
                step(*[nc.vector.max_index(topi[:, t, 0, :], top[:, t, 0, :], gpad[:, t, :]) for t in tiles])
                step(nc.vector.tensor_copy(f[:, :, 0:1], topi[:, :, 0, 0:1]))
                step(*[nc.vector.tensor_scalar(rt[:, t, 0, :], con[:, C_GID:C_GID + N_EXPERTS], f[:, t, 0:1], -FAR,
                                               ALU.is_equal, ALU.mult) for t in tiles])
                step(*[nc.vector.scalar_tensor_tensor(rt[:, t, 1, :], rt[:, t, 0, :], FAR, logit[:, t, N_GROUPS:],
                                                      ALU.add, ALU.add) for t in tiles])
                step(*[nc.vector.max(top[:, t, 2, :], rt[:, t, 1, :]) for t in tiles])
                step(*[nc.vector.max_index(topi[:, t, 1, :], top[:, t, 2, :], rt[:, t, 1, :]) for t in tiles])
                step(nc.vector.tensor_copy(f[:, :, 1:3], topi[:, :, 1, 0:2]))
                experts = con[:, C_IOTA:C_IOTA + N_EXPERTS]
                step(*[nc.vector.tensor_scalar(rt[:, t, 2 + i, :], experts, f[:, t, 1 + i:2 + i], None, ALU.is_equal)
                       for t in tiles for i in range(2)])
                nc.vector.tensor_tensor(chosen[:, :, :], rt[:, :, 2, :], rt[:, :, 3, :], ALU.add).then_inc(chosen_s, 1)
                nc.vector.tensor_scalar(small[:, 10:10 + TT], top[:, :, 0, 0], -1.0, None, ALU.mult)
                nc.vector.tensor_scalar(small[:, 12:12 + TT], top[:, :, 2, 0], -1.0, None, ALU.mult).then_inc(route_ask, 1)
                dve.wait_ge(ranked, l + 1)
                dve.wait_ge(chosen_s, l + 1)
                plain(dve)
                rank = bank[1][:, 0:64].rearrange("p (t n) -> p t n", t=TT)
                step(nc.vector.scalar_tensor_tensor(place[:, :, 0:N_EXPERTS], rank, 1.0, chosen[:, :, :], ALU.add, ALU.mult))
                nc.vector.tensor_tensor(
                    sel.rearrange("p t (e s) -> p t e s", e=QUAD),
                    places.rearrange("p (a b s) -> p a b s", a=1, b=1).broadcast_to([P, TT, QUAD, CAP]),
                    place[:, :, 0:QUAD].rearrange("p t (e s) -> p t e s", s=1).broadcast_to([P, TT, QUAD, CAP]),
                    ALU.is_equal).then_inc(main_r["sel_made"], 1)
                step(nc.vector.tensor_reduce(small[:, 47:48], bank[4][:, 0:32], AX_X, ALU.max))
                nc.vector.tensor_scalar(flag[:, :], small[:, 47:48], float(CAP), None, ALU.is_gt).then_inc(placed, 1)
                dve.wait_ge(route_exp, l * 2 + 2)
                step(*[nc.vector.tensor_scalar(f[:, t, 3:4], small[:, 25 + 2 * t:26 + 2 * t], 1.0,
                                               small[:, 24 + 2 * t:25 + 2 * t], ALU.add, ALU.mult) for t in tiles])
                step(nc.vector.reciprocal(f[:, :, 4:5], f[:, :, 3:4]))
                step(*[nc.vector.tensor_tensor(f[:, t, 5:6], f[:, t, 4:5], small[:, 25 + 2 * t:26 + 2 * t], ALU.mult)
                       for t in tiles])
                step(*[nc.vector.tensor_scalar(rt[:, t, 3, :], rt[:, t, 3, :], f[:, t, 5:6], None, ALU.mult) for t in tiles])
                step(*[nc.vector.scalar_tensor_tensor(weight[:, t, 0:N_EXPERTS], rt[:, t, 2, :], f[:, t, 4:5],
                                                      rt[:, t, 3, :], ALU.mult, ALU.add) for t in tiles])
                assert rstep[0] == ROUTE_STEPS, rstep[0]

                S = main_r
                dve.wait_ge(S["gathered"], l * (2 * QUADS + 2) + 2)
                nc.vector.tensor_copy(xt[:, 4:8, :], bank[1][:, :].rearrange("p (c n) -> p c n", c=4))\
                   .then_inc(S["xt_dve"], 1)

                def main_round(q):
                    base = l * PER_LAYER + q * PER_QUAD
                    experts_round(S, lambda e: e.wait_ge(slot_free, base + (Q_BASE + RING + 2 * KD)),
                                  lambda e: e.wait_ge(slot_free, base + (Q_BASE + RING + PER_QUAD)),
                                  l * QUADS + q, q, l * (QUADS + 1) + q + 2, None)

                with dve.Fori(0, QUADS - 1) as q:
                    main_round(q)
                with dve.If(l < DEPTH - 1):
                    mem_norm(dve.snap(l) + 1)
                    mem_values(dve.snap(l) + 1)
                main_round(QUADS - 1)
                dve.wait_ge(S["added"], l * (4 * QUADS) + (4 * QUADS + 1))
                dve.wait_ge(placed, l + 1)
                plain(dve)
                over = dve.value_load(flag[0:1, 0:1], min_val=0, max_val=1)
                with dve.If(over > 0):
                    with dve.Fori(0, PASSES - 1) as p:
                        nc.vector.tensor_scalar(place[:, :, 0:N_EXPERTS], place[:, :, 0:N_EXPERTS], -float(CAP), None,
                                                ALU.add).then_inc(shifted, 1)
                        with dve.Fori(0, QUADS) as q:
                            rd = dve.snap(more) + p * QUADS + q
                            dve.wait_ge(shifted, dve.snap(more_passes) + p + 1)
                            experts_round(more_r, lambda e: e.wait_ge(more_free, rd * PER_QUAD + (RING + 2 * KD)),
                                          lambda e: e.wait_ge(more_free, rd * PER_QUAD + (RING + PER_QUAD)),
                                          rd, q, None, None)
                    dve.reg_add(more, more, (PASSES - 1) * QUADS)
                    dve.reg_add(more_passes, more_passes, PASSES - 1)
                    dve.wait_ge(more_r["added"], dve.snap(more) * 4 + 1)
                    plain(dve)
                dve.sem_inc(layer_done, 1)
                norm(dve.snap(l) + 1, 0, x, h)

        @block.tensor
        def _(pe):
            more = pe.alloc_register("pe_more_rounds")
            pe.reg_mov(more, 0)
            pe.sem_inc(slot_free, RING)
            pe.sem_inc(more_free, RING)
            pe.wait_ge(con_in, 16)

            def turn_tile(l, n, src, t):
                pe.wait_ge(normed, l * 6 + (2 * n + t + 1))
                for g in range(4):
                    for kk in range(2):
                        k = 2 * g + kk
                        at = kk * SEQ + t * P
                        last = nc.tensor.transpose(bank[NORM_BANKS[g]][:, at:at + P], src[:, t, k * P:(k + 1) * P], ident)
                    if t == TT - 1:
                        last.then_inc(turned, 1)

            def wait_hT(l, n):
                pe.wait_ge(hT_act, l * 6 + (2 * n + 2))
                pe.wait_ge(hT_dve, l * 6 + (2 * n + 2))

            def turn_tokens(l, n, src):
                for t in range(TT):
                    turn_tile(l, n, src, t)
                wait_hT(l, n)

            def features(dst, w, cols, src, kn):
                for k in range(kn):
                    last = nc.tensor.matmul(dst, w[:, k, cols], src[:, k, :], start=k == 0, stop=k == kn - 1)
                return last

            def tokens(dst, w, src, t, kn):
                for k in range(kn):
                    last = nc.tensor.matmul(dst, src[:, k, t * P:(t + 1) * P], w[:, k], start=k == 0, stop=k == kn - 1)
                return last

            def job(l, name):
                n = JOB_NAMES.index(name)
                turn, frees = JOBS[n][1:3]
                if n >= 2:
                    wait_copied(pe, l, JOB_NAMES[n - 2])
                if turn is not None:
                    wait_turn(pe, l, turn)
                b = bank[n % 2]
                kind, i = name[:-1], name[-1]
                if kind in ("aq", "bq", "ak", "bk", "g") or name in ("c0", "c1"):
                    w = slot_k(turn, 8, 256)
                    for c in range(2):
                        last = features(b[:, c * SEQ:(c + 1) * SEQ], w, slice(c * P, (c + 1) * P), hT, KD)
                elif kind in ("av", "bv"):
                    w = slot_k(turn, 8, 256)
                    for t in range(TT):
                        last = tokens(b[:, t * 256:(t + 1) * 256], w, hT, t, KD)
                elif name == "c2":
                    w = slot_k(turn, 8, 160)
                    features(b[:, 0:SEQ], w, slice(0, P), hT, KD)
                    last = features(b[C_NOPE:C_DH, SEQ:2 * SEQ], w, slice(P, P + C_ROPE), hT, KD)
                elif name == "cs":
                    pe.wait_ge(c_squared, l + 1)
                    for k in range(3):
                        nc.tensor.matmul(b[:, 0:SEQ], ones, q0[:, k, :], start=k == 0, stop=k == 2)
                    for k in range(2):
                        last = nc.tensor.matmul(b[:, SEQ:2 * SEQ], ones, q0[:, 3 + k, :], start=k == 0, stop=k == 1)
                elif kind == "cq":
                    pe.wait_ge(c_scaled, l * 5 + 5)
                    w = slot_k(turn, 3, 384)
                    for j in range(2):
                        at = (2 * int(i) + j) % 4 * C_DH
                        last = features(b[0:C_DH, j * SEQ:(j + 1) * SEQ], w, slice(at, at + C_DH), cT, 3)
                elif kind == "ck" and name != "ckr":
                    w = slot_k(turn, 2, 1024)
                    for j in range(2):
                        at = (2 * int(i) + j) * (C_NOPE + C_DV)
                        last = features(b[0:C_NOPE, j * SEQ:(j + 1) * SEQ], w, slice(at, at + C_NOPE), cT[:, 3:5, :], 2)
                elif kind == "cv":
                    w = slot_k(turn, 2, 1024).rearrange("p k (h n) -> p k h n", h=C_HEADS)[:, :, :, C_NOPE:]
                    last = tokens(b[:, :].rearrange("p (h n) -> p h n", h=C_HEADS), w, cT[:, 3:5, :], int(i), 2)
                elif kind == "cr":
                    wait_copied(pe, l, "cq" + i)
                    last = nc.tensor.matmul(b[C_NOPE:C_DH, :], con[0:C_DH, C_SWAP:C_SWAP + C_ROPE],
                                            q0[0:C_DH, 2 * int(i):2 * int(i) + 2, :], start=True, stop=True)
                elif name == "ckr":
                    last = nc.tensor.matmul(b[C_NOPE:C_DH, 0:SEQ], con[0:C_DH, C_SWAP:C_SWAP + C_ROPE],
                                            kc[0:C_DH, 0, :], start=True, stop=True)
                elif kind == "as":
                    pe.wait_ge(a_squared, l + 1)
                    last = nc.tensor.matmul(b[:, :], ones, wide[:, 2 * int(i):2 * int(i) + 2, :], start=True, stop=True)
                last.then_inc(slot_free if frees else made, 1)

            def mem_stage(l):
                for t in range(TT):
                    pe.wait_ge(mem_normed, l * 2 + (t + 1))
                    for g in range(4):
                        for kk in range(2):
                            k = 2 * g + kk
                            at = kk * SEQ + t * P
                            last = nc.tensor.transpose(bank[NORM_BANKS[g]][:, at:at + P],
                                                       memx[:, t, k * P:(k + 1) * P], ident)
                        if t == TT - 1:
                            last.then_inc(mem_turned, 1)
                pe.wait_ge(memT_act, l * 2 + 2)
                pe.wait_ge(memT_dve, l * 2 + 2)
                pe.wait_ge(mem_w_in, l * 32 + 32)
                for c in range(2):
                    last = features(bank[0][:, c * SEQ:(c + 1) * SEQ], wxk, slice(c * P, (c + 1) * P), hT, KD)
                last.then_inc(mem_made, 1)
                for t in range(TT):
                    last = tokens(bank[1][:, t * 256:(t + 1) * 256], wxv, hT, t, KD)
                last.then_inc(mem_made, 1)

            def scores(l, i):
                u, b = divmod(i, 2)
                needed = {A0: ("ak0", "ak1"), B0: ("bk0", "bk1"), C0: ("cr0", "ck0"), C0 + 2: ("cr1", "ck0"),
                          C0 + 4: ("cr2", "ck2"), C0 + 6: ("cr3", "ck3")}
                for name in needed.get(i, ()):
                    wait_copied(pe, l, name)
                if i == C0:
                    pe.wait_ge(kr_spread, l + 1)
                if i == X0:
                    pe.wait_ge(qx_copied, l + 1)
                if i >= 2:
                    pe.wait_ge(exped, l * NI + (i - 1))
                dst = bank[2 + i % 2]
                qs = slice(b * P, (b + 1) * P)
                if C0 <= i < X0:
                    for j in range(2):
                        hd = 2 * (u - 8) + j
                        last = nc.tensor.matmul(dst[:, j * SEQ:(j + 1) * SEQ], q0[0:C_DH, hd, qs], kc[0:C_DH, hd, :],
                                                start=True, stop=True)
                else:
                    q, k, c = (q0, k0, u) if i < B0 else (q1, k1, u - 4) if i < C0 else (q1, kx, u - 12)
                    last = nc.tensor.matmul(dst[:, :], q[:, c, qs], k[:, c, :], start=True, stop=True)
                last.then_inc(scored, 1)

            def turn_probs(l, i):
                pe.wait_ge(weighed, l * NI + (i + 1))
                if i >= 2:
                    pe.wait_ge(probsT_copied, l * NI + (i - 1))
                for j in range(1 if i < B0 else 2):
                    for c in range(TT):
                        at = (2 * j + c) * P
                        last = nc.tensor.transpose(bank[4 + i % 2][:, at:at + P], prob[:, i % NPB, j, c * P:(c + 1) * P], ident)
                last.then_inc(probs_turned, 1)

            def products(l, i):
                u, b = divmod(i, 2)
                pe.wait_ge(probsT_copied, l * NI + (i + 1))
                if i == A0:
                    wait_copied(pe, l, "av0")
                    wait_copied(pe, l, "av1")
                if i == B0:
                    wait_copied(pe, l, "bv0")
                    wait_copied(pe, l, "bv1")
                if i == C0:
                    wait_copied(pe, l, "cv1")
                if b == 0 and u >= 2:
                    pe.wait_ge(out_copied, l * (NI // 2) + (u - 1))
                dst = bank[6 + u % 2]
                qs = slice(b * P, (b + 1) * P)
                if i < B0:
                    for c in range(TT):
                        last = nc.tensor.matmul(dst[:, qs], v0[:, c, u * P:(u + 1) * P], probT[:, i % 2, 0, c, :],
                                                start=c == 0, stop=c == TT - 1)
                else:
                    v, hd = (v1, 2 * (u - 4)) if i < C0 else (v0, 2 * (u - 8)) if i < X0 else (vx, 2 * (u - 12))
                    for c in range(TT):
                        for j in range(2):
                            last = nc.tensor.matmul(dst[64 * j:64 * j + 64, qs], v[:, c, (hd + j) * 64:(hd + j + 1) * 64],
                                                    probT[:, i % 2, j, c, :], start=c == 0, stop=c == TT - 1)
                last.then_inc(pv_done, 1)

            def gather(S, k):
                pe.wait_ge(S["sel_made"], k)
                for c in range(KD):
                    for t in range(TT):
                        last = nc.tensor.matmul(bank[c // 4][:, c % 4 * P:(c % 4 + 1) * P], h[:, t, c * P:(c + 1) * P],
                                                sel[:, t, :], start=t == 0, stop=t == TT - 1)
                    if c % 4 == 3:
                        last.then_inc(S["gathered"], 1)

            def experts_round(S, wait, free, rd, xts, look, extras_in=None):
                pe.wait_ge(S["xt_act"], xts)
                pe.wait_ge(S["added"], rd * 4 + 1)
                for m in range(2):
                    for k in range(KD):
                        j = m * KD + k
                        if j == 4:
                            pe.wait_ge(S["xt_dve"], xts)
                        beside = extras_in is not None and KD <= j < KD + EXTRA
                        if beside:
                            pe.wait_ge(extra_in[j - KD], extras_in)
                            w = extras[j - KD]
                        else:
                            wait(j)
                            w = slot_k(j if extras_in is None else quad_at(0, j), QUAD, 512)
                        for e in range(QUAD):
                            last = nc.tensor.matmul(bank[2 + m][e * CAP:(e + 1) * CAP, :], xt[:, k, e * CAP:(e + 1) * CAP],
                                                    w[:, e, :], start=k == 0, stop=k == KD - 1)
                        if not beside:
                            last.then_inc(free, 1)
                if look is not None:
                    gather(S, look)
                pe.wait_ge(S["selw_made"], rd + 1)
                for t in range(TT):
                    last = nc.tensor.transpose(bank[5][:, t * P:(t + 1) * P], selw[:, t, :], ident)
                last.then_inc(S["selw_turned"], 1)
                pe.wait_ge(S["hidden_made"], rd + 1)
                for k in range(4):
                    last = nc.tensor.transpose(bank[4][:, k * P:(k + 1) * P], hidden[:, k * P:(k + 1) * P], ident)
                last.then_inc(S["hidden_turned"], 1)
                pe.wait_ge(S["hiddenT_copied"], rd + 1)

                def combine(half):
                    pe.wait_ge(S["y_act"] if half == 0 else S["y_dve"], rd + 1)
                    for t in range(TT):
                        if half:
                            pe.wait_ge(S["added"], rd * 4 + (t + 2))
                        nc.tensor.matmul(bank[(5, 2)[t]][:, :], selwT[:, t * P:(t + 1) * P],
                                         yexp[:, half * 512:half * 512 + 512], start=True, stop=True)\
                          .then_inc(S["combined"], 1)

                for half in range(2):
                    for k in range(4):
                        j = 2 * KD + 4 * half + k
                        wait(j)
                        w = slot_k(j, QUAD, 512)
                        for e in range(QUAD):
                            last = nc.tensor.matmul(bank[6 + half][e * CAP:(e + 1) * CAP, :],
                                                    hiddenT[:, k, e * CAP:(e + 1) * CAP], w[:, e, :],
                                                    start=k == 0, stop=k == 3)
                        last.then_inc(free, 1)
                        if half == 1 and k == 1:
                            pe.wait_ge(S["selwT_copied"], rd + 1)
                            combine(0)
                combine(1)

            mem_stage(0)
            with pe.Fori(0, DEPTH) as l:
                turn_tokens(l, 0, h)
                pe.wait_ge(kx_copied, l + 1)
                pe.wait_ge(vx_copied, l + 1)
                for name in JOB_NAMES[0:4]:
                    job(l, name)
                for i in range(X0 + LAG_PV):
                    if i < X0:
                        scores(l, i)
                    for name in FILL.get(i, []):
                        job(l, name)
                    if LAG_T <= i < X0 + LAG_T:
                        turn_probs(l, i - LAG_T)
                    if i >= LAG_PV:
                        products(l, i - LAG_PV)
                pe.wait_ge(out_copied, l * (NI // 2) + 12)
                pe.wait_ge(a_normed, l + 1)
                for name in ("as1", f"g{EARLY - 2}", f"g{EARLY - 1}"):
                    wait_copied(pe, l, name)
                srcs = (oa, oBC[:, 0:4, :], oBC[:, 4:8, :])
                for g, (what, pair, n) in enumerate(PRODUCTS):
                    if g >= 8:
                        old, op, on = PRODUCTS[g - 8]
                        if old == "gate":
                            pe.wait_ge(gate_exp, l * len(LATE) + (LATE.index((op, on)) + 1))
                        else:
                            pe.wait_ge(mixed, l * 12 + (3 * op + on + 1))
                    turn = T_GATE[pair, n] if what == "gate" else T_BRANCH[pair, n]
                    wait_turn(pe, l, turn)
                    w = slot_k(turn, 4 if what == "branch" and n == 2 else 8, 256)
                    for c in range(2):
                        cols, dst = slice(c * P, (c + 1) * P), bank[g % 8][:, c * SEQ:(c + 1) * SEQ]
                        if what == "gate":
                            last = features(dst, w, cols, hT, KD)
                        else:
                            last = features(dst, w[:, 4 * (n % 2):4 * (n % 2) + 4], cols, srcs[n], 4)
                    last.then_inc(branch0 if what == "branch" and n == 0 else slot_free, 1)
                pe.wait_ge(gate_exp, l * len(LATE) + len(LATE))
                for o in range(4):
                    t, half = divmod(o, 2)
                    for kg in range(2):
                        turn = T_OUT + 2 * half + kg
                        wait_turn(pe, l, turn)
                        w = slot_k(turn, 4, 512)
                        for k in range(4):
                            if o == 0 and k % 2 == 0:
                                pe.wait_ge(mix_sum, l * 4 + (2 * kg + k // 2 + 2))
                            last = nc.tensor.matmul(bank[SUM_BANKS[o]][:, :], q0[:, 4 * kg + k, t * P:(t + 1) * P],
                                                    w[:, k, :], start=kg == 0 and k == 0, stop=kg == 1 and k == 3)
                        if t == 1:
                            last.then_inc(slot_free, 1 + EMPTY * (o == 3 and kg == 1))
                        elif kg == 1:
                            last.then_inc(projected, 1)
                    if o == 2:
                        turn_tile(l, 1, h, 0)
                turn_tile(l, 1, h, 1)
                wait_hT(l, 1)
                wait_turn(pe, l, T_XQ)
                for c in range(2):
                    last = features(bank[0][:, c * SEQ:(c + 1) * SEQ], slot_k(T_XQ, 8, 256), slice(c * P, (c + 1) * P), hT, KD)
                last.then_inc(slot_free, 1)
                for i in range(X0, NI + LAG_PV):
                    if i < NI:
                        scores(l, i)
                    if X0 + LAG_T <= i < NI + LAG_T:
                        turn_probs(l, i - LAG_T)
                    if i >= X0 + LAG_PV:
                        products(l, i - LAG_PV)
                pe.wait_ge(out_copied, l * (NI // 2) + 14)
                wait_turn(pe, l, T_XO)
                w = slot_k(T_XO, 2, 1024)
                for o in range(4):
                    t, half = divmod(o, 2)
                    for k in range(2):
                        last = nc.tensor.matmul(bank[SUM_BANKS[o]][:, :], oa[:, k, t * P:(t + 1) * P],
                                                w[:, k, half * 512:half * 512 + 512], start=k == 0, stop=k == 1)
                    if o < 3:
                        last.then_inc(projected, 1)
                    else:
                        last.then_inc(slot_free, 1)
                turn_tokens(l, 2, h)
                pe.wait_ge(router_in, l * 64 + 64)
                for t in range(TT):
                    for k in range(KD):
                        last = nc.tensor.matmul(bank[0][:, t * 64:t * 64 + 36], hT[:, k, t * P:(t + 1) * P], router_w[:, k, :],
                                                start=k == 0, stop=k == KD - 1)
                last.then_inc(logits_made, 1)
                pe.wait_ge(chosen_s, l + 1)
                b = bank[1]
                nc.tensor.matmul(b[:, 0:32], before, chosen[:, 0, :], start=True, stop=True)
                nc.tensor.matmul(b[:, 32:64], ones, chosen[:, 0, :], start=True, stop=False)
                nc.tensor.matmul(b[:, 32:64], before, chosen[:, 1, :], start=False, stop=True)
                nc.tensor.matmul(bank[4][:, 0:32], ones, chosen[:, 0, :], start=True, stop=False)
                nc.tensor.matmul(bank[4][:, 0:32], ones, chosen[:, 1, :], start=False, stop=True).then_inc(ranked, 1)
                S = main_r
                gather(S, l * (QUADS + 1) + 1)

                def main_round(q, extras_in=None):
                    def wait_main(j):
                        at = quad_at(q, j)
                        s = at % RING
                        pe.wait_ge(landed[s], l * (16 * real_turns(s, PER_LAYER)) + q * (16 * PER_QUAD // RING)
                                   + 16 * real_turns(s, at + 1))
                    experts_round(S, wait_main, slot_free, l * QUADS + q, l * (QUADS + 1) + q + 1,
                                  l * (QUADS + 1) + q + 2, extras_in)

                main_round(0, l * 16 + 16)
                with pe.Fori(1, QUADS - 1) as q:
                    main_round(q)
                with pe.If(l < DEPTH - 1):
                    pe.wait_ge(S["xt_act"], l * (QUADS + 1) + QUADS)
                    pe.wait_ge(S["xt_dve"], l * (QUADS + 1) + QUADS)
                    mem_stage(pe.snap(l) + 1)
                    pe.wait_ge(kx_copied, pe.snap(l) + 2)
                    pe.wait_ge(vx_copied, pe.snap(l) + 2)
                main_round(QUADS - 1)
                pe.wait_ge(placed, l + 1)
                plain(pe)
                over = pe.value_load(flag[0:1, 0:1], min_val=0, max_val=1)
                with pe.If(over > 0):
                    with pe.Fori(0, PASSES - 1) as p:
                        with pe.Fori(0, QUADS) as q:
                            rd = pe.snap(more) + p * QUADS + q

                            def wait_more(j):
                                pe.wait_ge(more_landed[j % RING], rd * (16 * PER_QUAD // RING) + 16 * (j // RING + 1))
                            pe.wait_ge(main_r["xt_act"], l * (QUADS + 1) + QUADS + 1)
                            pe.wait_ge(main_r["xt_dve"], l * (QUADS + 1) + QUADS + 1)
                            gather(more_r, rd + 1)
                            experts_round(more_r, wait_more, more_free, rd, rd + 1, None)
                    pe.reg_add(more, more, (PASSES - 1) * QUADS)
                pe.wait_ge(layer_done, l + 2)


_INS = ["x", "mem", "positions", "mix_norm_g", "w_in", "diff_lambda", "diff_subln_g", "mla_q_norm_g", "w_uq",
        "mla_kv_norm_g", "w_ukv", "w_branch", "w_out", "cross_norm_g", "mem_norm_g", "w_xq", "w_xkv", "w_xo",
        "ffn_norm_g", "w_group", "b_group", "w_router", "b_router", "w1", "w3", "w2", "final_norm_g"]


def kernel(**inputs):
    import numpy as np
    import concourse.bacc as bacc
    from concourse.bass_utils import run_bass_kernel_spmd

    nc = bacc.Bacc("TRN2", target_bir_lowering=False, num_devices=1)
    arrays, args = {}, []
    for name in _INS:
        a = np.ascontiguousarray(inputs[name])
        arrays[f"in_{name}_dram"] = a
        args.append(nc.dram_tensor(f"in_{name}_dram", a.shape, mybir.dt.from_np(a.dtype), kind="ExternalInput").ap())
    c = shape_constants()
    arrays["consts_dram"] = c
    args.append(nc.dram_tensor("consts_dram", c.shape, F32, kind="ExternalInput").ap())
    args.append(nc.dram_tensor("out_dram", (1, SEQ, D), F32, kind="ExternalOutput").ap())
    bass_hybrid_encoder(nc, *args)
    r = run_bass_kernel_spmd(nc, [arrays], core_ids=[0])
    return r.results[0]["out_dram"]
```
